# Optimizing a Trainium2 kernel written in Bass

```python
import math
import jax
import jax.numpy as jnp
from jax import lax
import numpy as np

D_MODEL = 2048
BATCH = 1
SEQ = 256
DEPTH = 1
DEC_BATCH = 8
DEC_SEQ = 8
PAST_LEN = 2048
PAGE_SIZE = 128

CONV_W = D_MODEL // 4
NSA_W = D_MODEL // 2
MLSTM_W = D_MODEL // 4
MIX_W = CONV_W + NSA_W + MLSTM_W
CONV_K = 3
HEAD_DIM = 64
NSA_HEADS = NSA_W // HEAD_DIM
NSA_KV_HEADS = 4
NSA_GROUP = NSA_HEADS // NSA_KV_HEADS
CMP_STRIDE = 16
CMP_BLOCK = 2 * CMP_STRIDE
SEL_BLOCK = 64
SEL_TOPN = 16
WINDOW = 512
SEL_QBLOCK = 64
WIN_QBLOCK = 128
MLSTM_HEADS = 4
MLSTM_DH = MLSTM_W // MLSTM_HEADS
MLSTM_CHUNK = 64
PEER_HEADS = 8
PEER_NKEYS = 128
PEER_EXPERTS = PEER_NKEYS * PEER_NKEYS
PEER_DKEY = 256
PEER_TOPK = 16
PEER_TBLOCK = 128
RMS_EPS = 1e-6
MASK_BIG = 1e9
SPLIT_SIZES = (CONV_W, CONV_W, CONV_W, NSA_W, 6 * NSA_KV_HEADS * HEAD_DIM, 3 * NSA_HEADS,
               MLSTM_W, MLSTM_W, MLSTM_W, MLSTM_W, MLSTM_HEADS, MLSTM_HEADS)
IN_COLS = sum(SPLIT_SIZES)

kernel_name = 'hymba_conv_nsa_mlstm_peer_step'

def rmsnorm(x, g):
    x32 = x.astype(jnp.float32)
    r = x32 * lax.rsqrt(jnp.mean(x32 * x32, -1, keepdims=True) + RMS_EPS)
    return (r * g.astype(jnp.float32)).astype(x.dtype)

def masked_softmax(s, mask):
    s = jnp.where(mask, s.astype(jnp.float32), -jnp.inf)
    m = jnp.max(s, -1, keepdims=True)
    m = jnp.where(jnp.isfinite(m), m, 0.0)
    e = jnp.where(mask, jnp.exp(s - m), 0.0)
    return e / jnp.maximum(jnp.sum(e, -1, keepdims=True), 1e-30)

def short_conv(u, buf, w):
    ext = jnp.concatenate([buf.astype(u.dtype), u], axis=1)
    y = lax.conv_general_dilated(ext, w[:, None, :].astype(u.dtype), (1,), 'VALID',
                                 dimension_numbers=('NWC', 'WIO', 'NWC'),
                                 feature_group_count=u.shape[-1])
    return y, ext[:, -(CONV_K - 1):]

def mlstm_chunkwise(q, k, v, i_pre, logf, C0, n0, m0):
    B, S, H, DH = q.shape
    L = MLSTM_CHUNK if S % MLSTM_CHUNK == 0 else S
    nc = S // L

    def chunks(a):
        a = a.astype(jnp.float32).reshape((B, nc, L) + a.shape[2:])
        return jnp.swapaxes(jnp.moveaxis(a, 1, 0), 2, 3)

    qc, kc, vc = chunks(q), chunks(k) * (DH ** -0.5), chunks(v)
    ic, fc = chunks(i_pre), chunks(logf)
    tril = jnp.tril(jnp.ones((L, L), bool))

    def step(carry, inp):
        C, n, m = carry
        qq, kk, vv, ii, ff = inp
        b = jnp.cumsum(ff, -1)
        dmat = jnp.where(tril, b[..., :, None] - b[..., None, :] + ii[..., None, :], -jnp.inf)
        inter = b + m[..., None]
        mt = jnp.maximum(inter, jnp.max(dmat, -1))
        w = jnp.exp(dmat - mt[..., None])
        a = jnp.exp(inter - mt)
        wqk = w * jnp.einsum('bhtd,bhsd->bhts', qq, kk)
        num = a[..., None] * jnp.einsum('bhtd,bhde->bhte', qq, C) + jnp.einsum('bhts,bhse->bhte', wqk, vv)
        den = a * jnp.einsum('bhtd,bhd->bht', qq, n) + jnp.sum(wqk, -1)
        h = num / jnp.maximum(jnp.abs(den), jnp.exp(-mt))[..., None]
        m_new = mt[..., -1]
        wl = jnp.exp(b[..., -1:] - b + ii - m_new[..., None])
        decay = jnp.exp(b[..., -1] + m - m_new)
        C_new = decay[..., None, None] * C + jnp.einsum('bhs,bhsd,bhse->bhde', wl, kk, vv)
        n_new = decay[..., None] * n + jnp.einsum('bhs,bhsd->bhd', wl, kk)
        return (C_new, n_new, m_new), h

    init = (C0.astype(jnp.float32), n0.astype(jnp.float32), m0.astype(jnp.float32))
    (C, n, m), hs = lax.scan(step, init, (qc, kc, vc, ic, fc))
    h = jnp.moveaxis(jnp.swapaxes(hs, 2, 3), 0, 1).reshape(B, S, H, DH)
    return h, C, n, m

def compress_kv(k):
    B, Lp = k.shape[:2]
    sub = jnp.mean(k.reshape((B, Lp // CMP_STRIDE, CMP_STRIDE) + k.shape[2:]), axis=2)
    nxt = jnp.concatenate([sub[:, 1:], jnp.zeros_like(sub[:, :1])], axis=1)
    return 0.5 * (sub + nxt)

def nsa_global_block(q, q_pos, kc, vc, kb, vb, n_sel):
    B, Q = q.shape[:2]
    scale = HEAD_DIM ** -0.5
    NC = kc.shape[1]
    NB = kb.shape[2]
    c_end = jnp.arange(NC) * CMP_STRIDE + CMP_BLOCK - 1
    c_mask = c_end[None, :] <= q_pos[:, None]
    p = masked_softmax(jnp.einsum('bqkgd,bckd->bkgqc', q, kc) * scale, c_mask)
    o_cmp = jnp.einsum('bkgqc,bckd->bqkgd', p.astype(vc.dtype), vc)
    imp = jnp.sum(p, axis=2).reshape(B, NSA_KV_HEADS, Q, NB, SEL_BLOCK // CMP_STRIDE).sum(-1)
    blk = jnp.arange(NB)[None, :]
    qblk = (q_pos // SEL_BLOCK)[:, None]
    valid = blk * SEL_BLOCK <= q_pos[:, None]
    forced = (blk == 0) | (blk == qblk) | (blk == qblk - 1)
    score = jnp.where(forced, MASK_BIG, jnp.where(valid, imp, -MASK_BIG))
    top, idx = lax.top_k(score, n_sel)
    sel_ok = top > -0.5 * MASK_BIG
    bi = jnp.arange(B)[:, None, None, None]
    hi = jnp.arange(NSA_KV_HEADS)[None, :, None, None]
    kg = kb[bi, hi, idx]
    vg = vb[bi, hi, idx]
    kpos = idx[..., None] * SEL_BLOCK + jnp.arange(SEL_BLOCK)
    k_mask = (kpos <= q_pos[None, None, :, None, None]) & sel_ok[..., None]
    M = n_sel * SEL_BLOCK
    s2 = jnp.einsum('bqkgd,bkqnjd->bkqgnj', q, kg) * scale
    p2 = masked_softmax(s2.reshape(B, NSA_KV_HEADS, Q, NSA_GROUP, M),
                        k_mask.reshape(B, NSA_KV_HEADS, Q, 1, M))
    o_sel = jnp.einsum('bkqgm,bkqmd->bqkgd', p2.astype(vg.dtype),
                       vg.reshape(B, NSA_KV_HEADS, Q, M, HEAD_DIM))
    return o_cmp, o_sel

def nsa_global(q, kvs, q_pos):
    B, L = kvs.shape[:2]
    Lp = -(-L // SEL_BLOCK) * SEL_BLOCK
    kvs = jnp.pad(kvs, ((0, 0), (0, Lp - L), (0, 0), (0, 0), (0, 0)))
    kc, vc = compress_kv(kvs[:, :, 0]), compress_kv(kvs[:, :, 1])
    NB = Lp // SEL_BLOCK

    def blocks(a):
        return a.reshape(B, NB, SEL_BLOCK, NSA_KV_HEADS, HEAD_DIM).transpose(0, 3, 1, 2, 4)

    kb, vb = blocks(kvs[:, :, 2]), blocks(kvs[:, :, 3])
    n_sel = min(SEL_TOPN, NB)
    Q = q.shape[1]
    if Q % SEL_QBLOCK == 0:
        nq = Q // SEL_QBLOCK
        qs = jnp.moveaxis(q.reshape((B, nq, SEL_QBLOCK) + q.shape[2:]), 1, 0)
        ps = q_pos.reshape(nq, SEL_QBLOCK)
        oc, osel = lax.map(lambda a: nsa_global_block(a[0], a[1], kc, vc, kb, vb, n_sel), (qs, ps))
        return jnp.moveaxis(oc, 0, 1).reshape(q.shape), jnp.moveaxis(osel, 0, 1).reshape(q.shape)
    return nsa_global_block(q, q_pos, kc, vc, kb, vb, n_sel)

def window_prompt(q, k, v):
    B, S = q.shape[:2]
    QB = WIN_QBLOCK if S % WIN_QBLOCK == 0 else S
    nq = S // QB
    span = WINDOW + QB
    pad = ((0, 0), (WINDOW, 0), (0, 0), (0, 0))
    kp, vp = jnp.pad(k, pad), jnp.pad(v, pad)
    kidx = jnp.arange(nq)[:, None] * QB + jnp.arange(span)[None, :]
    kpos = kidx - WINDOW
    qpos = jnp.arange(nq)[:, None] * QB + jnp.arange(QB)[None, :]
    kb, vb = kp[:, kidx], vp[:, kidx]
    qb = q.reshape(B, nq, QB, NSA_KV_HEADS, NSA_GROUP, HEAD_DIM)
    diff = qpos[:, :, None] - kpos[:, None, :]
    mask = (diff >= 0) & (diff < WINDOW) & (kpos[:, None, :] >= 0)
    s = jnp.einsum('bnqkgd,bnjkd->bnkgqj', qb, kb) * (HEAD_DIM ** -0.5)
    p = masked_softmax(s, mask[None, :, None, None])
    o = jnp.einsum('bnkgqj,bnjkd->bnqkgd', p.astype(vb.dtype), vb)
    return o.reshape(q.shape)

def window_cached(q, k_all, v_all, q_pos, k_pos):
    diff = q_pos[:, None] - k_pos[None, :]
    mask = (diff >= 0) & (diff < WINDOW)
    s = jnp.einsum('bqkgd,bjkd->bkgqj', q, k_all) * (HEAD_DIM ** -0.5)
    p = masked_softmax(s, mask)
    return jnp.einsum('bkgqj,bjkd->bqkgd', p.astype(v_all.dtype), v_all)

def nsa_prompt(q, kv):
    B, S = q.shape[:2]
    rows = kv[:, :, :2].reshape(B, S, 4, NSA_KV_HEADS, HEAD_DIM)
    o_cmp, o_sel = nsa_global(q, rows, jnp.arange(S))
    o_win = window_prompt(q, kv[:, :, 2, 0], kv[:, :, 2, 1])
    win_state = kv[:, S - min(WINDOW, S):, 2]
    return o_cmp, o_sel, o_win, rows, win_state

def make_nsa_sample(cache_nsa_kv, layer, page_table, win_buf):
    def nsa_sample(q, kv):
        B, S = q.shape[:2]
        past_len = page_table.shape[1] * cache_nsa_kv.shape[2]
        rows = kv[:, :, :2].reshape(B, S, 4, NSA_KV_HEADS, HEAD_DIM)
        past = cache_nsa_kv[layer, page_table].reshape(B, past_len, 4, NSA_KV_HEADS, HEAD_DIM)
        q_pos = past_len + jnp.arange(S)
        o_cmp, o_sel = nsa_global(q, jnp.concatenate([past, rows.astype(past.dtype)], axis=1), q_pos)
        wb = win_buf.shape[1]
        w_all = jnp.concatenate([win_buf, kv[:, :, 2].astype(win_buf.dtype)], axis=1)
        k_pos = past_len - wb + jnp.arange(wb + S)
        o_win = window_cached(q, w_all[:, :, 0], w_all[:, :, 1], q_pos, k_pos)
        return o_cmp, o_sel, o_win, rows, w_all[:, S:]
    return nsa_sample

def peer_block(x, wq, subkeys, u, v):
    T = x.shape[0]
    q = (x @ wq).reshape(T, PEER_HEADS, 2, PEER_DKEY // 2)
    s = jnp.einsum('thcd,hcnd->thcn', q, subkeys).astype(jnp.float32)
    s1, i1 = lax.top_k(s[:, :, 0], PEER_TOPK)
    s2, i2 = lax.top_k(s[:, :, 1], PEER_TOPK)
    cand = (s1[..., :, None] + s2[..., None, :]).reshape(T, PEER_HEADS, PEER_TOPK * PEER_TOPK)
    cidx = (i1[..., :, None] * PEER_NKEYS + i2[..., None, :]).reshape(T, PEER_HEADS, PEER_TOPK * PEER_TOPK)
    top, pos = lax.top_k(cand, PEER_TOPK)
    eidx = jnp.take_along_axis(cidx, pos, -1)
    g = jax.nn.softmax(top, -1)
    act = jax.nn.gelu(jnp.einsum('td,thkd->thk', x, u[eidx]).astype(jnp.float32))
    return jnp.einsum('thk,thkd->td', (g * act).astype(x.dtype), v[eidx])

def peer(x, wq, subkeys, u, v):
    B, S, D = x.shape
    T = B * S
    TB = PEER_TBLOCK if T % PEER_TBLOCK == 0 else T
    out = lax.map(lambda xb: peer_block(xb, wq, subkeys, u, v), x.reshape(T // TB, TB, D))
    return out.reshape(B, S, D)

def hybrid_layer(x, lw, conv_buf, C0, n0, m0, nsa_fn):
    (norm1_g, w_in, conv_w, gate_b, mnorm_g, w_out, norm2_g, pwq, psub, pu, pv) = lw
    B, S, _ = x.shape
    z = rmsnorm(x, norm1_g) @ w_in
    offs = np.cumsum(SPLIT_SIZES)[:-1].tolist()
    (cb, cc, ch, nq, nkv, ngate, mq, mk, mv, mo, mi, mf) = jnp.split(z, offs, axis=-1)
    u, conv_new = short_conv(cc * ch, conv_buf, conv_w)
    y_a = cb * u
    q = nq.reshape(B, S, NSA_KV_HEADS, NSA_GROUP, HEAD_DIM)
    kv = nkv.reshape(B, S, 3, 2, NSA_KV_HEADS, HEAD_DIM)
    o_cmp, o_sel, o_win, nsa_rows, win_state = nsa_fn(q, kv)
    g = jax.nn.sigmoid(ngate.astype(jnp.float32)).reshape(B, S, NSA_KV_HEADS, NSA_GROUP, 3).astype(x.dtype)
    y_b = (g[..., 0:1] * o_cmp + g[..., 1:2] * o_sel + g[..., 2:3] * o_win).reshape(B, S, NSA_W)
    hd = lambda a: a.reshape(B, S, MLSTM_HEADS, MLSTM_DH)
    i_pre = mi.astype(jnp.float32) + gate_b[0].astype(jnp.float32)
    logf = jax.nn.log_sigmoid(mf.astype(jnp.float32) + gate_b[1].astype(jnp.float32))
    h, C, n, m = mlstm_chunkwise(hd(mq), hd(mk), hd(mv), i_pre, logf, C0, n0, m0)
    h = h * lax.rsqrt(jnp.mean(h * h, -1, keepdims=True) + RMS_EPS)
    y_c = (jax.nn.sigmoid(mo.astype(jnp.float32)) * h.reshape(B, S, MLSTM_W)
           * mnorm_g.astype(jnp.float32)).astype(x.dtype)
    x = x + jnp.concatenate([y_a, y_b, y_c], axis=-1) @ w_out
    x = x + peer(rmsnorm(x, norm2_g), pwq, psub, pu, pv)
    return x, (nsa_rows, win_state, conv_new, C, n, m)

def setup_inputs(seed: int = 0) -> dict:
    key = jax.random.key(seed)
    ks = jax.random.split(key, 24)
    f32 = jnp.float32
    n_pages = PAST_LEN // PAGE_SIZE
    n_phys = (5 * DEC_BATCH * n_pages + 3) // 4
    win_buf = min(WINDOW, PAST_LEN)
    nrm = lambda k, shape, s: s * jax.random.normal(k, shape, f32)
    page_table = jax.random.permutation(ks[0], n_phys)[: DEC_BATCH * n_pages].reshape(DEC_BATCH, n_pages).astype(jnp.int32)
    gate_b = jnp.stack([nrm(ks[1], (DEPTH, MLSTM_HEADS), 0.1),
                        3.0 + nrm(ks[2], (DEPTH, MLSTM_HEADS), 0.5)], axis=1)
    return {
        'x_prompt': nrm(ks[3], (BATCH, SEQ, D_MODEL), 1.0),
        'x_sample': nrm(ks[4], (DEC_BATCH, DEC_SEQ, D_MODEL), 1.0),
        'cache_nsa_kv': nrm(ks[5], (DEPTH, n_phys, PAGE_SIZE, 4, NSA_KV_HEADS, HEAD_DIM), 1.0),
        'state_win_kv': nrm(ks[6], (DEPTH, DEC_BATCH, win_buf, 2, NSA_KV_HEADS, HEAD_DIM), 1.0),
        'state_conv': nrm(ks[7], (DEPTH, DEC_BATCH, CONV_K - 1, CONV_W), 1.0),
        'state_mlstm_C': nrm(ks[8], (DEPTH, DEC_BATCH, MLSTM_HEADS, MLSTM_DH, MLSTM_DH), 0.3),
        'state_mlstm_n': nrm(ks[9], (DEPTH, DEC_BATCH, MLSTM_HEADS, MLSTM_DH), 0.3),
        'state_mlstm_m': nrm(ks[10], (DEPTH, DEC_BATCH, MLSTM_HEADS), 0.5),
        'page_table': page_table,
        'norm1_g': 1.0 + nrm(ks[11], (DEPTH, D_MODEL), 0.1),
        'w_in': nrm(ks[12], (DEPTH, D_MODEL, IN_COLS), D_MODEL ** -0.5),
        'conv_w': nrm(ks[13], (DEPTH, CONV_K, CONV_W), CONV_K ** -0.5),
        'mlstm_gate_b': gate_b,
        'mlstm_norm_g': 1.0 + nrm(ks[14], (DEPTH, MLSTM_W), 0.1),
        'w_out': nrm(ks[15], (DEPTH, MIX_W, D_MODEL), MIX_W ** -0.5),
        'norm2_g': 1.0 + nrm(ks[16], (DEPTH, D_MODEL), 0.1),
        'peer_wq': nrm(ks[17], (DEPTH, D_MODEL, PEER_HEADS * PEER_DKEY), D_MODEL ** -0.5),
        'peer_subkeys': nrm(ks[18], (DEPTH, PEER_HEADS, 2, PEER_NKEYS, PEER_DKEY // 2), (PEER_DKEY // 2) ** -0.5),
        'peer_u': nrm(ks[19], (DEPTH, PEER_EXPERTS, D_MODEL), D_MODEL ** -0.5),
        'peer_v': nrm(ks[20], (DEPTH, PEER_EXPERTS, D_MODEL), PEER_HEADS ** -0.5),
        'final_norm_g': 1.0 + nrm(ks[21], (D_MODEL,), 0.1),
    }

def reference(x_prompt, x_sample, cache_nsa_kv, state_win_kv, state_conv, state_mlstm_C, state_mlstm_n,
              state_mlstm_m, page_table, norm1_g, w_in, conv_w, mlstm_gate_b, mlstm_norm_g, w_out, norm2_g,
              peer_wq, peer_subkeys, peer_u, peer_v, final_norm_g):
    xp, xs = x_prompt, x_sample
    bp = xp.shape[0]
    p_st, s_st = [], []
    for l in range(DEPTH):
        lw = (norm1_g[l], w_in[l], conv_w[l], mlstm_gate_b[l], mlstm_norm_g[l], w_out[l], norm2_g[l],
              peer_wq[l], peer_subkeys[l], peer_u[l], peer_v[l])
        xp, st = hybrid_layer(xp, lw,
                              jnp.zeros((bp, CONV_K - 1, CONV_W), xp.dtype),
                              jnp.zeros((bp, MLSTM_HEADS, MLSTM_DH, MLSTM_DH), jnp.float32),
                              jnp.zeros((bp, MLSTM_HEADS, MLSTM_DH), jnp.float32),
                              jnp.zeros((bp, MLSTM_HEADS), jnp.float32),
                              nsa_prompt)
        p_st.append(st)
        xs, st = hybrid_layer(xs, lw, state_conv[l], state_mlstm_C[l], state_mlstm_n[l], state_mlstm_m[l],
                              make_nsa_sample(cache_nsa_kv, l, page_table, state_win_kv[l]))
        s_st.append(st)
    p_rows, p_win, p_conv, p_C, p_n, p_m = [jnp.stack(a) for a in zip(*p_st)]
    s_rows, s_win, s_conv, s_C, s_n, s_m = [jnp.stack(a) for a in zip(*s_st)]
    y_prompt = rmsnorm(xp, final_norm_g)
    y_sample = rmsnorm(xs, final_norm_g)
    return (y_prompt, y_sample, p_rows, p_win, p_conv, p_C, p_n, p_m, s_rows, s_win, s_conv, s_C, s_n, s_m)


_drawn_inputs = setup_inputs


def setup_inputs(seed=0):
    import zlib

    import numpy as np

    out = dict(_drawn_inputs(seed))
    spreads = {}
    factors = {}
    for name, (base, spread) in spreads.items():
        noise = np.random.default_rng([zlib.crc32(name.encode()), seed]).standard_normal(out[name].shape)
        drawn = base * np.exp(spread * noise) if base else spread * noise
        out[name] = jnp.asarray(drawn.astype(out[name].dtype))
    for name, factor in factors.items():
        out[name] = (out[name] * factor).astype(out[name].dtype)
    return out
```

```python
from contextlib import ExitStack

import numpy as np

import concourse.bass as bass
from concourse import mybir

F32 = mybir.dt.float32
I32 = mybir.dt.int32
U32 = mybir.dt.uint32
ALU = mybir.AluOpType
ACT = mybir.ActivationFunctionType
AX = mybir.AxisListType.X

P = 128
D = 2048
SEQ, DEC_B, DEC_S = 256, 8, 8
PAST, PAGE = 2048, 128
NPAGE = PAST // PAGE
CONV_W, NSA_W, ML_W = 512, 1024, 512
HD, KVH, GRP = 64, 4, 4
HEADS = KVH * GRP
WIN = 512
MH, DH = 4, 128
PH, NKEY, TOPK = 8, 128, 16
EPS = 1e-6
NEG = -1e30
BIG = 1e9
GELU_C = 2.0 * (2.0 / np.pi) ** 0.5
GELU_K = 0.044715

CB, CC, CH = 0, 512, 1024
ZQ = 1536
ZKV = 2560
ZG = 4096
ZMQ, ZMK, ZMV, ZMO = 4144, 4656, 5168, 5680
ZMI, ZMF = 6192, 6196
ZC = 6200

TILES = 3
ROWS = [128, 128, 64]
KT = D // P
TOK = SEQ + DEC_B * DEC_S

WC = 512
NFULL = ZC // WC
TAIL = ZC - NFULL * WC
NSLOT = 4


def constants():
    r = np.arange(P)
    parts = {}
    parts["ident"] = np.eye(P)
    parts["ones"] = np.ones((P, P))
    parts["tri"] = (r[:, None] <= r[None, :]) * 1.0
    s = np.arange(64)
    same = (s[:, None] // 8 == s[None, :] // 8)
    parts["blocktri"] = np.concatenate([(same & (s[:, None] <= s[None, :])) * 1.0, np.zeros((64, 64))])
    parts["causal"] = np.where(r[None, :] <= r[:, None], 0.0, NEG)
    parts["blockcausal"] = np.concatenate([np.where(same & (s[None, :] <= s[:, None]), 0.0, NEG), np.zeros((64, 64))])
    parts["batchmask"] = np.concatenate([(s[:, None] // 8 == np.arange(8)[None, :]) * 1.0, np.zeros((64, 8))])
    parts["lastmask"] = np.concatenate([(s[:, None] == 8 * np.arange(8)[None, :] + 7) * 1.0, np.zeros((64, 8))])
    parts["lastrow"] = (r[:, None] == 127) * np.ones((P, P))
    parts["blocklast"] = np.concatenate([(s[:, None] == 8 * (s[None, :] // 8) + 7) * 1.0, np.zeros((64, 64))])
    e8 = np.zeros((P, 64))
    e8[:8] = (np.arange(8)[:, None] == s[None, :] // 8)
    parts["spread"] = e8
    y = np.arange(248) - 120
    parts["compress"] = ((16 * y[None, :] <= r[:, None]) & (r[:, None] < 16 * y[None, :] + 32)) / 32.0
    c = np.arange(16)
    for t in range(2):
        q = t * 128 + r
        parts["cmpneg%d" % t] = np.where(16 * c[None, :] + 31 <= q[:, None], 0.0, NEG)
        parts["cmpone%d" % t] = (16 * c[None, :] + 31 <= q[:, None]) * 1.0
    kv, q = r // 32, r % 8
    parts["groupsum"] = ((kv[:, None] == kv[None, :]) & (q[:, None] == q[None, :])) * 1.0
    j = np.arange(8)
    parts["newneg"] = np.where(j[None, :] <= q[:, None], 0.0, NEG)
    parts["oldneg"] = np.where(j[None, :] > q[:, None], 0.0, NEG)
    parts["headmask"] = (r[:, None] // 16 == np.arange(8)[None, :]) * 1.0
    parts["iota16"] = np.ones((P, 1)) * c[None, :]
    at, cols, n = {}, [], 0
    for k, v in parts.items():
        at[k] = (n, n + v.shape[1])
        n += v.shape[1]
        cols.append(v)
    return at, np.ascontiguousarray(np.concatenate(cols, axis=1).astype(np.float32))


class Counts:

    def __init__(self, eng):
        self.eng, self.n, self.i, self.per, self.base = eng, {}, None, {}, {}

    def value(self, sem):
        if self.i is not None and sem in self.per:
            return self.i * self.per[sem] + (self.base.get(sem, 0) + self.n.get(sem, 0))
        return self.n.get(sem, 0)

    def sig(self, ins, sem, amount=1):
        assert self.i is None or sem in self.per, "a semaphore without a count for this loop"
        self.n[sem] = self.n.get(sem, 0) + amount
        ins.then_inc(sem, amount)

    def own(self, ins, sem):
        self.sig(ins, sem)
        self.eng.wait_ge(sem, self.value(sem))

    def enter(self, i, per):
        self.i, self.per = i, per
        self.base = {s: self.n.get(s, 0) for s in per}
        for s in per:
            self.n[s] = 0

    def leave(self, count):
        for s, k in self.per.items():
            assert self.n[s] == k, ("per iteration", self.n[s], "stated", k)
            self.n[s] = self.base[s] + count * k
        self.i, self.per = None, {}


def bc(ap, shape):
    return ap.to_broadcast(shape)


def hybrid_step(nc, at, ncol, const, x_prompt, x_sample, cache_nsa_kv, state_win_kv, state_conv, state_mlstm_C,
                state_mlstm_n, state_mlstm_m, page_table, norm1_g, w_in, conv_w, mlstm_gate_b, mlstm_norm_g,
                w_out, norm2_g, peer_wq, peer_subkeys, peer_u, peer_v, final_norm_g,
                y_prompt, y_sample, p_rows, p_win, p_conv, p_C, p_n, p_m,
                s_rows, s_win, s_conv, s_C, s_n, s_m,
                new_kv, conv_ext, branch_out):
    with ExitStack() as ctx:
        def sem(name):
            return ctx.enter_context(nc.semaphore(name))

        A, B, C, DD = 0, 18600, 34984, 41128
        CONST = DD + 3840
        SMALL = CONST + ncol
        TEMP = SMALL + 552
        ARENA = TEMP + 6224

        arena = ctx.enter_context(nc.sbuf_tensor("arena", [P, ARENA], F32))

        def mem(start, cols):
            assert start + cols <= ARENA
            return arena[:, start:start + cols]

        def mem3(start, a, b):
            return mem(start, a * b).rearrange("p (a b) -> p a b", a=a)

        Z = mem3(A, TILES, ZC)
        XN, JUNK0 = mem3(A, TILES, D), mem(A + TILES * D, D)
        RING = mem(B, NSLOT * 8 * WC).rearrange("p (s k n) -> p s k n", s=NSLOT, k=8)
        TAILW = mem3(B, KT, TAIL)
        XT = mem3(C, KT, TOK)
        Y = mem3(C, TILES, D)
        QT, KTS, KTW = mem3(DD, 8, TOK), mem3(DD + 8 * TOK, 2, TOK), mem3(DD + 10 * TOK, 2, TOK)
        PAGES = mem3(B, NPAGE, 1024)
        SS, SW, PC = mem(TEMP, 2056), mem(TEMP + 2056, 520), mem(TEMP + 2576, 128)
        KTG = mem3(TEMP + 2704, 2, 512)
        PTB = mem3(TEMP + 3728, 2, 512)
        CK, CV = mem3(TEMP + 4752, 2, 128), mem(TEMP + 5008, 256)
        QB = mem3(TEMP + 5264, 2, 128)
        VN = mem3(TEMP + 5520, 2, 256)
        OROW = mem3(TEMP + 6032, 3, 64)
        assert TEMP + 6224 <= ARENA
        OS = mem3(TEMP, 3, 1024)
        PP = mem(TEMP, 2048).rearrange("p (u g n) -> p u g n", u=2, g=4)
        PPT = mem3(TEMP + 2048, 2, 512)
        PCM = mem3(TEMP + 3072, 2, 256)
        PCT = mem3(TEMP + 3584, 2, 256)
        VBD = mem3(TEMP + 4096, 2, 512)
        KC = mem3(TEMP + 5120, 2, 16)
        OTMP = mem(TEMP + 5152, 512)
        CREP = mem3(TEMP + 5664, 2, 128)
        MQT, MKT = mem3(TEMP, MH, TOK), mem3(TEMP + MH * TOK, MH, TOK)
        MT = TEMP + 2 * MH * TOK
        MD = mem(MT, 448)
        MW = mem(MT + 448, 448)
        MWT = mem(MT + 896, 448)
        DG = mem(MT + 1344, 320)
        KW = mem3(MT + 1664, 3, 128)
        HN = mem3(MT + 2048, 3, 128)
        MC = mem3(DD, DEC_B, DH)
        VB = mem3(DD + 1024, DEC_B, DH)
        QCM = mem3(DD + 2048, DEC_B, DH)
        MNG = mem(A + ZC + ZQ, 512)
        CW = mem3(TEMP, 3, 512)
        CT = mem3(TEMP + 1536, TILES, 512)
        ZERO2 = mem(TEMP + 5664, 512)
        JUNK2 = mem(TEMP, D)
        YT = mem3(A, KT, TOK)
        HT = mem3(A, KT, TOK)
        X1 = mem3(A + 5120, TILES, D)
        G2B, GFB = mem(A + 11264, D), mem(A + 13312, D)
        SK = mem3(A + 15360, 16, 128)
        H = mem3(C, TILES, D)
        SKT = mem3(DD, 16, 128)
        QP = mem3(TEMP, 16, TOK)
        SC = mem3(B, TILES, D)
        ACC = mem(DD + 0, D)
        PROD = mem(TEMP, D)
        BUF = mem3(B, 8, D)
        KONST = mem(CONST, ncol)
        SCW = mem3(B + 6144, 16, 128)
        CAND = mem3(B + 8192, PH, 256)
        CANDW = mem3(B + 10240, PH, 256)
        OH = mem(B + 12288, 2048)

        def k_(name):
            a, b = at[name]
            return KONST[:, a:b]

        small_at = [SMALL]

        def small(cols):
            a = small_at[0]
            small_at[0] += cols
            assert small_at[0] <= TEMP
            return arena[:, a:a + cols]

        def small3(a, b):
            return small(a * b).rearrange("p (a b) -> p a b", a=a)

        G1T, G2T = small(KT), small(KT)
        GB = small(8)
        ss, rstd = small(4), small(4)
        WAITED = small(1)
        GATE = small3(TILES, 48)
        PT_ROW = small(128).bitcast(I32)
        smx, ssum, srec = small(4), small(4), small(4)
        blk, blkw = small(33), small(33)
        blkb = small(33)
        top8 = small(8)
        pmx, psm, pfac = small3(2, 4), small3(2, 4), small3(2, 4)
        cmx, csm = small3(2, 16), small3(2, 16)
        mcol_at = [A + ZQ]

        def mcol(a, b):
            mcol_at[0] += a * b
            assert mcol_at[0] <= A + ZQ + 512
            return arena[:, mcol_at[0] - a * b:mcol_at[0]].rearrange("p (a b) -> p a b", a=a)

        ILOG, FLOG, BCUM, GLOG, MMAX, MT1, MT2 = (mcol(TILES, MH) for _ in range(7))
        MLAST, MNEW, WL = mcol(TILES, MH), mcol(TILES, MH), mcol(TILES, MH)
        M0 = mcol(1, MH)[:, 0]
        DECD, DECB = mcol(MH, DEC_B), mcol(MH, DEC_B)
        DEN, QN, EX = mcol(1, 4)[:, 0], mcol(1, 8)[:, 0], mcol(1, 4)[:, 0]
        SSQ, BM, M0B = mcol(TILES, MH), mcol(TILES, MH), mcol(1, MH)[:, 0]
        NT, NO, N32 = mcol(1, 32)[:, 0], mcol(1, 36)[:, 0], mcol(1, 128)[:, 0]
        R0 = DD + 2048
        EIDX, GG = mem3(R0, TILES, 128).bitcast(I32), mem3(R0 + 384, TILES, 128)
        TV = mem3(R0 + 768, 16, TOPK)
        TI = mem3(R0 + 1024, 16, TOPK).bitcast(U32)
        TIF = mem3(R0 + 1280, 16, TOPK)
        CVAL, CPOS = mem3(B + 14336, PH, TOPK), mem3(B + 14464, PH, TOPK).bitcast(U32)
        CHI, CLO = mem3(B + 14592, PH, TOPK).bitcast(U32), mem3(B + 14720, PH, TOPK).bitcast(U32)
        FHI, FLO = mem3(B + 14848, PH, TOPK), mem3(B + 14976, PH, TOPK)
        E1, E2 = mem3(B + 15104, PH, TOPK), mem3(B + 15232, PH, TOPK)
        GSUM = mem(B + 15360, PH)
        CUR = mem3(SMALL + 192, 2, TOPK).bitcast(I32)
        DOTS, GE1, GE2 = mem(SMALL + 224, TOPK), mem(SMALL + 240, TOPK), mem(SMALL + 256, TOPK)
        WV = mem(SMALL + 272, TOPK)
        WCELL = mem(SMALL + 288, 18)

        ps = ctx.enter_context(nc.psum_tensor("ps", [P, 8, 512], F32))

        ld_const, ld_x, ld_small, ld_pt = sem("ld_const"), sem("ld_x"), sem("ld_small"), sem("ld_page_table")
        v_own, a_own, a_xn = sem("vector_step_done"), sem("scalar_step_done"), sem("x_scaled")
        v_ss0, v_rstd1, t_x, v_xt = sem("ss_set"), sem("rstd1_ready"), sem("x_transposed"), sem("xt_stored")
        w_slot = [sem("w_slot%d_in" % s) for s in range(NSLOT)]
        w_used, w_tail = sem("w_slot_used"), sem("w_tail_in")
        z_done, z_evac_a, z_evac_v = sem("z_product_done"), sem("z_by_scalar"), sem("z_by_vector")
        st_kv, st_out = sem("new_kv_stored"), sem("outputs_stored")
        t_qk, v_qk = sem("qk_transposed"), sem("qkt_stored")
        pages_in, win_in, vnew_in = sem("pages_in"), sem("window_in"), sem("new_values_in")
        v_qb, t_cmp, a_cmp, t_kt, a_kt = sem("qb_ready"), sem("cmp_kv_done"), sem("cmp_kv_stored"), sem("keys_transposed"), sem("keys_stored")
        t_wins, t_small, t_sel = sem("win_scores_done"), sem("cmp_new_scores_done"), sem("sel_scores_done")
        v_winm, v_cmpm, v_selm = sem("win_masked"), sem("cmp_max_ready"), sem("sel_masked")
        a_p, v_pc, t_imp = sem("sample_exp_done"), sem("cmp_probs_ready"), sem("importance_done")
        t_pt, a_pt, t_pv, v_or = sem("probs_transposed"), sem("probs_t_stored"), sem("values_done"), sem("branch_rows_ready")
        st_or, ld_os, v_ys = sem("branch_rows_stored"), sem("branch_rows_in"), sem("y_sample_ready")
        a_gate = sem("gate_exp_done")
        v_crep, t_pc, v_pck, t_pcs, v_pcm, a_pce = sem("compress_repeated"), sem("pcmp_kv_done"), sem("pcmp_kv_stored"), sem("pcmp_scores_done"), sem("pcmp_masked"), sem("pcmp_exp_done")
        v_pcp, t_pct, v_pct, t_pcv, v_pcy = sem("pcmp_probs_ready"), sem("pcmp_transposed"), sem("pcmp_t_stored"), sem("pcmp_values_done"), sem("pcmp_y_ready")
        t_us, v_um, a_ue, t_ut, a_ut, t_uv, v_uy = (sem("unit_scores_done"), sem("unit_masked"), sem("unit_exp_done"),
                                                    sem("unit_transposed"), sem("unit_t_stored"), sem("unit_values_done"), sem("unit_y_ready"))
        v_u, st_u, ld_u, ld_cw, v_y = sem("conv_u_ready"), sem("conv_u_stored"), sem("shifted_u_in"), sem("conv_w_in"), sem("y_ready")
        ld_m, t_mt, a_mt, t_mn, v_mn = sem("mlstm_state_in"), sem("mlstm_qk_transposed"), sem("mlstm_qkt_stored"), sem("n_m_spread"), sem("n_m_stored")
        v_mf, a_mf, v_flog, t_bc = sem("gate_columns"), sem("gate_exp_ln_done"), sem("log_forget_ready"), sem("cumsum_done")
        v_dg, t_gr, v_md, a_mw, v_wqk = sem("gate_diag_ready"), sem("weights_scores_done"), sem("log_weights_masked"), sem("mlstm_exp_done"), sem("weighted_scores_ready")
        t_mwt, a_mwt, ld_mc, t_num, v_hn = sem("mlstm_w_transposed"), sem("mlstm_wt_stored"), sem("memory_in"), sem("numerator_done"), sem("head_out_ready")
        v_bm, t_ml, v_wl, a_wl, v_decd, t_decb, v_kw, t_c, v_c, st_c = (
            sem("last_columns_ready"), sem("last_rows_spread"), sem("state_weight_logs"), sem("state_weights_exp"), sem("decay_diag_ready"),
            sem("decay_spread"), sem("weighted_keys_ready"), sem("memory_update_done"), sem("memory_ready"), sem("memory_stored"))
        t_no, v_no, a_sig, v_ssq, a_ssq, ld_g = sem("n_transposed"), sem("n_ready"), sem("out_gate_exp"), sem("head_ss_ready"), sem("head_rms_ready"), sem("mlstm_g_in")
        t_y, v_yt, v_x1, ld_xr, a_ss2, v_ss2, a_h, t_h, v_ht, v_h = (
            sem("y_transposed"), sem("yt_stored"), sem("x1_ready"), sem("x_again_in"), sem("x1_ss"), sem("x1_rstd"), sem("h_scaled"),
            sem("h_transposed"), sem("ht_stored"), sem("h_ready"))
        ld_g2, ld_sk, t_sk, v_sk, a_qp, t_sc, a_sc = (
            sem("norm_g_in"), sem("subkeys_in"), sem("subkeys_transposed"), sem("subkeys_t_stored"), sem("peer_q_stored"),
            sem("key_scores_done"), sem("key_scores_stored"))
        v_cd, a_cd, v_route = sem("candidates_shifted"), sem("gates_exp"), sem("routes_ready")
        g_in = [sem("rows_in%d" % n) for n in range(8)]
        g_used, p_cur = sem("rows_used"), sem("numbers_copied")
        v_dot, v_ge, a_ge, v_acc = sem("dots_done"), sem("gelu_in_ready"), sem("gelu_exp_done"), sem("peer_sum_step")
        v_x2, a_ss3, v_ss3, v_out = sem("x2_ready"), sem("x2_ss"), sem("x2_rstd"), sem("y_out_ready")
        block = ctx.enter_context(nc.Block())

        def w_half(w, c, half):
            return w[0].rearrange("(k p) n -> p k n", p=P)[:, 8 * half:8 * half + 8, bass.ts(c, WC)]

        WINP = [Z[:, w // 2, ZQ + (w % 2) * 512:ZQ + (w % 2) * 512 + 512] for w in range(4)]
        YB = CONV_W
        UNITS = [(t, br, kv) for t in range(2) for br in (1, 2) for kv in range(KVH)]
        UTR = [sum(u[0] + 1 for u in UNITS[:n]) for n in range(len(UNITS) + 1)]

        KVB = ZKV
        SCALE = HD ** -0.5
        TOFF = [0, 128, 256]

        @block.sync
        def _(sp):
            sp.dma_start(KONST, const).then_inc(ld_const, 16)
            sp.dma_start(XN[:, 0:2, :], x_prompt[0].rearrange("(t p) d -> p t d", p=P)).then_inc(ld_x, 16)
            sp.dma_start(XN[0:64, 2, :], x_sample.rearrange("b s d -> (b s) d")).then_inc(ld_x, 16)
            with nc.allow_non_contiguous_dma(reason="vectors laid along partitions"):
                sp.dma_start(G1T, norm1_g[0].rearrange("(k p) -> p k", p=P)).then_inc(ld_small, 16)
                sp.dma_start(G2T, norm2_g[0].rearrange("(k p) -> p k", p=P)).then_inc(ld_small, 16)
            sp.dma_start(GB, mlstm_gate_b.rearrange("a b h -> a (b h)").to_broadcast([P, 8])).then_inc(ld_small, 16)
            sp.dma_start(PT_ROW[0:1, :], page_table.rearrange("(a b) g -> a (b g)", a=1)).then_inc(ld_pt, 16)
            for s in range(NSLOT):
                sp.dma_start(RING[:, s], w_half(w_in, s // 2, s % 2)).then_inc(w_slot[s], 16)
            with sp.Fori(1, NFULL // 2) as i:
                for s in range(NSLOT):
                    sp.wait_ge(w_used, i * NSLOT + (s - 3))
                    sp.dma_start(RING[:, s], w_half(w_in, i * 2 + s // 2, s % 2)).then_inc(w_slot[s], 16)
            sp.wait_ge(w_used, 2 * NFULL - 3)
            sp.dma_start(TAILW, w_in[0].rearrange("(k p) n -> p k n", p=P)[:, :, NFULL * WC:]).then_inc(w_tail, 16)
            sp.wait_ge(z_evac_a, 4 + 2 * NFULL + 2)
            sp.wait_ge(z_evac_v, 2 + NFULL + 1)
            sp.dma_start(new_kv, Z[0:64, 2, KVB:KVB + 1536]).then_inc(st_kv, 16)
            sp.dma_start(p_rows[0, 0].rearrange("(t p) a h d -> p t (a h d)", p=P), Z[:, 0:2, KVB:KVB + 1024]).then_inc(st_out, 16)
            sp.dma_start(p_win[0, 0].rearrange("(t p) a h d -> p t (a h d)", p=P), Z[:, 0:2, KVB + 1024:KVB + 1536]).then_inc(st_out, 16)
            sp.dma_start(s_rows[0].rearrange("b s a h d -> (b s) (a h d)"), Z[0:64, 2, KVB:KVB + 1024]).then_inc(st_out, 16)
            sp.dma_start(s_win[0].rearrange("b w a h d -> b w (a h d)")[:, 0:WIN - 8],
                         state_win_kv[0].rearrange("b w a h d -> b w (a h d)")[:, 8:WIN]).then_inc(st_out, 16)
            sp.wait_ge(st_kv, 16)
            sp.dma_start(s_win[0].rearrange("b w a h d -> b w (a h d)")[:, WIN - 8:WIN],
                         new_kv.rearrange("(b s) n -> b s n", s=8)[:, :, 1024:1536]).then_inc(st_out, 16)
            sp.wait_ge(ld_pt, 16)
            sp.wait_ge(v_qk, 20)
            with sp.Fori(0, DEC_B) as b:
                sp.wait_ge(t_pv, b * 7 + 7)
                for g in range(NPAGE):
                    page = sp.value_load(PT_ROW[0:1, bass.ds(b * NPAGE + g, 1)], min_val=0, max_val=159)
                    sp.dma_start(PAGES[:, g, :],
                                 cache_nsa_kv[0].rearrange("g p a h d -> g p (a h d)")[bass.ds(page, 1)].rearrange("g p n -> (g p) n")
                                 ).then_inc(pages_in, 16)
                for w in range(4):
                    sp.dma_start(WINP[w], state_win_kv[0].rearrange("b (w p) a h d -> b w p (a h d)", p=P)[bass.ds(b, 1), w]
                                 .rearrange("b p n -> (b p) n")).then_inc(win_in, 16)
                for n in range(2):
                    sp.dma_start(VN[0:8, n, :], new_kv.rearrange("(b s) n -> b s n", s=8)[bass.ds(b, 1), :, 768 + 512 * n:1024 + 512 * n]
                                 .rearrange("b s n -> (b s) n")).then_inc(vnew_in, 16)
                sp.wait_ge(v_or, b + 2)
                for n in range(3):
                    sp.dma_start(branch_out[n].rearrange("b q h d -> b h q d")[bass.ds(b, 1)].rearrange("b h q d -> (b h) q d"),
                                 OROW[:, n, :]).then_inc(st_or, 16)
            sp.wait_ge(st_or, 48 * DEC_B + 48)
            sp.wait_ge(t_pv, 7 * DEC_B + 7)
            for n in range(3):
                sp.dma_start(OS[0:64, n, :], branch_out[n].rearrange("b q h d -> (b q) (h d)")).then_inc(ld_os, 16)
            ext_s = conv_ext[258:338].rearrange("(b s) n -> b s n", s=10)
            sp.wait_ge(v_u, 3)
            sp.dma_start(conv_ext[0:2], ZERO2[0:2]).then_inc(st_u, 16)
            sp.dma_start(conv_ext[2:258].rearrange("(t p) n -> p t n", p=P), Z[:, 0:2, CC:CC + 512]).then_inc(st_u, 16)
            sp.dma_start(ext_s[:, 0:2], state_conv[0]).then_inc(st_u, 16)
            sp.dma_start(ext_s[:, 2:10], Z[0:64, 2, CC:CC + 512]).then_inc(st_u, 16)
            for s in range(NSLOT):
                sp.dma_start(RING[:, s], w_half(w_out, s // 2, s % 2)).then_inc(w_slot[s], 16)
            sp.dma_start(MNG, mlstm_norm_g.to_broadcast([P, 512])).then_inc(ld_g, 16)
            sp.dma_start(N32[0:32], state_mlstm_n[0].rearrange("b h d -> (b h) d")).then_inc(ld_m, 16)
            sp.dma_start(M0B[0:8], state_mlstm_m[0]).then_inc(ld_m, 16)
            sp.wait_ge(st_u, 64)
            sp.dma_start(p_conv[0, 0], conv_ext[256:258]).then_inc(st_out, 16)
            sp.dma_start(s_conv[0], ext_s[:, 8:10]).then_inc(st_out, 16)
            for j, o in ((0, ZQ + 512), (1, CH)):
                sp.dma_start(Z[:, 0:2, o:o + 512], conv_ext[j:j + 256].rearrange("(t p) n -> p t n", p=P)).then_inc(ld_u, 16)
                sp.dma_start(Z[0:64, 2, o:o + 512], ext_s[:, j:j + 8]).then_inc(ld_u, 16)
            for n in range(2 * MH):
                h = n % MH
                if n == 0:
                    sp.wait_ge(v_uy, 16)
                elif n <= MH:
                    sp.wait_ge(t_num, n)
                else:
                    sp.wait_ge(st_c, 16 * (2 * (n - MH)))
                sp.dma_start(MC, state_mlstm_C[0].rearrange("b h d e -> h d b e")[h]).then_inc(ld_mc, 16)
                if n >= MH:
                    sp.wait_ge(v_c, n - MH + 1)
                    sp.dma_start(s_C[0].rearrange("b h d e -> h d b e")[h], MC).then_inc(st_c, 16)
                    sp.dma_start(p_C[0, 0, h], HN[:, 0]).then_inc(st_c, 16)
            sp.wait_ge(v_no, 1)
            sp.dma_start(s_n[0].rearrange("b h d -> (b h) d"), N32[0:32]).then_inc(st_out, 16)
            sp.dma_start(p_n[0, 0], N32[32:36]).then_inc(st_out, 16)
            sp.dma_start(p_m[0], MNEW[0:1, 1]).then_inc(st_out, 16)
            for b in range(DEC_B):
                sp.dma_start(s_m[0, b:b + 1], MNEW[8 * b:8 * b + 1, 2]).then_inc(st_out, 16)
            sp.wait_ge(st_c, 32 * MH)
            sp.dma_start(CW, conv_w.rearrange("a k n -> a (k n)").to_broadcast([P, 1536])).then_inc(ld_cw, 16)
            sp.wait_ge(v_y, 1)
            sp.wait_ge(st_out, 16 * 18)
            sp.dma_start(X1[:, 0:2, :], x_prompt[0].rearrange("(t p) d -> p t d", p=P)).then_inc(ld_xr, 16)
            sp.dma_start(X1[0:64, 2, :], x_sample.rearrange("b s d -> (b s) d")).then_inc(ld_xr, 16)
            sp.dma_start(G2B, norm2_g.to_broadcast([P, D])).then_inc(ld_g2, 16)
            sp.dma_start(GFB, final_norm_g.rearrange("(a n) -> a n", a=1).to_broadcast([P, D])).then_inc(ld_g2, 16)
            sp.dma_start(SK, peer_subkeys[0].rearrange("h c n d -> n (h c) d")).then_inc(ld_sk, 16)
            for n in range(28, 40):
                w = w_out if n < 32 else peer_wq
                sp.wait_ge(w_used, n - 3)
                sp.dma_start(RING[:, n % 4], w_half(w, (n - 24) % 8 // 2, n % 2)).then_inc(w_slot[n % 4], 16)
            sp.wait_ge(v_out, 3)
            sp.dma_start(y_prompt[0].rearrange("(t p) d -> p t d", p=P), X1[:, 0:2]).then_inc(st_out, 16)
            sp.dma_start(y_sample.rearrange("b s d -> (b s) d"), X1[0:64, 2]).then_inc(st_out, 16)
            sp.wait_ge(st_out, 16 * 20)


        @block.tensor
        def _(pe):
            cnt = Counts(pe)
            ident = k_("ident")
            pe.wait_ge(ld_const, 16)
            for n in range(TILES * 4):
                t, j = n // 4, n % 4
                pe.wait_ge(a_xn, t + 1)
                if n >= 8:
                    pe.wait_ge(v_xt, n - 7)
                for q in range(4):
                    k = 4 * j + q
                    last = nc.tensor.transpose(ps[:, n % 8, q * 128:q * 128 + ROWS[t]], XN[0:ROWS[t], t, k * 128:(k + 1) * 128],
                                               ident[0:ROWS[t], 0:ROWS[t]])
                last.then_inc(t_x, 1)
            pe.wait_ge(v_xt, 12)

            def product(lhs, slots, banks, n_cols=WC):
                for half in range(2):
                    s, arrived = slots[half]
                    pe.wait_ge(w_slot[s], arrived)
                    for t in range(TILES):
                        for j in range(8):
                            k = 8 * half + j
                            last = nc.tensor.matmul(ps[0:ROWS[t], banks[t], :], lhs[:, k, TOFF[t]:TOFF[t] + ROWS[t]],
                                                    RING[:, s, j, :], start=(k == 0), stop=(k == KT - 1))
                    last.then_inc(w_used, 1)

            with pe.Fori(0, NFULL // 2) as i:
                for c in range(2):
                    pe.wait_ge(z_evac_a, i * 4 + 2 * c + 2)
                    pe.wait_ge(z_evac_v, i * 2 + c + 1)
                    product(XT, [(2 * c, i * 16 + 16), (2 * c + 1, i * 16 + 16)], [3 * c, 3 * c + 1, 3 * c + 2])
            pe.wait_ge(w_tail, 16)
            pe.wait_ge(z_evac_a, 2 * NFULL + 2)
            pe.wait_ge(z_evac_v, NFULL + 1)
            for t in range(TILES):
                for k in range(KT):
                    last = nc.tensor.matmul(ps[0:ROWS[t], t, 0:TAIL], XT[:, k, TOFF[t]:TOFF[t] + ROWS[t]], TAILW[:, k, :],
                                            start=(k == 0), stop=(k == KT - 1))
            last.then_inc(z_done, 1)
            for n in range(12):
                o = ZQ + 128 * n if n < 8 else KVB + 512 * (1 + (n - 8) // 2) + 128 * (n % 2)
                cols = [Z[0:ROWS[t], t, o:o + 128] for t in range(TILES)]
                if n == 0:
                    pe.wait_ge(z_evac_a, 2 * NFULL + 6)
                    pe.wait_ge(z_evac_v, NFULL + 3)
                if n >= 8:
                    pe.wait_ge(v_qk, 2 * (n - 7))
                for t in range(TILES):
                    last = nc.tensor.transpose(ps[:, n % 8, TOFF[t]:TOFF[t] + ROWS[t]], cols[t], ident[0:ROWS[t], 0:ROWS[t]])
                last.then_inc(t_qk, 1)
            pe.sem_inc(t_pv, 7)
            pe.wait_ge(v_qk, 20)

            comp = k_("compress")
            with pe.Fori(0, DEC_B) as b:
                pe.wait_ge(v_or, b + 1)
                pe.wait_ge(pages_in, b * 256 + 256)
                for hp in range(2):
                    for g in range(NPAGE):
                        nc.tensor.matmul(ps[:, 6, hp * 128:hp * 128 + 128], PAGES[:, g, hp * 128:hp * 128 + 128],
                                         comp[:, 120 - 8 * g:248 - 8 * g], start=(g == 0), stop=(g == NPAGE - 1))
                for g in range(NPAGE):
                    last = nc.tensor.matmul(ps[:, 6, 256:512], comp[:, 120 - 8 * g:248 - 8 * g], PAGES[:, g, 256:512],
                                            start=(g == 0), stop=(g == NPAGE - 1))
                last.then_inc(t_cmp, 1)
                pe.wait_ge(win_in, b * 64 + 64)
                for hp in range(2):
                    for w in range(4):
                        last = nc.tensor.transpose(ps[:, 4 + hp, w * 128:w * 128 + 128], WINP[w][:, hp * 128:hp * 128 + 128], ident)
                last.then_inc(t_kt, 1)
                pe.wait_ge(v_qb, b * 4 + 4)
                pe.wait_ge(a_cmp, b * 2 + 2)
                pe.wait_ge(a_kt, b * 5 + 1)
                for hp in range(2):
                    last = nc.tensor.matmul(ps[:, 6, :], QB[:, hp], KTG[:, hp], start=(hp == 0), stop=(hp == 1))
                last.then_inc(t_wins, 1)
                for hp in range(2):
                    nc.tensor.matmul(ps[:, 7, 0:128], QB[:, hp], CK[:, hp], start=(hp == 0), stop=(hp == 1))
                for o, keys in ((128, KTS), (136, KTW)):
                    for hp in range(2):
                        last = nc.tensor.matmul(ps[:, 7, o:o + 8], QB[:, hp], keys[:, hp, bass.ds(b * 8 + SEQ, 8)],
                                                start=(hp == 0), stop=(hp == 1))
                last.then_inc(t_small, 1)
                for g in range(4):
                    for hp in range(2):
                        for q in range(4):
                            last = nc.tensor.transpose(ps[:, 4 + hp, q * 128:q * 128 + 128],
                                                       PAGES[:, 4 * g + q, 512 + hp * 128:640 + hp * 128], ident)
                    last.then_inc(t_kt, 1)
                    pe.wait_ge(a_kt, b * 5 + g + 2)
                    for hp in range(2):
                        last = nc.tensor.matmul(ps[:, g, :], QB[:, hp], KTG[:, hp], start=(hp == 0), stop=(hp == 1))
                    last.then_inc(t_sel, 1)
                pe.wait_ge(v_pc, b + 1)
                nc.tensor.matmul(ps[:, 7, 0:128], k_("groupsum"), PC, start=True, stop=True).then_inc(t_imp, 1)

                def turn(n):
                    bank = 4 + n % 2
                    if n == 0:
                        last = nc.tensor.transpose(ps[:, bank, 0:128], PC, ident)
                    elif n == 1:
                        pe.wait_ge(a_p, b * 3 + 2)
                        for w in range(4):
                            last = nc.tensor.transpose(ps[:, bank, w * 128:w * 128 + 128], SW[:, w * 128:w * 128 + 128], ident)
                    elif n == 2:
                        pe.wait_ge(a_p, b * 3 + 3)
                        nc.tensor.transpose(ps[0:8, bank, 0:128], SW[:, 512:520], ident)
                        last = nc.tensor.transpose(ps[0:8, bank, 128:256], SS[:, 2048:2056], ident)
                    else:
                        for q in range(4):
                            o = (n - 3) * 512 + q * 128
                            last = nc.tensor.transpose(ps[:, bank, q * 128:q * 128 + 128], SS[:, o:o + 128], ident)
                    last.then_inc(t_pt, 1)

                def values(n):
                    pe.wait_ge(a_pt, b * 7 + n + 1)
                    if n == 0:
                        pe.wait_ge(v_winm, b + 1)
                        last = nc.tensor.matmul(ps[:, 6, 0:256], PTB[:, 0, 0:128], CV, start=True, stop=True)
                    elif n == 1:
                        for w in range(4):
                            last = nc.tensor.matmul(ps[:, 6, 256:512], PTB[:, 1, w * 128:w * 128 + 128], WINP[w][:, 256:512],
                                                    start=(w == 0), stop=False)
                    elif n == 2:
                        pe.wait_ge(vnew_in, b * 32 + 32)
                        nc.tensor.matmul(ps[:, 6, 256:512], PTB[0:8, 0, 0:128], VN[0:8, 1], start=False, stop=True)
                        last = nc.tensor.matmul(ps[:, 7, 256:512], PTB[0:8, 0, 128:256], VN[0:8, 0], start=True, stop=False)
                    else:
                        for q in range(4):
                            last = nc.tensor.matmul(ps[:, 7, 256:512], PTB[:, n % 2, q * 128:q * 128 + 128],
                                                    PAGES[:, (n - 3) * 4 + q, 768:1024], start=False, stop=(n == 6 and q == 3))
                    last.then_inc(t_pv, 1)

                turn(0)
                for n in range(7):
                    if n < 6:
                        turn(n + 1)
                    values(n)

            pe.wait_ge(v_or, DEC_B + 1)
            for hp in range(2):
                for t in range(2):
                    nc.tensor.matmul(ps[:, 0, hp * 16:hp * 16 + 16], Z[:, t, KVB + hp * 128:KVB + hp * 128 + 128],
                                     comp[:, 120 - 8 * t:136 - 8 * t], start=(t == 0), stop=(t == 1))
            for t in range(2):
                pe.wait_ge(v_crep, t + 1)
                last = nc.tensor.matmul(ps[:, 1, 0:256], CREP[:, t],
                                        Z[:, t, KVB + 256:KVB + 512], start=(t == 0), stop=(t == 1))
            last.then_inc(t_pc, 1)
            pe.wait_ge(v_pck, 5)
            for t in range(2):
                for h in range(HEADS):
                    hp, e, g = h // 8, h // 4 % 2, h % 4
                    last = nc.tensor.matmul(ps[:, 2 + 2 * t + e, (hp * 4 + g) * 16:(hp * 4 + g) * 16 + 16], QT[64 * e:64 * e + 64, hp * 4 + g, t * 128:t * 128 + 128],
                                            KC[64 * e:64 * e + 64, hp], start=True, stop=True)
                last.then_inc(t_pcs, 1)
            for t in range(2):
                pe.wait_ge(v_pcp, t + 1)
                for o in range(2):
                    last = nc.tensor.transpose(ps[:, 1 + t, o * 128:o * 128 + 128], PCM[:, t, o * 128:o * 128 + 128], ident)
                last.then_inc(t_pct, 1)
            for t in range(2):
                pe.wait_ge(v_pct, t + 1)
                for o in range(2):
                    nc.tensor.matmul(ps[:, (5, 6, 7, 0)[2 * t + o], :], PCT[:, t, o * 128:o * 128 + 128], VBD[:, o],
                                     start=True, stop=True).then_inc(t_pcv, 1)

            def unit_scores(n):
                t, br, kv = UNITS[n]
                hp, e = kv // 2, kv % 2
                w = (t + 1) * 128
                keys = (KTS, KTW)[br - 1]
                if n >= 2:
                    pe.wait_ge(v_um, n - 1)
                for g in range(GRP):
                    out = ps[:, 2 * (n % 2) + g // 2, (g % 2) * 256:(g % 2) * 256 + w]
                    last = nc.tensor.matmul(out, QT[64 * e:64 * e + 64, hp * 4 + g, t * 128:t * 128 + 128],
                                            keys[64 * e:64 * e + 64, hp, 0:w], start=True, stop=True)
                last.then_inc(t_us, 1)

            pe.wait_ge(v_pcy, 4)
            unit_scores(0)
            for n, (t, br, kv) in enumerate(UNITS):
                if n + 1 < len(UNITS):
                    unit_scores(n + 1)
                pe.wait_ge(a_ue, 4 * n + 4)
                for kt in range(t + 1):
                    for g in range(GRP):
                        last = nc.tensor.transpose(ps[:, 4 + kt, g * 128:g * 128 + 128], PP[:, n % 2, g, kt * 128:kt * 128 + 128], ident)
                    last.then_inc(t_ut, 1)
                pe.wait_ge(a_ut, UTR[n + 1])
                if n >= 2:
                    pe.wait_ge(v_uy, n - 1)
                for g in range(GRP):
                    for kt in range(t + 1):
                        o = KVB + 512 * br + 256 + kv * 64
                        last = nc.tensor.matmul(ps[:, 6 + n % 2, g * 64:g * 64 + 64], PPT[:, kt, g * 128:g * 128 + 128],
                                                Z[:, kt, o:o + 64], start=(kt == 0), stop=(kt == t))
                last.then_inc(t_uv, 1)
            pe.wait_ge(v_uy, 16)
            for n in range(8):
                o = (ZMQ, ZMK)[n // 4] + 128 * (n % 4)
                for t in range(TILES):
                    last = nc.tensor.transpose(ps[:, n, TOFF[t]:TOFF[t] + ROWS[t]], Z[0:ROWS[t], t, o:o + 128], ident[0:ROWS[t], 0:ROWS[t]])
                last.then_inc(t_mt, 1)
            pe.wait_ge(ld_m, 32)
            pe.wait_ge(a_mt, 2)
            nc.tensor.transpose(ps[:, 0, 0:32], N32[0:32, :], ident[0:32, 0:32])
            nc.tensor.matmul(ps[0:64, 1, 0:4], k_("spread")[0:8, :], M0B[0:8, :], start=True, stop=True).then_inc(t_mn, 1)
            pe.wait_ge(v_flog, 2)
            pe.wait_ge(a_mt, 8)
            nc.tensor.matmul(ps[:, 2, 0:4], k_("tri"), FLOG[:, 0], start=True, stop=True)
            nc.tensor.matmul(ps[:, 2, 4:8], k_("ones"), FLOG[:, 0], start=True, stop=False)
            nc.tensor.matmul(ps[:, 2, 4:8], k_("tri"), FLOG[:, 1], start=False, stop=True)
            nc.tensor.matmul(ps[0:64, 2, 8:12], k_("blocktri")[0:64, :], FLOG[0:64, 2], start=True, stop=True).then_inc(t_bc, 1)
            pe.wait_ge(v_mn, 2)
            ones = k_("ones")
            for h in range(MH):
                v = [Z[0:ROWS[t], t, ZMV + h * 128:ZMV + h * 128 + 128] for t in range(TILES)]
                pe.wait_ge(v_dg, 3 * h + 3)
                for t in range(TILES):
                    r = ROWS[t]
                    nc.tensor.matmul(ps[0:r, 0, TOFF[t]:TOFF[t] + r], ones[0:r, 0:r], DG[0:r, TOFF[t]:TOFF[t] + r], start=True, stop=True)
                if h:
                    pe.wait_ge(v_wqk, 3 * h)
                nc.tensor.matmul(ps[:, 1, 0:128], MQT[:, h, 0:128], MKT[:, h, 0:128], start=True, stop=True)
                nc.tensor.matmul(ps[:, 1, 128:384], MQT[:, h, 128:256], MKT[:, h, 0:256], start=True, stop=True)
                nc.tensor.matmul(ps[0:64, 1, 384:448], MQT[:, h, 256:320], MKT[:, h, 256:320], start=True, stop=True).then_inc(t_gr, 1)
                pe.wait_ge(v_wqk, 3 * h + 3)
                for n in range(3):
                    nc.tensor.transpose(ps[:, 2, n * 128:n * 128 + 128], MW[:, n * 128:n * 128 + 128], ident)
                nc.tensor.transpose(ps[0:64, 2, 384:448], MW[0:64, 384:448], ident[0:64, 0:64]).then_inc(t_mwt, 1)
                pe.wait_ge(a_mwt, 2 * h + 2)
                if h:
                    pe.wait_ge(v_hn, h)
                nc.tensor.matmul(ps[:, 3, 0:128], MWT[:, 0:128], v[0], start=True, stop=True)
                nc.tensor.matmul(ps[:, 3, 128:256], MWT[:, 128:256], v[0], start=True, stop=False)
                nc.tensor.matmul(ps[:, 3, 128:256], MWT[:, 256:384], v[1], start=False, stop=True)
                nc.tensor.matmul(ps[0:64, 3, 256:384], MWT[0:64, 384:448], v[2], start=True, stop=True)
                nc.tensor.matmul(ps[0:64, 3, 384:392], MQT[:, h, 256:320], NT.rearrange("p (b h) -> p h b", h=MH)[:, h], start=True, stop=True)
                pe.wait_ge(ld_mc, 16 * h + 16)
                for j in range(2):
                    last = nc.tensor.matmul(ps[0:64, 4 + j, :], MQT[:, h, 256:320], MC[:, 4 * j:4 * j + 4], start=True, stop=True)
                last.then_inc(t_num, 1)
            pe.wait_ge(v_bm, 2)
            pe.wait_ge(v_hn, MH)
            nc.tensor.matmul(ps[:, 0, 0:4], k_("lastrow"), MMAX[:, 1], start=True, stop=True)
            nc.tensor.matmul(ps[:, 0, 8:12], k_("lastrow"), BM[:, 1], start=True, stop=True)
            nc.tensor.matmul(ps[0:64, 0, 4:8], k_("blocklast")[0:64], MMAX[0:64, 2], start=True, stop=True)
            nc.tensor.matmul(ps[0:64, 0, 12:16], k_("blocklast")[0:64], BM[0:64, 2], start=True, stop=True).then_inc(t_ml, 1)
            pe.wait_ge(v_decd, 4)
            nc.tensor.matmul(ps[:, 1, 0:32], ones[0:64], DECD[0:64].rearrange("p h b -> p (h b)"), start=True, stop=True).then_inc(t_decb, 1)
            for h in range(MH):
                v = [Z[0:ROWS[t], t, ZMV + h * 128:ZMV + h * 128 + 128] for t in range(TILES)]
                pe.wait_ge(v_kw, 4 * h + 4)
                if h:
                    pe.wait_ge(v_c, h)
                for t in range(2):
                    nc.tensor.matmul(ps[:, 2, 0:128], KW[:, t], v[t], start=(t == 0), stop=(t == 1))
                for t in range(2):
                    nc.tensor.matmul(ps[:, 2, 128:129], KW[:, t], ones[:, 0:1], start=(t == 0), stop=(t == 1))
                nc.tensor.matmul(ps[:, 2, 136:144], KW[0:64, 2], k_("batchmask")[0:64], start=True, stop=True)
                for j in range(2):
                    last = nc.tensor.matmul(ps[:, 3 + j, :], KW[0:64, 2], VB[0:64, 4 * j:4 * j + 4], start=True, stop=True)
                last.then_inc(t_c, 1)
            pe.wait_ge(v_c, MH)
            nc.tensor.transpose(ps[0:36, 0, 0:128], NO, ident).then_inc(t_no, 1)

            def transposed(src, ready, start, sem_done, sem_stored):
                for n in range(TILES * 4):
                    t, j = n // 4, n % 4
                    pe.wait_ge(ready, start + t)
                    if n >= 8:
                        pe.wait_ge(sem_stored, n - 7)
                    for q in range(4):
                        k = 4 * j + q
                        last = nc.tensor.transpose(ps[:, n % 8, q * 128:q * 128 + ROWS[t]], src[0:ROWS[t], t, k * 128:(k + 1) * 128],
                                                   ident[0:ROWS[t], 0:ROWS[t]])
                    last.then_inc(sem_done, 1)
                pe.wait_ge(sem_stored, 12)

            pe.wait_ge(v_no, 1)
            pe.wait_ge(v_y, 1)
            transposed(Y, v_y, 1, t_y, v_yt)
            for c in range(4):
                if c >= 2:
                    pe.wait_ge(v_x1, 3 * c - 3)
                product(YT, [(2 * (c % 2), 112 + 16 * (c // 2)), (2 * (c % 2) + 1, 112 + 16 * (c // 2))],
                        [3 * (c % 2), 3 * (c % 2) + 1, 3 * (c % 2) + 2])
            pe.wait_ge(v_x1, 12)
            pe.wait_ge(ld_sk, 16)
            for j in range(4):
                for q in range(4):
                    last = nc.tensor.transpose(ps[:, j, q * 128:q * 128 + 128], SK[:, 4 * j + q], ident)
                last.then_inc(t_sk, 1)
            pe.wait_ge(v_sk, 4)
            transposed(H, a_h, 1, t_h, v_ht)
            for c in range(4):
                if c >= 2:
                    pe.wait_ge(a_qp, 4 * c - 4)
                for half in range(2):
                    s = 2 * (c % 2) + half
                    pe.wait_ge(w_slot[s], 144 + 16 * (c // 2))
                    for j in range(4):
                        for k in range(8):
                            last = nc.tensor.matmul(ps[:, 4 * (c % 2) + j, 0:TOK], RING[:, s, k, j * 128:j * 128 + 128], HT[:, 8 * half + k],
                                                    start=(half == 0 and k == 0), stop=(half == 1 and k == 7))
                    last.then_inc(w_used, 1)
            pe.wait_ge(a_qp, 16)
            for t in range(TILES):
                for j in range(4):
                    if t == 2:
                        pe.wait_ge(a_sc, j + 1)
                    for q in range(4):
                        last = nc.tensor.matmul(ps[0:ROWS[t], 4 * (t % 2) + j, q * 128:q * 128 + 128], QP[:, 4 * j + q, TOFF[t]:TOFF[t] + ROWS[t]],
                                                SKT[:, 4 * j + q], start=True, stop=True)
                    last.then_inc(t_sc, 1)


        @block.scalar
        def _(act):
            cnt = Counts(act)
            act.sem_inc(z_evac_a, 4)
            act.wait_ge(ld_x, 32)
            act.wait_ge(v_ss0, 1)
            for t in range(TILES):
                r = ROWS[t]
                nc.scalar.activation(JUNK0[0:r, :], XN[0:r, t, :], ACT.Square, accum_out=ss[0:r, t:t + 1]).then_inc(a_own, 1)
                act.wait_ge(a_own, t + 1)
            act.wait_ge(v_rstd1, 1)
            nc.scalar.activation(rstd[:, 0:3], ss[:, 0:3], ACT.Sqrt).then_inc(a_own, 1)
            act.wait_ge(v_rstd1, 2)
            for t in range(TILES):
                r = ROWS[t]
                nc.scalar.activation(XN[0:r, t, :], XN[0:r, t, :], ACT.Copy, scale=rstd[0:r, t:t + 1]).then_inc(a_xn, 1)
            with act.Fori(0, NFULL // 2) as i:
                for c in range(2):
                    act.wait_ge(w_used, i * 4 + 2 * c + 2)
                    for t in (0, 2):
                        nc.scalar.copy(Z[0:ROWS[t], t, bass.ds(i * 2 * WC + c * WC, WC)], ps[0:ROWS[t], 3 * c + t, :]).then_inc(z_evac_a, 1)
            act.wait_ge(z_done, 1)
            for t in (0, 2):
                nc.scalar.copy(Z[0:ROWS[t], t, NFULL * WC:ZC], ps[0:ROWS[t], t, 0:TAIL]).then_inc(z_evac_a, 1)
            act.wait_ge(z_evac_v, NFULL + 3)
            act.wait_ge(z_evac_a, 2 * NFULL + 6)
            for t in range(TILES):
                nc.scalar.activation(GATE[0:ROWS[t], t], Z[0:ROWS[t], t, ZG:ZG + 48], ACT.Exp, scale=-1.0).then_inc(a_gate, 1)
            with act.Fori(0, DEC_B) as b:
                act.wait_ge(t_cmp, b + 1)
                nc.scalar.copy(CK.rearrange("p a b -> p (a b)"), ps[:, 6, 0:256]).then_inc(a_cmp, 1)
                nc.scalar.copy(CV, ps[:, 6, 256:512]).then_inc(a_cmp, 1)

                def keys(g):
                    act.wait_ge(t_kt, b * 5 + g + 1)
                    if g == 1:
                        act.wait_ge(t_wins, b + 1)
                    elif g > 1:
                        act.wait_ge(t_sel, b * 4 + g - 1)
                    nc.scalar.copy(KTG, ps[:, 4:6, :]).then_inc(a_kt, 1)

                def probs(n):
                    act.wait_ge(t_pt, b * 7 + n + 1)
                    act.wait_ge(t_pv, b * 7 + n + 6)
                    if n == 0:
                        nc.scalar.copy(PTB[:, 0, 0:128], ps[:, 4, 0:128]).then_inc(a_pt, 1)
                    elif n == 2:
                        nc.scalar.copy(PTB[0:8, 0, 0:256], ps[0:8, 4, 0:256]).then_inc(a_pt, 1)
                    else:
                        nc.scalar.copy(PTB[:, n % 2, :], ps[:, 4 + n % 2, :]).then_inc(a_pt, 1)

                keys(0)
                keys(1)
                act.wait_ge(v_cmpm, b + 1)
                nc.scalar.activation(PC[:, 0:127], PC[:, 0:127], ACT.Exp, bias=smx[:, 0:1], scale=SCALE,
                                     accum_out=ssum[:, 0:1]).then_inc(a_p, 1)
                keys(2)
                act.wait_ge(v_winm, b + 1)
                nc.scalar.activation(SW, SW, ACT.Exp, bias=smx[:, 2:3], scale=SCALE, accum_out=ssum[:, 2:3]).then_inc(a_p, 1)
                keys(3)
                keys(4)
                probs(0)
                probs(1)
                act.wait_ge(v_selm, b + 1)
                nc.scalar.activation(SS, SS, ACT.Exp, bias=smx[:, 1:2], scale=SCALE, accum_out=ssum[:, 1:2]).then_inc(a_p, 1)
                for n in range(2, 7):
                    probs(n)
            for t in range(2):
                act.wait_ge(v_pcm, t + 1)
                nc.scalar.activation(PCM[:, t], PCM[:, t], ACT.Exp, scale=SCALE).then_inc(a_pce, 1)

            def unit_exp(n):
                t = UNITS[n][0]
                act.wait_ge(v_um, n + 1)
                for g in range(GRP):
                    row = PP[:, n % 2, g, 0:(t + 1) * 128]
                    nc.scalar.activation(row, row, ACT.Exp, bias=pmx[:, n % 2, g:g + 1], scale=SCALE,
                                         accum_out=psm[:, n % 2, g:g + 1]).then_inc(a_ue, 1)

            unit_exp(0)
            for n, (t, br, kv) in enumerate(UNITS):
                if n + 1 < len(UNITS):
                    unit_exp(n + 1)
                if n >= 1:
                    act.wait_ge(t_uv, n)
                for kt in range(t + 1):
                    act.wait_ge(t_ut, UTR[n] + kt + 1)
                    nc.scalar.copy(PPT[:, kt], ps[:, 4 + kt, :]).then_inc(a_ut, 1)
            act.wait_ge(v_uy, 16)
            for n in range(8):
                act.wait_ge(t_mt, n + 1)
                nc.scalar.copy((MQT, MKT)[n // 4][:, n % 4], ps[:, n, 0:TOK]).then_inc(a_mt, 1)
            act.wait_ge(v_mf, 2)
            parts = ((slice(0, P), slice(0, 2)), (slice(0, 64), slice(2, 3)))
            for r, t in parts:
                nc.scalar.activation(MT2[r, t], MT2[r, t], ACT.Exp, scale=-1.0).then_inc(a_mf, 1)
            act.wait_ge(v_mf, 4)
            for r, t in parts:
                nc.scalar.activation(MT2[r, t], MT2[r, t], ACT.Ln).then_inc(a_mf, 1)
            for h in range(MH):
                act.wait_ge(v_md, h + 1)
                for r, a, b, t in ((P, 0, 128, 0), (P, 128, 384, 1), (64, 384, 448, 2)):
                    nc.scalar.activation(MW[0:r, a:b], MD[0:r, a:b], ACT.Exp, bias=MT1[0:r, t, h:h + 1]).then_inc(a_mw, 1)
                nc.scalar.activation(EX, EX, ACT.Exp).then_inc(a_mw, 1)
                act.wait_ge(t_mwt, h + 1)
                nc.scalar.copy(MWT[:, 0:384], ps[:, 2, 0:384]).then_inc(a_mwt, 1)
                nc.scalar.copy(MWT[0:64, 384:448], ps[0:64, 2, 384:448]).then_inc(a_mwt, 1)
            act.wait_ge(v_wl, 3)
            nc.scalar.activation(WL[:, 0:2], WL[:, 0:2], ACT.Exp).then_inc(a_wl, 1)
            nc.scalar.activation(WL[0:64, 2], WL[0:64, 2], ACT.Exp).then_inc(a_wl, 1)
            nc.scalar.activation(MT1[0:64, 2], MT1[0:64, 2], ACT.Exp).then_inc(a_wl, 1)
            for r, t in parts:
                nc.scalar.activation(Z[r, t, ZMO:ZMO + 512], Z[r, t, ZMO:ZMO + 512], ACT.Exp, scale=-1.0).then_inc(a_sig, 1)
            act.wait_ge(v_ssq, 2)
            for r, t in parts:
                nc.scalar.activation(SSQ[r, t], SSQ[r, t], ACT.Sqrt).then_inc(a_ssq, 1)
            act.wait_ge(v_x1, 12)
            for t in range(TILES):
                r = ROWS[t]
                nc.scalar.activation(JUNK2[0:r], X1[0:r, t], ACT.Square, accum_out=ss[0:r, t:t + 1]).then_inc(a_ss2, 1)
                act.wait_ge(a_ss2, t + 1)
            act.wait_ge(v_ss2, 1)
            nc.scalar.activation(rstd[:, 0:3], ss[:, 0:3], ACT.Sqrt).then_inc(a_ss2, 1)
            act.wait_ge(v_ss2, 2)
            for t in range(TILES):
                r = ROWS[t]
                nc.scalar.activation(H[0:r, t], X1[0:r, t], ACT.Copy, scale=rstd[0:r, t:t + 1]).then_inc(a_h, 1)
            for c in range(4):
                act.wait_ge(w_used, 32 + 2 * c + 2)
                for j in range(4):
                    nc.scalar.copy(QP[:, 4 * c + j], ps[:, 4 * (c % 2) + j, 0:TOK]).then_inc(a_qp, 1)
            for t in range(TILES):
                for j in range(4):
                    act.wait_ge(t_sc, 4 * t + j + 1)
                    nc.scalar.copy(SC[0:ROWS[t], t, j * 512:j * 512 + 512], ps[0:ROWS[t], 4 * (t % 2) + j, :]).then_inc(a_sc, 1)
            for t in range(TILES):
                act.wait_ge(v_cd, t + 1)
                g = GG[0:ROWS[t], t]
                nc.scalar.activation(g, g, ACT.Exp).then_inc(a_cd, 1)
            with act.Fori(0, TILES * PH) as i:
                act.wait_ge(v_ge, i + 1)
                nc.scalar.activation(GE1, GE1, ACT.Exp, scale=-GELU_C).then_inc(a_ge, 1)
            for t in range(TILES):
                r = ROWS[t]
                act.wait_ge(v_x2, t + 1)
                nc.scalar.activation(JUNK2[0:r], X1[0:r, t], ACT.Square, accum_out=ss[0:r, t:t + 1]).then_inc(a_ss3, 1)
                act.wait_ge(a_ss3, t + 1)
            act.wait_ge(v_ss3, 1)
            nc.scalar.activation(rstd[:, 0:3], ss[:, 0:3], ACT.Sqrt).then_inc(a_ss3, 1)


        @block.vector
        def _(dve):
            cnt = Counts(dve)

            def own(ins, plain=False):
                cnt.own(ins, v_own)
                if plain:
                    nc.vector.memset(WAITED, 0.0)

            dve.sem_inc(z_evac_v, 2)
            dve.wait_ge(ld_const, 16)
            nc.vector.memset(ss[:, :], 1.0).then_inc(v_ss0, 1)
            own(nc.vector.memset(QB, 0.0))
            own(nc.vector.memset(PC[:, 127:128], 0.0))
            dve.wait_ge(a_own, 3)
            nc.vector.tensor_scalar(ss[:, 0:3], ss[:, 0:3], 1.0 / D, EPS, ALU.mult, ALU.add).then_inc(v_rstd1, 1)
            dve.wait_ge(a_own, 4)
            nc.vector.reciprocal(rstd[:, 0:3], rstd[:, 0:3]).then_inc(v_rstd1, 1)
            dve.wait_ge(ld_small, 48)
            for n in range(TILES * 4):
                t, j = n // 4, n % 4
                r = ROWS[t]
                dve.wait_ge(t_x, n + 1)
                nc.vector.tensor_tensor(XT[:, 4 * j:4 * j + 4, TOFF[t]:TOFF[t] + r],
                                        ps[:, n % 8].rearrange("p (q n) -> p q n", q=4)[:, :, 0:r],
                                        bc(G1T[:, 4 * j:4 * j + 4].unsqueeze(2), [P, 4, r]), ALU.mult).then_inc(v_xt, 1)
            with dve.Fori(0, NFULL // 2) as i:
                for c in range(2):
                    dve.wait_ge(w_used, i * 4 + 2 * c + 2)
                    nc.vector.tensor_copy(Z[:, 1, bass.ds(i * 2 * WC + c * WC, WC)], ps[:, 3 * c + 1, :]).then_inc(z_evac_v, 1)
            dve.wait_ge(z_done, 1)
            nc.vector.tensor_copy(Z[:, 1, NFULL * WC:ZC], ps[:, 1, 0:TAIL]).then_inc(z_evac_v, 1)
            for n in range(12):
                dve.wait_ge(t_qk, n + 1)
                if n < 8:
                    for x in range(2):
                        e, i = n // 2 % 2, n // 4 * 4 + 2 * (n % 2) + x
                        nc.vector.tensor_copy(QT[64 * e:64 * e + 64, i], ps[64 * x:64 * x + 64, n % 8, 0:TOK]).then_inc(v_qk, 1)
                else:
                    nc.vector.tensor_copy((KTS, KTW)[(n - 8) // 2][:, n % 2], ps[:, n % 8, 0:TOK]).then_inc(v_qk, 1)
            dve.wait_ge(a_gate, 3)
            for t in range(TILES):
                own(nc.vector.tensor_scalar(GATE[0:ROWS[t], t], GATE[0:ROWS[t], t], 1.0, None, ALU.add))
                own(nc.vector.reciprocal(GATE[0:ROWS[t], t], GATE[0:ROWS[t], t]))
            dve.sem_inc(v_or, 1)
            dve.sem_inc(st_or, 48)
            PER_BATCH = 34
            with dve.Fori(0, DEC_B) as b:
                cnt.enter(b, {v_own: PER_BATCH})
                for hp in range(2):
                    for e in range(2):
                        o = (2 * hp + e) * 32
                        nc.vector.tensor_copy(QB[64 * e:64 * e + 64, hp, o:o + 32].rearrange("p (g q) -> p g q", g=GRP),
                                              QT[64 * e:64 * e + 64, hp * 4:hp * 4 + 4, bass.ds(b * 8 + SEQ, 8)]).then_inc(v_qb, 1)
                dve.wait_ge(t_small, b + 1)
                own(nc.vector.tensor_copy(PC[:, 0:127], ps[:, 7, 0:127]))
                own(nc.vector.tensor_tensor(SS[:, 2048:2056], ps[:, 7, 128:136], k_("newneg"), ALU.add))
                own(nc.vector.tensor_tensor(SW[:, 512:520], ps[:, 7, 136:144], k_("newneg"), ALU.add))
                own(nc.vector.reduce_max(smx[:, 0:1], PC[:, 0:127], AX))
                nc.vector.tensor_scalar(smx[:, 0:1], smx[:, 0:1], -SCALE, None, ALU.mult).then_inc(v_cmpm, 1)
                dve.wait_ge(t_wins, b + 1)
                own(nc.vector.tensor_tensor(SW[:, 0:8], ps[:, 6, 0:8], k_("oldneg"), ALU.add))
                own(nc.vector.tensor_copy(SW[:, 8:512], ps[:, 6, 8:512]))
                own(nc.vector.reduce_max(smx[:, 2:3], SW, AX))
                nc.vector.tensor_scalar(smx[:, 2:3], smx[:, 2:3], -SCALE, None, ALU.mult).then_inc(v_winm, 1)
                dve.wait_ge(a_p, b * 3 + 1)
                own(nc.vector.reciprocal(srec[:, 0:1], ssum[:, 0:1]))
                nc.vector.tensor_scalar(PC, PC, srec[:, 0:1], None, ALU.mult).then_inc(v_pc, 1)
                dve.wait_ge(t_imp, b + 1)
                own(nc.vector.reduce_sum(blk[:, 0:32], ps[:, 7, 0:128].rearrange("p (n c) -> p n c", c=4), AX))
                own(nc.vector.memset(blk[:, 0:1], BIG))
                own(nc.vector.memset(blk[:, 31:33], BIG), plain=True)
                own(nc.vector.max(top8, blk), plain=True)
                own(nc.vector.match_replace(blkw, top8, blk, NEG), plain=True)
                own(nc.vector.max(top8, blkw), plain=True)
                own(nc.vector.match_replace(blkw, top8, blkw, NEG))
                own(nc.vector.tensor_tensor(blkb, blk, blkw, ALU.is_equal))
                own(nc.vector.tensor_scalar(blkb, blkb, NEG, None, ALU.mult))
                for g in range(4):
                    dve.wait_ge(t_sel, b * 4 + g + 1)
                    own(nc.vector.tensor_tensor(SS[:, g * 512:g * 512 + 512].rearrange("p (n k) -> p n k", k=64),
                                                ps[:, g].rearrange("p (n k) -> p n k", k=64),
                                                bc(blkb[:, 8 * g:8 * g + 8].unsqueeze(2), [P, 8, 64]), ALU.add))
                own(nc.vector.reduce_max(smx[:, 1:2], SS, AX))
                nc.vector.tensor_scalar(smx[:, 1:2], smx[:, 1:2], -SCALE, None, ALU.mult).then_inc(v_selm, 1)
                dve.wait_ge(a_p, b * 3 + 3)
                own(nc.vector.reciprocal(srec[:, 1:3], ssum[:, 1:3]))
                dve.wait_ge(st_or, b * 48 + 48)
                dve.wait_ge(t_pv, b * 7 + 14)
                for kv in range(KVH):
                    r = slice(32 * kv, 32 * kv + 32)
                    own(nc.vector.tensor_copy(OROW[r, 0], ps[r, 6, 64 * kv:64 * kv + 64]))
                    own(nc.vector.tensor_scalar(OROW[r, 2], ps[r, 6, 256 + 64 * kv:320 + 64 * kv], srec[r, 2:3], None, ALU.mult))
                    ins = nc.vector.tensor_scalar(OROW[r, 1], ps[r, 7, 256 + 64 * kv:320 + 64 * kv], srec[r, 1:2], None, ALU.mult)
                    own(ins) if kv < 3 else ins.then_inc(v_or, 1)
                cnt.leave(DEC_B)
            dve.wait_ge(ld_os, 48)
            gate = GATE[0:64, 2].rearrange("p (h n) -> p n h", n=3)
            for n in range(3):
                o = OS[0:64, n].rearrange("p (h d) -> p h d", d=HD)
                own(nc.vector.tensor_tensor(o, o, bc(gate[:, n].unsqueeze(2), [64, HEADS, HD]), ALU.mult))
            own(nc.vector.tensor_tensor(Y[0:64, 2, YB:YB + NSA_W], OS[0:64, 0], OS[0:64, 1], ALU.add))
            own(nc.vector.tensor_tensor(Y[0:64, 2, YB:YB + NSA_W], Y[0:64, 2, YB:YB + NSA_W], OS[0:64, 2], ALU.add))
            for t in range(2):
                nc.vector.tensor_copy(CREP[:, t].rearrange("p (h c) -> p h c", c=16),
                                      bc(k_("compress")[:, 120 - 8 * t:136 - 8 * t].unsqueeze(1), [P, 8, 16])).then_inc(v_crep, 1)
            dve.wait_ge(t_pc, 1)
            nc.vector.tensor_copy(KC.rearrange("p a b -> p (a b)"), ps[:, 0, 0:32]).then_inc(v_pck, 1)
            for o in range(2):
                for v in range(2):
                    nc.vector.tensor_tensor(VBD[:, o, 256 * v:256 * v + 256].rearrange("p (g d) -> p g d", g=GRP),
                                            bc(ps[:, 1, (2 * o + v) * 64:(2 * o + v) * 64 + 64].unsqueeze(1), [P, GRP, HD]),
                                            bc(k_("headmask")[:, 4 * v:4 * v + 4].unsqueeze(2), [P, GRP, HD]), ALU.mult).then_inc(v_pck, 1)
            for t in range(2):
                s3 = PCM[:, t].rearrange("p (h c) -> p h c", c=16)
                dve.wait_ge(t_pcs, t + 1)
                for e in range(2):
                    own(nc.vector.tensor_tensor(PCM[:, t].rearrange("p (k e g c) -> p e k g c", e=2, k=2, g=GRP)[:, e],
                                                ps[:, 2 + 2 * t + e, 0:128].rearrange("p (k g c) -> p k g c", k=2, g=GRP),
                                                bc(k_("cmpneg%d" % t).unsqueeze(1).unsqueeze(1), [P, 2, GRP, 16]), ALU.add))
                own(nc.vector.reduce_max(cmx[:, t], s3, AX))
                nc.vector.tensor_tensor(s3, s3, bc(cmx[:, t].unsqueeze(2), [P, HEADS, 16]), ALU.subtract).then_inc(v_pcm, 1)
            for t in range(2):
                s3 = PCM[:, t].rearrange("p (h c) -> p h c", c=16)
                dve.wait_ge(a_pce, t + 1)
                nc.vector.tensor_tensor(s3, s3, bc(k_("cmpone%d" % t).unsqueeze(1), [P, HEADS, 16]), ALU.mult).then_inc(v_pcp, 1)
                dve.wait_ge(v_pcp, t + 1)
                own(nc.vector.reduce_sum(csm[:, t], s3, AX))
                own(nc.vector.tensor_scalar(csm[:, t], csm[:, t], 1e-30, None, ALU.max))
                own(nc.vector.reciprocal(csm[:, t], csm[:, t]))
                own(nc.vector.tensor_tensor(csm[:, t], csm[:, t], GATE[:, t].rearrange("p (h n) -> p n h", n=3)[:, 0], ALU.mult))
            for t in range(2):
                dve.wait_ge(t_pct, t + 1)
                nc.vector.tensor_copy(PCT[:, t], ps[:, 1 + t, 0:256]).then_inc(v_pct, 1)
            for t in range(2):
                for o in range(2):
                    dve.wait_ge(t_pcv, 2 * t + o + 1)
                    nc.vector.tensor_tensor(Y[:, t, YB + o * 512:YB + o * 512 + 512].rearrange("p (h d) -> p h d", d=HD),
                                            ps[:, (5, 6, 7, 0)[2 * t + o]].rearrange("p (h d) -> p h d", d=HD),
                                            bc(csm[:, t, 8 * o:8 * o + 8].unsqueeze(2), [P, 8, HD]), ALU.mult).then_inc(v_pcy, 1)

            def unit_mask(n):
                t, br, kv = UNITS[n]
                if n >= 2:
                    dve.wait_ge(t_ut, UTR[n - 1])
                dve.wait_ge(t_us, n + 1)
                src = ps[:, 2 * (n % 2):2 * (n % 2) + 2].rearrange("p b (g n) -> p (b g) n", n=256)
                if t:
                    own(nc.vector.tensor_copy(PP[:, n % 2, :, 0:128], src[:, :, 0:128]))
                own(nc.vector.tensor_tensor(PP[:, n % 2, :, t * 128:t * 128 + 128], src[:, :, t * 128:t * 128 + 128],
                                            bc(k_("causal").unsqueeze(1), [P, GRP, 128]), ALU.add))
                own(nc.vector.reduce_max(pmx[:, n % 2], PP[:, n % 2, :, 0:(t + 1) * 128], AX))
                nc.vector.tensor_scalar(pmx[:, n % 2], pmx[:, n % 2], -SCALE, None, ALU.mult).then_inc(v_um, 1)

            unit_mask(0)
            dve.wait_ge(v_pcy, 4)
            for n, (t, br, kv) in enumerate(UNITS):
                if n + 1 < len(UNITS):
                    unit_mask(n + 1)
                dve.wait_ge(a_ue, 4 * n + 4)
                own(nc.vector.reciprocal(pfac[:, n % 2], psm[:, n % 2]))
                own(nc.vector.tensor_tensor(pfac[:, n % 2], pfac[:, n % 2],
                                            GATE[:, t].rearrange("p (h n) -> p n h", n=3)[:, br, 4 * kv:4 * kv + 4], ALU.mult))
                dve.wait_ge(t_uv, n + 1)
                own(nc.vector.tensor_tensor(OTMP[:, 0:256].rearrange("p (g d) -> p g d", g=GRP),
                                            ps[:, 6 + n % 2, 0:256].rearrange("p (g d) -> p g d", g=GRP),
                                            bc(pfac[:, n % 2].unsqueeze(2), [P, GRP, HD]), ALU.mult))
                y = Y[:, t, YB + kv * 256:YB + kv * 256 + 256]
                nc.vector.tensor_tensor(y, y, OTMP[:, 0:256], ALU.add).then_inc(v_uy, 1)
                dve.wait_ge(v_uy, n + 1)
            own(nc.vector.memset(ZERO2, 0.0))
            parts = ((slice(0, P), slice(0, 2)), (slice(0, 64), slice(2, 3)))
            nc.vector.memset(WAITED, 0.0).then_inc(v_u, 1)
            for r, t in parts:
                nc.vector.tensor_tensor(Z[r, t, CC:CC + 512], Z[r, t, CC:CC + 512], Z[r, t, CH:CH + 512], ALU.mult).then_inc(v_u, 1)
            own(nc.vector.memset(EX, 0.0))
            own(nc.vector.memset(MT1, 0.0))
            for r, t in parts:
                n, m = t.stop - t.start, r.stop
                own(nc.vector.tensor_tensor(ILOG[r, t], Z[r, t, ZMI:ZMI + 4], bc(GB[r, 0:4].unsqueeze(1), [m, n, 4]), ALU.add))
                own(nc.vector.tensor_tensor(FLOG[r, t], Z[r, t, ZMF:ZMF + 4], bc(GB[r, 4:8].unsqueeze(1), [m, n, 4]), ALU.add))
                nc.vector.scalar_tensor_tensor(out=MT2[r, t], in0=FLOG[r, t], scalar=-1.0, in1=FLOG[r, t], op0=ALU.mult, op1=ALU.max).then_inc(v_mf, 1)
            dve.wait_ge(a_mf, 2)
            for r, t in parts:
                nc.vector.tensor_scalar(MT2[r, t], MT2[r, t], 1.0, None, ALU.add).then_inc(v_mf, 1)
            dve.wait_ge(a_mf, 4)
            for r, t in parts:
                nc.vector.scalar_tensor_tensor(out=FLOG[r, t], in0=FLOG[r, t], scalar=0.0, in1=MT2[r, t], op0=ALU.min, op1=ALU.subtract).then_inc(v_flog, 1)
            dve.wait_ge(t_mn, 1)
            nc.vector.tensor_copy(NT, ps[:, 0, 0:32]).then_inc(v_mn, 1)
            nc.vector.tensor_copy(M0[0:64], ps[0:64, 1, 0:4]).then_inc(v_mn, 1)
            dve.wait_ge(t_bc, 1)
            own(nc.vector.tensor_copy(BCUM[:, 0:2], ps[:, 2, 0:8].rearrange("p (t h) -> p t h", h=MH)))
            own(nc.vector.tensor_copy(BCUM[0:64, 2], ps[0:64, 2, 8:12]))
            for r, t in parts:
                own(nc.vector.tensor_tensor(GLOG[r, t], ILOG[r, t], BCUM[r, t], ALU.subtract))
            for h in range(MH):
                if h:
                    dve.wait_ge(t_gr, h)
                for t in range(TILES):
                    r = ROWS[t]
                    nc.vector.tensor_scalar(DG[0:r, TOFF[t]:TOFF[t] + r], k_("ident")[0:r, 0:r], GLOG[0:r, t, h:h + 1], None, ALU.mult).then_inc(v_dg, 1)
                dve.wait_ge(t_gr, h + 1)
                own(nc.vector.tensor_tensor(MD[:, 0:128], ps[:, 0, 0:128], k_("causal"), ALU.add))
                own(nc.vector.tensor_copy(MD[:, 128:256], ps[:, 0, 0:128]))
                own(nc.vector.tensor_tensor(MD[:, 256:384], ps[:, 0, 128:256], k_("causal"), ALU.add))
                own(nc.vector.tensor_tensor(MD[0:64, 384:448], ps[0:64, 0, 256:320], k_("blockcausal")[0:64], ALU.add))
                own(nc.vector.reduce_max(MMAX[:, 0, h:h + 1], MD[:, 0:128], AX))
                own(nc.vector.reduce_max(MMAX[:, 1, h:h + 1], MD[:, 128:384], AX))
                own(nc.vector.reduce_max(MMAX[0:64, 2, h:h + 1], MD[0:64, 384:448], AX))
                own(nc.vector.tensor_scalar(MMAX[:, 0:2, h], MMAX[:, 0:2, h], 0.0, None, ALU.max))
                own(nc.vector.tensor_tensor(MMAX[0:64, 2, h:h + 1], MMAX[0:64, 2, h:h + 1], M0[0:64, h:h + 1], ALU.max))
                own(nc.vector.tensor_scalar(MT1[:, 0:2, h], MMAX[:, 0:2, h], -1.0, None, ALU.mult))
                own(nc.vector.tensor_scalar(MT1[0:64, 2, h:h + 1], MMAX[0:64, 2, h:h + 1], -1.0, None, ALU.mult))
                own(nc.vector.tensor_tensor(EX[:, 0:2], MT1[:, 0:2, h], BCUM[:, 0:2, h], ALU.subtract))
                own(nc.vector.tensor_tensor(EX[0:64, 2:3], MT1[0:64, 2, h:h + 1], BCUM[0:64, 2, h:h + 1], ALU.subtract))
                nc.vector.tensor_tensor(EX[0:64, 3:4], M0[0:64, h:h + 1], MMAX[0:64, 2, h:h + 1], ALU.subtract).then_inc(v_md, 1)
                dve.wait_ge(a_mw, 4 * h + 4)
                for r, a, b, t in ((P, 0, 128, 0), (P, 128, 384, 1), (64, 384, 448, 2)):
                    nc.vector.scalar_tensor_tensor(out=MW[0:r, a:b], in0=ps[0:r, 1, a:b], scalar=DH ** -0.5, in1=MW[0:r, a:b],
                                                   op0=ALU.mult, op1=ALU.mult, accum_out=DEN[0:r, t:t + 1]).then_inc(v_wqk, 1)
                dve.wait_ge(v_wqk, 3 * h + 3)
                dve.wait_ge(t_num, h + 1)
                bm = k_("batchmask")
                own(nc.vector.tensor_tensor(QCM[0:64], ps[0:64, 4:6, :].rearrange("p j (b e) -> p (j b) e", e=DH),
                                            bc(bm[0:64].unsqueeze(2), [64, DEC_B, DH]), ALU.mult))
                own(nc.vector.reduce_sum(HN[0:64, 2], QCM[0:64].rearrange("p b e -> p e b"), AX))
                own(nc.vector.scalar_tensor_tensor(out=HN[0:64, 2], in0=HN[0:64, 2], scalar=EX[0:64, 3:4], in1=ps[0:64, 3, 256:384],
                                                   op0=ALU.mult, op1=ALU.add))
                own(nc.vector.tensor_tensor(QN[0:64], ps[0:64, 3, 384:392], bm[0:64], ALU.mult))
                own(nc.vector.reduce_sum(DEN[0:64, 3:4], QN[0:64], AX))
                own(nc.vector.scalar_tensor_tensor(out=DEN[0:64, 2:3], in0=DEN[0:64, 3:4], scalar=EX[0:64, 3:4], in1=DEN[0:64, 2:3],
                                                   op0=ALU.mult, op1=ALU.add))
                for r, a, b in ((P, 0, 2), (64, 2, 3)):
                    own(nc.vector.scalar_tensor_tensor(out=DEN[0:r, a:b], in0=DEN[0:r, a:b], scalar=-1.0, in1=DEN[0:r, a:b], op0=ALU.mult, op1=ALU.max))
                    own(nc.vector.tensor_tensor(DEN[0:r, a:b], DEN[0:r, a:b], EX[0:r, a:b], ALU.max))
                    own(nc.vector.reciprocal(DEN[0:r, a:b], DEN[0:r, a:b]))
                yh = [Y[0:ROWS[t], t, 1536 + h * 128:1664 + h * 128] for t in range(TILES)]
                for t in range(2):
                    own(nc.vector.tensor_scalar(yh[t], ps[:, 3, t * 128:t * 128 + 128], DEN[:, t:t + 1], None, ALU.mult))
                own(nc.vector.tensor_scalar(yh[2], HN[0:64, 2], DEN[0:64, 2:3], None, ALU.mult))
                for t in range(TILES):
                    r = ROWS[t]
                    own(nc.vector.tensor_tensor_reduce(out=HN[0:r, t], in0=yh[t], in1=yh[t], scale=1.0, scalar=0.0, op0=ALU.mult, op1=ALU.add,
                                                       accum_out=SSQ[0:r, t, h:h + 1]))
                nc.vector.memset(WAITED, 0.0).then_inc(v_hn, 1)
            for r, t in parts:
                nc.vector.tensor_tensor(BM[r, t], BCUM[r, t], MMAX[r, t], ALU.add).then_inc(v_bm, 1)
            dve.wait_ge(t_ml, 1)
            for t in range(2):
                own(nc.vector.tensor_copy(MLAST[:, t], ps[:, 0, 0:4]))
            own(nc.vector.tensor_copy(MLAST[0:64, 2], ps[0:64, 0, 4:8]))
            own(nc.vector.tensor_copy(MNEW[:, 1], ps[:, 0, 8:12]))
            own(nc.vector.tensor_copy(MNEW[0:64, 2], ps[0:64, 0, 12:16]))
            for r, t in parts:
                nc.vector.tensor_tensor(WL[r, t], GLOG[r, t], MLAST[r, t], ALU.subtract).then_inc(v_wl, 1)
            nc.vector.tensor_tensor(MT1[0:64, 2], M0[0:64], MLAST[0:64, 2], ALU.subtract).then_inc(v_wl, 1)
            dve.wait_ge(a_wl, 3)
            for h in range(MH):
                nc.vector.tensor_scalar(DECD[0:64, h], k_("lastmask")[0:64], MT1[0:64, 2, h:h + 1], None, ALU.mult).then_inc(v_decd, 1)
            dve.wait_ge(t_decb, 1)
            own(nc.vector.tensor_copy(DECB.rearrange("p h b -> p (h b)"), ps[:, 1, 0:32]))
            for h in range(MH):
                if h:
                    dve.wait_ge(t_c, h)
                for t in range(TILES):
                    r = ROWS[t]
                    nc.vector.tensor_scalar(KW[0:r, t], Z[0:r, t, ZMK + h * 128:ZMK + h * 128 + 128], WL[0:r, t, h:h + 1], DH ** -0.5,
                                            ALU.mult, ALU.mult).then_inc(v_kw, 1)
                nc.vector.tensor_tensor(VB[0:64], bc(Z[0:64, 2, ZMV + h * 128:ZMV + h * 128 + 128].unsqueeze(1), [64, DEC_B, DH]),
                                        bc(k_("batchmask")[0:64].unsqueeze(2), [64, DEC_B, DH]), ALU.mult).then_inc(v_kw, 1)
                dve.wait_ge(ld_mc, 16 * (MH + h) + 16)
                own(nc.vector.tensor_tensor(MC, MC, bc(DECB[:, h].unsqueeze(2), [P, DEC_B, DH]), ALU.mult))
                nt = NT.rearrange("p (b h) -> p h b", h=MH)[:, h]
                no = NO[:, 0:32].rearrange("p (b h) -> p h b", h=MH)[:, h]
                own(nc.vector.tensor_tensor(no, nt, DECB[:, h], ALU.mult))
                dve.wait_ge(t_c, h + 1)
                own(nc.vector.tensor_tensor(no, no, ps[:, 2, 136:144], ALU.add))
                own(nc.vector.tensor_copy(NO[:, 32 + h:33 + h], ps[:, 2, 128:129]))
                if h:
                    dve.wait_ge(st_c, 32 * h)
                own(nc.vector.tensor_copy(HN[:, 0], ps[:, 2, 0:128]))
                nc.vector.tensor_tensor(MC, MC, ps[:, 3:5, :].rearrange("p j (b e) -> p (j b) e", e=DH), ALU.add).then_inc(v_c, 1)
            dve.wait_ge(t_no, 1)
            nc.vector.tensor_copy(N32[0:36], ps[0:36, 0, 0:128]).then_inc(v_no, 1)
            for r, t in parts:
                nc.vector.tensor_scalar(SSQ[r, t], SSQ[r, t], 1.0 / DH, EPS, ALU.mult, ALU.add).then_inc(v_ssq, 1)
            dve.wait_ge(a_sig, 2)
            dve.wait_ge(ld_g, 16)
            for r, t in parts:
                n, m = t.stop - t.start, r.stop
                o = Z[r, t, ZMO:ZMO + 512]
                own(nc.vector.tensor_scalar(o, o, 1.0, None, ALU.add))
                own(nc.vector.reciprocal(o, o))
                own(nc.vector.tensor_tensor(o, o, bc(MNG[r].unsqueeze(1), [m, n, 512]), ALU.mult))
                own(nc.vector.tensor_tensor(Y[r, t, 1536:2048], Y[r, t, 1536:2048], o, ALU.mult))
            dve.wait_ge(a_ssq, 2)
            for r, t in parts:
                own(nc.vector.reciprocal(SSQ[r, t], SSQ[r, t]))
            for t in range(TILES):
                r = ROWS[t]
                y = Y[0:r, t, 1536:2048].rearrange("p (h e) -> p h e", h=MH)
                own(nc.vector.tensor_tensor(y, y, bc(SSQ[0:r, t].unsqueeze(2), [r, MH, DH]), ALU.mult))
            dve.wait_ge(ld_u, 64)
            dve.wait_ge(ld_cw, 16)
            for r, t in parts:
                n, m = t.stop - t.start, r.stop
                w = [bc(CW[r, j].unsqueeze(1), [m, n, 512]) for j in range(3)]
                u = [Z[r, t, ZQ + 512:ZQ + 1024], Z[r, t, CH:CH + 512], Z[r, t, CC:CC + 512]]
                for j in range(3):
                    own(nc.vector.tensor_tensor(u[j], u[j], w[j], ALU.mult))
                own(nc.vector.tensor_tensor(u[0], u[0], u[1], ALU.add))
                own(nc.vector.tensor_tensor(u[0], u[0], u[2], ALU.add))
                own(nc.vector.tensor_tensor(Y[r, t, 0:512], Z[r, t, CB:CB + 512], u[0], ALU.mult))
            dve.sem_inc(v_y, 3)

            def store_transposed(dst, sem_done, sem_stored, g):
                for n in range(TILES * 4):
                    t, j = n // 4, n % 4
                    r = ROWS[t]
                    dve.wait_ge(sem_done, n + 1)
                    out = dst[:, 4 * j:4 * j + 4, TOFF[t]:TOFF[t] + r]
                    src = ps[:, n % 8].rearrange("p (q n) -> p q n", q=4)[:, :, 0:r]
                    if g is None:
                        nc.vector.tensor_copy(out, src).then_inc(sem_stored, 1)
                    else:
                        nc.vector.tensor_tensor(out, src, bc(g[:, 4 * j:4 * j + 4].unsqueeze(2), [P, 4, r]), ALU.mult).then_inc(sem_stored, 1)

            store_transposed(YT, t_y, v_yt, None)
            dve.wait_ge(ld_xr, 32)
            for c in range(4):
                dve.wait_ge(w_used, 24 + 2 * c + 2)
                for t in range(TILES):
                    x = X1[0:ROWS[t], t, c * WC:c * WC + WC]
                    nc.vector.tensor_tensor(x, x, ps[0:ROWS[t], 3 * (c % 2) + t, :], ALU.add).then_inc(v_x1, 1)
            for j in range(4):
                dve.wait_ge(t_sk, j + 1)
                nc.vector.tensor_copy(SKT[:, 4 * j:4 * j + 4], ps[:, j].rearrange("p (q n) -> p q n", q=4)).then_inc(v_sk, 1)
            dve.wait_ge(a_ss2, 3)
            nc.vector.tensor_scalar(ss[:, 0:3], ss[:, 0:3], 1.0 / D, EPS, ALU.mult, ALU.add).then_inc(v_ss2, 1)
            dve.wait_ge(a_ss2, 4)
            nc.vector.reciprocal(rstd[:, 0:3], rstd[:, 0:3]).then_inc(v_ss2, 1)
            store_transposed(HT, t_h, v_ht, G2T)
            dve.wait_ge(ld_g2, 32)
            for r, t in parts:
                n, m = t.stop - t.start, r.stop
                own(nc.vector.tensor_tensor(H[r, t], H[r, t], bc(G2B[r].unsqueeze(1), [m, n, D]), ALU.mult))
            tvp = lambda r, c: TV[r].rearrange("p (h c) k -> p c h k", c=2)[:, c]
            tip = lambda r, c: TIF[r].rearrange("p (h c) k -> p c h k", c=2)[:, c]
            for t in range(TILES):
                m = ROWS[t]
                r = slice(0, m)
                dve.wait_ge(a_sc, 4 * t + 4)

                def best(vals, idx, src, work, n):
                    for first in (True, False):
                        k = slice(0, 8) if first else slice(8, 16)
                        for i in range(n):
                            ins = nc.vector.max(vals[r, i, k], (src if first else work)[r, i])
                        own(ins)
                        for i in range(n):
                            ins = nc.vector.max_index(idx[r, i, k], vals[r, i, k], (src if first else work)[r, i])
                            if first:
                                ins = nc.vector.match_replace(work[r, i], vals[r, i, k], src[r, i], NEG)
                        own(ins)

                best(TV, TI, SC[:, t].rearrange("p (a b) -> p a b", a=16), SCW, 16)
                own(nc.vector.tensor_copy(TIF[r], TI[r]))
                own(nc.vector.tensor_tensor(CAND[r].rearrange("p h (i j) -> p h i j", i=TOPK), bc(tvp(r, 0).unsqueeze(3), [m, PH, TOPK, TOPK]),
                                            bc(tvp(r, 1).unsqueeze(2), [m, PH, TOPK, TOPK]), ALU.add))
                best(CVAL, CPOS, CAND, CANDW, PH)
                g = GG[r, t].rearrange("p (h k) -> p h k", h=PH)
                nc.vector.tensor_tensor(g, CVAL[r], bc(CVAL[r, :, 0:1], [m, PH, TOPK]), ALU.subtract).then_inc(v_cd, 1)
                own(nc.vector.tensor_scalar(CHI[r], CPOS[r], 4, None, ALU.logical_shift_right))
                own(nc.vector.tensor_scalar(CLO[r], CPOS[r], 15, None, ALU.bitwise_and))
                own(nc.vector.tensor_copy(FHI[r], CHI[r]))
                own(nc.vector.tensor_copy(FLO[r], CLO[r]))
                for c, rank, num in ((0, FHI, E1), (1, FLO, E2)):
                    oh = OH[r].rearrange("p (h k i) -> p h k i", h=PH, k=TOPK)
                    own(nc.vector.tensor_tensor(OH[r].rearrange("p (x i) -> p x i", i=TOPK), bc(k_("iota16")[r].unsqueeze(1), [m, 128, TOPK]),
                                                bc(rank[r].rearrange("p h k -> p (h k)").unsqueeze(2), [m, 128, TOPK]), ALU.is_equal))
                    own(nc.vector.tensor_tensor(oh, oh, bc(tip(r, c).unsqueeze(2), [m, PH, TOPK, TOPK]), ALU.mult))
                    own(nc.vector.reduce_sum(num[r].rearrange("p h k -> p (h k)"), OH[r].rearrange("p (x i) -> p x i", i=TOPK), AX))
                own(nc.vector.scalar_tensor_tensor(out=EIDX[r, t], in0=E1[r].rearrange("p h k -> p (h k)"), scalar=float(NKEY),
                                                   in1=E2[r].rearrange("p h k -> p (h k)"), op0=ALU.mult, op1=ALU.add))
                dve.wait_ge(a_cd, t + 1)
                own(nc.vector.reduce_sum(GSUM[r], g, AX))
                own(nc.vector.reciprocal(GSUM[r], GSUM[r]))
                own(nc.vector.tensor_tensor(g, g, bc(GSUM[r].unsqueeze(2), [m, PH, TOPK]), ALU.mult))
            dve.sem_inc(v_route, 1)
            own(nc.vector.memset(GE1, 0.0))
            dve.sem_inc(g_used, 8)
            for t in range(TILES):
                m = ROWS[t]
                r = slice(0, m)
                own(nc.vector.memset(ACC, 0.0))
                with dve.Fori(t * PH, t * PH + PH) as i:
                    for n in range(16):
                        dve.wait_ge(g_in[n % 8], i * 64 + 16 * (n // 8) + 16)
                        nc.vector.tensor_tensor_reduce(out=PROD[r], in0=BUF[r, n % 8], in1=H[r, t], scale=1.0, scalar=0.0, op0=ALU.mult,
                                                       op1=ALU.add, accum_out=DOTS[r, n:n + 1]).then_inc(g_used, 1)
                        dve.wait_ge(g_used, i * 32 + n + 9)
                    cnt.enter(i - t * PH, {v_own: 6})
                    own(nc.vector.tensor_tensor(GE1[r], DOTS[r], DOTS[r], ALU.mult))
                    own(nc.vector.tensor_scalar(GE1[r], GE1[r], GELU_K, 1.0, ALU.mult, ALU.add))
                    nc.vector.tensor_tensor(GE1[r], GE1[r], DOTS[r], ALU.mult).then_inc(v_ge, 1)
                    dve.wait_ge(a_ge, i + 1)
                    own(nc.vector.tensor_scalar(GE2[r], GE1[r], 1.0, None, ALU.add))
                    own(nc.vector.reciprocal(GE2[r], GE2[r]))
                    own(nc.vector.tensor_tensor(GE2[r], GE2[r], DOTS[r], ALU.mult))
                    own(nc.vector.tensor_tensor(WV[r], GE2[r], GG[r, t, bass.ds((i - t * PH) * TOPK, TOPK)], ALU.mult))
                    cnt.leave(PH)
                    for n in range(16, 32):
                        dve.wait_ge(g_in[n % 8], i * 64 + 16 * (n // 8) + 16)
                        nc.vector.scalar_tensor_tensor(out=ACC[r], in0=BUF[r, n % 8], scalar=WV[r, n - 16:n - 15], in1=ACC[r],
                                                       op0=ALU.mult, op1=ALU.add).then_inc(g_used, 1)
                        dve.wait_ge(g_used, i * 32 + n + 9)
                nc.vector.tensor_tensor(X1[r, t], X1[r, t], ACC[r], ALU.add).then_inc(v_x2, 1)
                dve.wait_ge(v_x2, t + 1)
            dve.wait_ge(a_ss3, 3)
            nc.vector.tensor_scalar(ss[:, 0:3], ss[:, 0:3], 1.0 / D, EPS, ALU.mult, ALU.add).then_inc(v_ss3, 1)
            dve.wait_ge(a_ss3, 4)
            own(nc.vector.reciprocal(rstd[:, 0:3], rstd[:, 0:3]))
            for t in range(TILES):
                r = ROWS[t]
                nc.vector.scalar_tensor_tensor(out=X1[0:r, t], in0=X1[0:r, t], scalar=rstd[0:r, t:t + 1], in1=GFB[0:r],
                                               op0=ALU.mult, op1=ALU.mult).then_inc(v_out, 1)


        @block.gpsimd
        def _(pool):
            u_rows, v_rows = peer_u[0], peer_v[0]
            pool.wait_ge(v_route, 1)


            def wait_apart(sem, value, cell):
                pool.wait_ge(sem, value)
                one = k_("ones")[:, 0:1]
                nc.gpsimd.tensor_tensor(WCELL[:, cell:cell + 1], one, one, ALU.add)

            for t in range(TILES):
                m = ROWS[t]
                with pool.Fori(t * (PH // 2), (t + 1) * (PH // 2)) as i:
                    for x in range(2):
                        pool.wait_ge(g_used, i * 64 + 32 * x + 1)
                        nc.gpsimd.tensor_copy(CUR[0:m, x], EIDX[0:m, t, bass.ds((i * 2 + x - t * PH) * TOPK, TOPK)]).then_inc(p_cur, 1)
                        wait_apart(p_cur, i * 2 + x + 1, 9 * x)
                        for n in range(32):
                            if n % 4 == 0:
                                wait_apart(g_used, i * 64 + 32 * x + n + 4, 9 * x + 1 + n // 4)
                            nc.gpsimd.indirect_dma_start(BUF[0:m, n % 8], None, u_rows if n < 16 else v_rows,
                                                         bass.IndirectOffsetOnAxis(CUR[0:m, x, n % 16:n % 16 + 1].bitcast(U32), 0)).then_inc(g_in[n % 8], 16)



_INS = ["x_prompt", "x_sample", "cache_nsa_kv", "state_win_kv", "state_conv", "state_mlstm_C", "state_mlstm_n",
        "state_mlstm_m", "page_table", "norm1_g", "w_in", "conv_w", "mlstm_gate_b", "mlstm_norm_g", "w_out", "norm2_g",
        "peer_wq", "peer_subkeys", "peer_u", "peer_v", "final_norm_g"]
_OUTS = [("y_prompt", (1, 256, 2048)), ("y_sample", (8, 8, 2048)), ("p_rows", (1, 1, 256, 4, 4, 64)),
         ("p_win", (1, 1, 256, 2, 4, 64)), ("p_conv", (1, 1, 2, 512)), ("p_C", (1, 1, 4, 128, 128)), ("p_n", (1, 1, 4, 128)),
         ("p_m", (1, 1, 4)), ("s_rows", (1, 8, 8, 4, 4, 64)), ("s_win", (1, 8, 512, 2, 4, 64)), ("s_conv", (1, 8, 2, 512)),
         ("s_C", (1, 8, 4, 128, 128)), ("s_n", (1, 8, 4, 128)), ("s_m", (1, 8, 4))]


def kernel(**inputs):
    import concourse.bacc as _bacc
    from concourse.bass_utils import run_bass_kernel_spmd as _run

    nc = _bacc.Bacc("TRN2", target_bir_lowering=False, num_devices=1)
    at, const = constants()
    arrays = {"in_const_dram": const}
    args = [nc.dram_tensor("in_const_dram", const.shape, F32, kind="ExternalInput").ap()]
    for name in _INS:
        a = np.ascontiguousarray(inputs[name])
        arrays["in_%s_dram" % name] = a
        args.append(nc.dram_tensor("in_%s_dram" % name, a.shape, mybir.dt.from_np(a.dtype), kind="ExternalInput").ap())
    for name, shape in _OUTS:
        args.append(nc.dram_tensor("out_%s_dram" % name, shape, F32, kind="ExternalOutput").ap())
    for name, shape in (("new_kv", (64, 1536)), ("conv_ext", (340, 512)), ("branch_out", (3, 8, 8, 16, 64))):
        args.append(nc.dram_tensor(name, shape, F32, kind="Internal").ap())
    hybrid_step(nc, at, const.shape[1], *args)
    r = _run(nc, [arrays], core_ids=[0])
    return tuple(r.results[0]["out_%s_dram" % name] for name, _ in _OUTS)
```

```python
from contextlib import ExitStack

import numpy as np

import concourse.bass as bass
from concourse import mybir

F32 = mybir.dt.float32
I32 = mybir.dt.int32
BF16 = mybir.dt.bfloat16
U32 = mybir.dt.uint32
ALU = mybir.AluOpType
ACT = mybir.ActivationFunctionType
AX = mybir.AxisListType.X

P = 128
D = 2048
SEQ, DEC_B, DEC_S = 256, 8, 8
PAST, PAGE = 2048, 128
NPAGE = PAST // PAGE
CONV_W, NSA_W, ML_W = 512, 1024, 512
HD, KVH, GRP = 64, 4, 4
HEADS = KVH * GRP
WIN = 512
MH, DH = 4, 128
PH, NKEY, TOPK = 8, 128, 16
EPS = 1e-6
NEG = -1e30
BIG = 1e9
GELU_C = 2.0 * (2.0 / np.pi) ** 0.5
GELU_K = 0.044715

CB, CC, CH = 0, 512, 1024
ZQ = 1536
ZKV = 2560
ZG = 4096
ZMQ, ZMK, ZMV, ZMO = 4144, 4656, 5168, 5680
ZMI, ZMF = 6192, 6196
ZC = 6200

TILES = 3
ROWS = [128, 128, 64]
KT = D // P
TOK = SEQ + DEC_B * DEC_S

WC = 512
NFULL = ZC // WC
TAIL = ZC - NFULL * WC
NSLOT = 4
KS = KT // NSLOT
W_LOADS = 4 * (NFULL + 8)
NBUF = 4


def constants():
    r = np.arange(P)
    parts = {}
    parts["ident"] = np.eye(P)
    parts["ones"] = np.ones((P, P))
    parts["tri"] = (r[:, None] <= r[None, :]) * 1.0
    s = np.arange(64)
    same = (s[:, None] // 8 == s[None, :] // 8)
    parts["blocktri"] = np.concatenate([(same & (s[:, None] <= s[None, :])) * 1.0, np.zeros((64, 64))])
    parts["causal"] = np.where(r[None, :] <= r[:, None], 0.0, NEG)
    parts["blockcausal"] = np.concatenate([np.where(same & (s[None, :] <= s[:, None]), 0.0, NEG), np.zeros((64, 64))])
    parts["batchmask"] = np.concatenate([(s[:, None] // 8 == np.arange(8)[None, :]) * 1.0, np.zeros((64, 8))])
    parts["lastmask"] = np.concatenate([(s[:, None] == 8 * np.arange(8)[None, :] + 7) * 1.0, np.zeros((64, 8))])
    parts["lastrow"] = (r[:, None] == 127) * np.ones((P, P))
    parts["blocklast"] = np.concatenate([(s[:, None] == 8 * (s[None, :] // 8) + 7) * 1.0, np.zeros((64, 64))])
    e8 = np.zeros((P, 64))
    e8[:8] = (np.arange(8)[:, None] == s[None, :] // 8)
    parts["spread"] = e8
    y = np.arange(248) - 120
    parts["compress"] = ((16 * y[None, :] <= r[:, None]) & (r[:, None] < 16 * y[None, :] + 32)) / 32.0
    c = np.arange(16)
    for t in range(2):
        q = t * 128 + r
        parts["cmpneg%d" % t] = np.where(16 * c[None, :] + 31 <= q[:, None], 0.0, NEG)
        parts["cmpone%d" % t] = (16 * c[None, :] + 31 <= q[:, None]) * 1.0
    kv, q = r // 32, r % 8
    parts["groupsum"] = ((kv[:, None] == kv[None, :]) & (q[:, None] == q[None, :])) * 1.0
    j = np.arange(8)
    parts["newneg"] = np.where(j[None, :] <= q[:, None], 0.0, NEG)
    parts["oldneg"] = np.where(j[None, :] > q[:, None], 0.0, NEG)
    parts["headmask"] = (r[:, None] // 16 == np.arange(8)[None, :]) * 1.0
    parts["iota16"] = np.ones((P, 1)) * c[None, :]
    at, cols, n = {}, [], 0
    for k, v in parts.items():
        at[k] = (n, n + v.shape[1])
        n += v.shape[1]
        cols.append(v)
    return at, np.ascontiguousarray(np.concatenate(cols, axis=1).astype(np.float32))


class Counts:

    def __init__(self, eng):
        self.eng, self.n, self.i, self.per, self.base = eng, {}, None, {}, {}

    def value(self, sem):
        if self.i is not None and sem in self.per:
            return self.i * self.per[sem] + (self.base.get(sem, 0) + self.n.get(sem, 0))
        return self.n.get(sem, 0)

    def sig(self, ins, sem, amount=1):
        assert self.i is None or sem in self.per, "a semaphore without a count for this loop"
        self.n[sem] = self.n.get(sem, 0) + amount
        ins.then_inc(sem, amount)

    def own(self, ins, sem):
        self.sig(ins, sem)
        self.eng.wait_ge(sem, self.value(sem))

    def enter(self, i, per):
        self.i, self.per = i, per
        self.base = {s: self.n.get(s, 0) for s in per}
        for s in per:
            self.n[s] = 0

    def leave(self, count):
        for s, k in self.per.items():
            assert self.n[s] == k, ("per iteration", self.n[s], "stated", k)
            self.n[s] = self.base[s] + count * k
        self.i, self.per = None, {}


def bc(ap, shape):
    return ap.to_broadcast(shape)


def hybrid_step(nc, at, ncol, const, x_prompt, x_sample, cache_nsa_kv, state_win_kv, state_conv, state_mlstm_C,
                state_mlstm_n, state_mlstm_m, page_table, norm1_g, w_in, conv_w, mlstm_gate_b, mlstm_norm_g,
                w_out, norm2_g, peer_wq, peer_subkeys, peer_u, peer_v, final_norm_g,
                y_prompt, y_sample, p_rows, p_win, p_conv, p_C, p_n, p_m,
                s_rows, s_win, s_conv, s_C, s_n, s_m,
                new_kv, conv_ext, branch_out, x2_rows):
    with ExitStack() as ctx:
        def sem(name):
            return ctx.enter_context(nc.semaphore(name))

        CONST = 0
        SMALL = CONST + ncol
        R_BUF = SMALL + 1500
        R_H = R_BUF + NBUF * D
        R_ACC = R_H + 2 * D
        R_PROD = R_ACC + D
        R_X = R_PROD + D // 2
        R_XT = R_X + D
        R_Y = R_XT + D
        R_SKT = R_Y + D
        R_RING = R_SKT + D
        R_Z = R_RING + NSLOT * KS * WC
        R_TEMP = R_Z + 2 * ZC
        ARENA = 53200
        arena = ctx.enter_context(nc.sbuf_tensor("arena", [P, ARENA], F32))

        def mem(start, cols):
            assert start + cols <= ARENA
            return arena[:, start:start + cols]

        def mem3(start, a, b):
            return mem(start, a * b).rearrange("p (a b) -> p a b", a=a)

        KONST = mem(CONST, ncol)
        X, XT, Y = mem(R_X, D), mem3(R_XT, KT, P), mem(R_Y, D)
        QP = mem3(R_Y, 16, P)
        RING = mem(R_RING, NSLOT * KS * WC).rearrange("p (s k n) -> p s k n", s=NSLOT, k=KS)
        TAILW = mem3(R_RING, KT, TAIL)
        Z = [mem(R_Z, ZC), mem(R_Z + ZC, ZC), mem(R_Z, ZC)]
        G2B = [z[:, 0:D] for z in Z]
        SKT = mem3(R_SKT, 16, P)
        SK = mem3(R_Z + ZC, 16, P)
        BUF = mem3(R_BUF, NBUF, D)
        H = [mem(R_H, D), mem(R_H + D, D), mem(R_H, D)]
        ACC = mem(R_ACC, D)
        PROD = mem(R_PROD, D // 2).bitcast(BF16)
        PP = mem(R_RING, 2048).rearrange("p (u g n) -> p u g n", u=2, g=4)
        PPT = mem3(R_RING + 2048, 2, 512)
        PCM, PCT = mem(R_RING + 3072, 256), mem(R_RING + 3328, 256)
        VBD = mem3(R_RING + 3584, 2, 512)
        KC = mem3(R_RING + 4608, 2, 16)
        OTMP = mem(R_RING + 4640, 256)
        CREP = mem3(R_RING + 4896, 2, 128)
        CW = [mem3(R_RING + 5152, 3, 512)] * 2 + [mem3(R_Z + ZC + 3072, 3, 512)]
        QT, KTS, KTW = mem3(R_TEMP, 8, P), mem3(R_TEMP + 1024, 2, SEQ), mem3(R_TEMP + 1536, 2, SEQ)
        MQT = mem3(R_TEMP + 2048, MH, P)
        MKT = mem3(R_TEMP + 2560, MH, SEQ)
        MD, MW, MWT, DG = (mem(R_TEMP + 3584 + 256 * n, 256) for n in range(4))
        KW = mem3(R_TEMP + 4608, 2, DH)
        HN = mem(R_TEMP + 4864, DH)
        CP = mem(R_TEMP + 4992, DH)
        N32 = mem(R_TEMP + 5120, DH)
        ZERO2 = mem(R_TEMP + 5248, 512)
        PAGES = [mem(R_Z + ZC + 1024 * g, 1024) for g in range(6)] + [mem(R_RING + 1024 * g, 1024) for g in range(8)] \
            + [mem(R_XT + 1024 * g, 1024) for g in range(2)]
        WINP = [Z[2][:, ZQ + 512 * w:ZQ + 512 * w + 512] for w in range(2)] + [mem(R_X + 512 * w, 512) for w in range(2)]
        QTS = mem3(R_X + 1024, 8, 64)
        KTN = mem(R_X + 1536, 256).rearrange("p (b i n) -> p b i n", b=2, i=2)
        OROW = mem3(R_X + 1792, 3, 64)
        SS, SW, PC = mem(R_TEMP, 2056), mem(R_TEMP + 2056, 520), mem(R_TEMP + 2576, 128)
        KTG, PTB = mem3(R_TEMP + 2704, 2, 512), mem3(R_TEMP + 3728, 2, 512)
        CK, CV = mem3(R_TEMP + 4752, 2, 128), mem(R_TEMP + 5008, 256)
        QB, VN = mem3(R_TEMP + 5264, 2, 128), mem3(R_TEMP + 5520, 2, 256)
        assert R_TEMP + 6032 <= ARENA
        OS = mem3(R_TEMP, 3, 1024)
        MC, VB, QCM = (mem3(R_Z + ZC + 1024 * n, DEC_B, DH) for n in range(3))
        SC, SCW = mem3(R_RING, 16, P), mem3(R_RING + D, 16, P)
        CAND, CANDW = mem3(R_RING + 2 * D, PH, 256), mem3(R_RING + 3 * D, PH, 256)
        OH = mem(R_XT, D)
        TV, TIF = mem3(R_Y, 16, TOPK), mem3(R_Y + 256, 16, TOPK)
        TI = mem3(R_Y + 512, 16, TOPK).bitcast(U32)
        CVAL, FHI, FLO, E1, E2 = (mem3(R_Y + 768 + 128 * n, PH, TOPK) for n in range(5))
        CPOS, CHI, CLO = (mem3(R_Y + 1408 + 128 * n, PH, TOPK).bitcast(U32) for n in range(3))
        GSUM = mem(R_Y + 1792, PH)
        X2, GFB = mem3(R_Z, TILES, D), mem(R_RING, D)
        JUNK = [mem(R_Y, D), mem(R_RING + D, D)]

        def k_(name):
            a, b = at[name]
            return KONST[:, a:b]

        small_at = [SMALL]

        def small(cols):
            a = small_at[0]
            small_at[0] += cols
            assert small_at[0] <= R_BUF, small_at[0] - SMALL
            return arena[:, a:a + cols]

        def small3(a, b):
            return small(a * b).rearrange("p (a b) -> p a b", a=a)

        G1T, G2T, GB = small(KT), small(KT), small(8)
        ss, rstd = small(4), small(4)
        WAITED = small(1)
        GATE = small(48)
        PT_ROW = small(128).bitcast(I32)
        smx, ssum, srec = small(4), small(4), small(4)
        blk, blkw, blkb, top8 = small(33), small(33), small(33), small(8)
        pmx, psm, pfac = small3(2, 4), small3(2, 4), small3(2, 4)
        cmx, csm = small(16), small(16)
        ILOG, FLOG, BCUM, GLOG, MMAX, MT1, MT2, MLAST, MNEW, WL, SSQ, BM = (small3(TILES, MH) for _ in range(12))
        M0, M0B, DEN, EX, QN = small(MH), small(MH), small(2), small(2), small(8)
        DECD, DECB = small3(MH, DEC_B), small3(MH, DEC_B)
        NT, NO = small(32), small(36)
        EIDX, GG = small3(2, 128).bitcast(I32), small3(2, 128)
        CUR = small3(2, TOPK).bitcast(I32)
        DOTS, GE1, GE2, WV = small(TOPK), small(TOPK), small(TOPK), small(TOPK)
        WCELL = small(34)

        ps = ctx.enter_context(nc.psum_tensor("ps", [P, 8, 512], F32))

        ld_const, ld_x, ld_small, ld_pt = sem("ld_const"), sem("x_in"), sem("ld_small"), sem("ld_page_table")
        v_own, a_own, a_xn, v_set = sem("vector_step_done"), sem("x_ss"), sem("x_scaled"), sem("places_set")
        v_rstd1, t_x, v_xt = sem("rstd1_ready"), sem("x_transposed"), sem("xt_stored")
        w_slot = [sem("w_slot%d_in" % s) for s in range(NSLOT)]
        w_used, w_tail = sem("w_slot_used"), sem("w_tail_in")
        z_done, a_z = sem("z_product_done"), sem("z_stored")
        st_kv, st_out = sem("new_kv_stored"), sem("outputs_stored")
        t_qk, v_qk = sem("qk_transposed"), sem("qkt_stored")
        pages_in, sel_in, win_in, vnew_in = sem("pages_to_compress_in"), sem("pages_to_select_in"), sem("window_in"), sem("new_values_in")
        v_qb, t_cmp, a_cmp, t_kt, a_kt = sem("qb_ready"), sem("cmp_kv_done"), sem("cmp_kv_stored"), sem("keys_transposed"), sem("keys_stored")
        t_wins, t_small, t_sel = sem("win_scores_done"), sem("cmp_new_scores_done"), sem("sel_scores_done")
        v_winm, v_cmpm, v_selm = sem("win_masked"), sem("cmp_max_ready"), sem("sel_masked")
        a_p, v_pc, t_imp = sem("sample_exp_done"), sem("cmp_probs_ready"), sem("importance_done")
        t_pt, a_pt, t_pv, v_or = sem("probs_transposed"), sem("probs_t_stored"), sem("values_done"), sem("branch_rows_ready")
        st_or, ld_os, a_gate = sem("branch_rows_stored"), sem("branch_rows_in"), sem("gate_exp_done")
        v_crep, t_pc, v_pck, t_pcs, v_pcm, a_pce = (sem("compress_repeated"), sem("pcmp_kv_done"), sem("pcmp_kv_stored"),
                                                    sem("pcmp_scores_done"), sem("pcmp_masked"), sem("pcmp_exp_done"))
        v_pcp, t_pct, v_pct, t_pcv, v_pcy = sem("pcmp_probs_ready"), sem("pcmp_transposed"), sem("pcmp_t_stored"), sem("pcmp_values_done"), sem("pcmp_y_ready")
        t_us, v_um, a_ue, t_ut, a_ut, t_uv, v_uy = (sem("unit_scores_done"), sem("unit_masked"), sem("unit_exp_done"),
                                                    sem("unit_transposed"), sem("unit_t_stored"), sem("unit_values_done"), sem("unit_y_ready"))
        v_u, st_u, ld_u, ld_cw, v_y = sem("conv_u_ready"), sem("conv_u_stored"), sem("shifted_u_in"), sem("conv_w_in"), sem("y_ready")
        ld_m, t_mt, a_mt, t_mn, v_mn = sem("mlstm_state_in"), sem("mlstm_qk_transposed"), sem("mlstm_qkt_stored"), sem("n_m_spread"), sem("n_m_stored")
        v_mf, a_mf, v_flog, t_bc = sem("gate_columns"), sem("gate_exp_ln_done"), sem("log_forget_ready"), sem("cumsum_done")
        v_dg, t_gr, v_md, a_mw, v_wqk = sem("gate_diag_ready"), sem("weights_scores_done"), sem("log_weights_masked"), sem("mlstm_exp_done"), sem("weighted_scores_ready")
        t_mwt, a_mwt, ld_mc, t_num, v_hn = sem("mlstm_w_transposed"), sem("mlstm_wt_stored"), sem("memory_in"), sem("numerator_done"), sem("head_out_ready")
        v_bm, t_ml, v_wl, a_wl, v_decd, t_decb, v_kw, t_c, v_c, st_c = (
            sem("last_columns_ready"), sem("last_rows_spread"), sem("state_weight_logs"), sem("state_weights_exp"), sem("decay_diag_ready"),
            sem("decay_spread"), sem("weighted_keys_ready"), sem("memory_update_done"), sem("memory_ready"), sem("memory_stored"))
        t_no, v_no, a_sig, v_ssq, a_ssq, ld_g = sem("n_transposed"), sem("n_ready"), sem("out_gate_exp"), sem("head_ss_ready"), sem("head_rms_ready"), sem("mlstm_g_in")
        t_y, a_yt, v_x1, ld_xr, a_ss2, v_ss2, a_h, t_h, a_ht = (
            sem("y_transposed"), sem("yt_stored"), sem("x1_ready"), sem("x_again_in"), sem("x1_ss"), sem("x1_rstd"), sem("h_scaled"),
            sem("h_transposed"), sem("ht_stored"))
        ld_g2, ld_gf, ld_sk, t_sk, v_sk, t_qp, a_qp, t_sc, a_sc = (
            sem("norm2_g_in"), sem("final_g_in"), sem("subkeys_in"), sem("subkeys_transposed"), sem("subkeys_t_stored"), sem("peer_q_done"),
            sem("peer_q_stored"), sem("key_scores_done"), sem("key_scores_stored"))
        v_cd, a_cd, v_route, v_acc0 = sem("candidates_shifted"), sem("gates_exp"), sem("routes_ready"), sem("peer_sum_starts")
        g_in = [sem("rows_in%d" % n) for n in range(NBUF)]
        g_used, p_cur = sem("rows_used"), sem("numbers_copied")
        v_ge, a_ge = sem("gelu_in_ready"), sem("gelu_exp_done")
        v_x2, st_x2, ld_x2, a_ss3, v_ss3, v_out = sem("x2_ready"), sem("x2_stored"), sem("x2_in"), sem("x2_ss"), sem("x2_rstd"), sem("y_out_ready")
        block = ctx.enter_context(nc.Block())

        SCALE = HD ** -0.5
        YB = CONV_W
        YM = CONV_W + NSA_W
        UNITS = [(br, kv) for br in (1, 2) for kv in range(KVH)]
        NU = len(UNITS)
        UT0 = [0, NU]
        rows = lambda t: slice(0, ROWS[t])
        TURNS = [PH, PH, PH // 2]
        GELU_CHUNKS = [[], [2, 6, 10], [3, 8]]

        def w_part(w, c, part):
            return w[0].rearrange("(k p) n -> p k n", p=P)[:, KS * part:KS * part + KS, bass.ts(c, WC)]

        def sample_nsa(pe):
            ident, comp = k_("ident"), k_("compress")
            pe.sem_inc(t_pv, 7)
            with pe.Fori(0, DEC_B) as b:
                pe.wait_ge(v_or, b + 1)
                pe.wait_ge(pages_in, b * 256 + 256)

                def selected_keys(g):
                    if g == 0:
                        pe.wait_ge(sel_in, b * 256 + 256)
                    for hp in range(2):
                        for q in range(4):
                            last = nc.tensor.transpose(ps[:, (2, 4)[g % 2] + hp, q * 128:q * 128 + 128],
                                                       PAGES[4 * g + q][:, 512 + hp * 128:640 + hp * 128], ident)
                    last.then_inc(t_kt, 1)

                for hp in range(2):
                    for g in range(NPAGE):
                        nc.tensor.matmul(ps[:, 6, hp * 128:hp * 128 + 128], PAGES[g][:, hp * 128:hp * 128 + 128],
                                         comp[:, 120 - 8 * g:248 - 8 * g], start=(g == 0), stop=(g == NPAGE - 1))
                for g in range(NPAGE):
                    last = nc.tensor.matmul(ps[:, 6, 256:512], comp[:, 120 - 8 * g:248 - 8 * g], PAGES[g][:, 256:512],
                                            start=(g == 0), stop=(g == NPAGE - 1))
                last.then_inc(t_cmp, 1)
                pe.wait_ge(win_in, b * 64 + 64)
                for hp in range(2):
                    for w in range(4):
                        last = nc.tensor.transpose(ps[:, 4 + hp, w * 128:w * 128 + 128], WINP[w][:, hp * 128:hp * 128 + 128], ident)
                last.then_inc(t_kt, 1)
                selected_keys(0)
                pe.wait_ge(v_qb, b * 4 + 4)
                pe.wait_ge(a_cmp, b * 2 + 2)
                pe.wait_ge(a_kt, b * 5 + 1)
                for hp in range(2):
                    last = nc.tensor.matmul(ps[:, 6, :], QB[:, hp], KTG[:, hp], start=(hp == 0), stop=(hp == 1))
                last.then_inc(t_wins, 1)
                for hp in range(2):
                    nc.tensor.matmul(ps[:, 7, 0:128], QB[:, hp], CK[:, hp], start=(hp == 0), stop=(hp == 1))
                for n in range(2):
                    for hp in range(2):
                        last = nc.tensor.matmul(ps[:, 7, 128 + 8 * n:136 + 8 * n], QB[:, hp], KTN[:, n, hp, bass.ds(b * 8, 8)],
                                                start=(hp == 0), stop=(hp == 1))
                last.then_inc(t_small, 1)
                for g in range(4):
                    if g < 3:
                        selected_keys(g + 1)
                    pe.wait_ge(a_kt, b * 5 + g + 2)
                    for hp in range(2):
                        last = nc.tensor.matmul(ps[:, g, :], QB[:, hp], (PTB, KTG)[g % 2][:, hp], start=(hp == 0), stop=(hp == 1))
                    last.then_inc(t_sel, 1)
                pe.wait_ge(v_pc, b + 1)
                nc.tensor.matmul(ps[:, 7, 0:128], k_("groupsum"), PC, start=True, stop=True).then_inc(t_imp, 1)

                def turn(n):
                    bank = 4 + n % 2
                    if n == 0:
                        last = nc.tensor.transpose(ps[:, bank, 0:128], PC, ident)
                    elif n == 1:
                        pe.wait_ge(a_p, b * 3 + 2)
                        for w in range(4):
                            last = nc.tensor.transpose(ps[:, bank, w * 128:w * 128 + 128], SW[:, w * 128:w * 128 + 128], ident)
                    elif n == 2:
                        pe.wait_ge(a_p, b * 3 + 3)
                        nc.tensor.transpose(ps[0:8, bank, 0:128], SW[:, 512:520], ident)
                        last = nc.tensor.transpose(ps[0:8, bank, 128:256], SS[:, 2048:2056], ident)
                    else:
                        for q in range(4):
                            o = (n - 3) * 512 + q * 128
                            last = nc.tensor.transpose(ps[:, bank, q * 128:q * 128 + 128], SS[:, o:o + 128], ident)
                    last.then_inc(t_pt, 1)

                def values(n):
                    pe.wait_ge(a_pt, b * 7 + n + 1)
                    if n == 0:
                        pe.wait_ge(v_winm, b + 1)
                        last = nc.tensor.matmul(ps[:, 6, 0:256], PTB[:, 0, 0:128], CV, start=True, stop=True)
                    elif n == 1:
                        for w in range(4):
                            last = nc.tensor.matmul(ps[:, 6, 256:512], PTB[:, 1, w * 128:w * 128 + 128], WINP[w][:, 256:512],
                                                    start=(w == 0), stop=False)
                    elif n == 2:
                        pe.wait_ge(vnew_in, b * 32 + 32)
                        nc.tensor.matmul(ps[:, 6, 256:512], PTB[0:8, 0, 0:128], VN[0:8, 1], start=False, stop=True)
                        last = nc.tensor.matmul(ps[:, 7, 256:512], PTB[0:8, 0, 128:256], VN[0:8, 0], start=True, stop=False)
                    else:
                        for q in range(4):
                            last = nc.tensor.matmul(ps[:, 7, 256:512], PTB[:, n % 2, q * 128:q * 128 + 128],
                                                    PAGES[(n - 3) * 4 + q][:, 768:1024], start=False, stop=(n == 6 and q == 3))
                    last.then_inc(t_pv, 1)

                turn(0)
                for n in range(7):
                    if n < 6:
                        turn(n + 1)
                    values(n)
            pe.wait_ge(v_or, DEC_B + 1)

        def prompt_nsa(pe, t):
            ident, comp = k_("ident"), k_("compress")
            for hp in range(2):
                for u in range(t + 1):
                    nc.tensor.matmul(ps[:, 5, hp * 16:hp * 16 + 16], Z[u][:, ZKV + hp * 128:ZKV + hp * 128 + 128],
                                     comp[:, 120 - 8 * u:136 - 8 * u], start=(u == 0), stop=(u == t))
            pe.wait_ge(v_crep, (1, 3)[t])
            for u in range(t + 1):
                last = nc.tensor.matmul(ps[:, 6, 0:256], CREP[:, u], Z[u][:, ZKV + 256:ZKV + 512], start=(u == 0), stop=(u == t))
            last.then_inc(t_pc, 1)
            pe.wait_ge(v_pck, 5 * t + 5)
            for h in range(HEADS):
                hp, e, g = h // 8, h // 4 % 2, h % 4
                last = nc.tensor.matmul(ps[:, 0 if e else 7, (hp * 4 + g) * 16:(hp * 4 + g) * 16 + 16], QT[64 * e:64 * e + 64, hp * 4 + g, :],
                                        KC[64 * e:64 * e + 64, hp], start=True, stop=True)
            last.then_inc(t_pcs, 1)
            pe.wait_ge(v_pcp, t + 1)
            for o in range(2):
                last = nc.tensor.transpose(ps[:, 5, o * 128:o * 128 + 128], PCM[:, o * 128:o * 128 + 128], ident)
            last.then_inc(t_pct, 1)
            pe.wait_ge(v_pct, t + 1)
            for o in range(2):
                nc.tensor.matmul(ps[:, 6 + o, :], PCT[:, o * 128:o * 128 + 128], VBD[:, o], start=True, stop=True).then_inc(t_pcv, 1)

            def unit_scores(n):
                br, kv = UNITS[n]
                hp, e = kv // 2, kv % 2
                w = (t + 1) * P
                keys = (KTS, KTW)[br - 1]
                if n >= 2:
                    pe.wait_ge(v_um, NU * t + n - 1)
                for g in range(GRP):
                    out = ps[:, 2 * (n % 2) + g // 2, (g % 2) * 256:(g % 2) * 256 + w]
                    last = nc.tensor.matmul(out, QT[64 * e:64 * e + 64, hp * 4 + g, :], keys[64 * e:64 * e + 64, hp, 0:w], start=True, stop=True)
                last.then_inc(t_us, 1)

            pe.wait_ge(v_pcy, 2 * t + 2)
            unit_scores(0)
            for n, (br, kv) in enumerate(UNITS):
                if n + 1 < NU:
                    unit_scores(n + 1)
                pe.wait_ge(a_ue, 4 * (NU * t + n) + 4)
                for kt in range(t + 1):
                    for g in range(GRP):
                        last = nc.tensor.transpose(ps[:, 4 + kt, g * P:g * P + P], PP[:, n % 2, g, kt * P:kt * P + P], ident)
                    last.then_inc(t_ut, 1)
                pe.wait_ge(a_ut, UT0[t] + (t + 1) * (n + 1))
                if n >= 2:
                    pe.wait_ge(v_uy, NU * t + n - 1)
                for g in range(GRP):
                    for kt in range(t + 1):
                        o = ZKV + 512 * br + 256 + kv * 64
                        last = nc.tensor.matmul(ps[:, 6 + n % 2, g * 64:g * 64 + 64], PPT[:, kt, g * P:g * P + P],
                                                Z[kt][:, o:o + 64], start=(kt == 0), stop=(kt == t))
                last.then_inc(t_uv, 1)

        @block.sync
        def _(sp):
            sp.dma_start(KONST, const).then_inc(ld_const, 16)
            sp.dma_start(GB, mlstm_gate_b.rearrange("a b h -> a (b h)").to_broadcast([P, 8])).then_inc(ld_small, 16)
            sp.dma_start(PT_ROW[0:1, :], page_table.rearrange("(a b) g -> a (b g)", a=1)).then_inc(ld_pt, 16)
            x_rows = [x_prompt[0, 0:P], x_prompt[0, P:SEQ], x_sample.rearrange("b s d -> (b s) d")]
            ext_rows = [conv_ext[0:258], conv_ext[0:258], conv_ext[258:338].rearrange("(b s) n -> b s n", s=10)]
            for t in range(TILES):
                r = rows(t)
                W0 = W_LOADS * t
                if t:
                    sp.wait_ge(v_acc0, t)
                sp.dma_start(X[r], x_rows[t]).then_inc(ld_x, 16)
                if t == 0:
                    with nc.allow_non_contiguous_dma(reason="vectors laid along partitions"):
                        sp.dma_start(G1T, norm1_g[0].rearrange("(k p) -> p k", p=P)).then_inc(ld_small, 16)
                        sp.dma_start(G2T, norm2_g[0].rearrange("(k p) -> p k", p=P)).then_inc(ld_small, 16)
                for s in range(NSLOT):
                    sp.dma_start(RING[:, s], w_part(w_in, 0, s)).then_inc(w_slot[s], 16)
                with sp.Fori(1, NFULL) as i:
                    for s in range(NSLOT):
                        sp.wait_ge(w_used, i * NSLOT + (W0 + s - 3))
                        sp.dma_start(RING[:, s], w_part(w_in, i, s)).then_inc(w_slot[s], 16)
                sp.wait_ge(w_used, W0 + 4 * NFULL - 3)
                sp.dma_start(TAILW, w_in[0].rearrange("(k p) n -> p k n", p=P)[:, :, NFULL * WC:]).then_inc(w_tail, 16)
                if t == 0:
                    sp.dma_start(SK, peer_subkeys[0].rearrange("h c n d -> n (h c) d")).then_inc(ld_sk, 16)
                sp.wait_ge(a_z, 13 * t + 17)
                kv = Z[t][r, ZKV:ZKV + 1536]
                if t < 2:
                    q = slice(P * t, P * t + P)
                    sp.dma_start(p_rows[0, 0, q].rearrange("p a h d -> p (a h d)"), kv[:, 0:1024]).then_inc(st_out, 16)
                    sp.dma_start(p_win[0, 0, q].rearrange("p a h d -> p (a h d)"), kv[:, 1024:1536]).then_inc(st_out, 16)
                else:
                    sp.dma_start(new_kv, kv).then_inc(st_kv, 16)
                    sp.dma_start(s_rows[0].rearrange("b s a h d -> (b s) (a h d)"), kv[:, 0:1024]).then_inc(st_out, 16)
                    sp.wait_ge(st_kv, 16)
                    sp.wait_ge(ld_pt, 16)
                    sp.wait_ge(v_qk, 9 * 3)
                    def pages(b, half, done):
                        for g in range(NPAGE):
                            page = sp.value_load(PT_ROW[0:1, bass.ds(b * NPAGE + g, 1)], min_val=0, max_val=159)
                            sp.dma_start(PAGES[g][:, half], cache_nsa_kv[0].rearrange("g p a h d -> g p (a h d)")[bass.ds(page, 1)]
                                         .rearrange("g p n -> (g p) n")[:, half]).then_inc(done, 16)

                    def batch(b):
                        sp.wait_ge(t_pv, b * 7 + 7)
                        for w in range(4):
                            sp.dma_start(WINP[w], state_win_kv[0].rearrange("b (w p) a h d -> b w p (a h d)", p=P)[bass.ds(b, 1), w]
                                         .rearrange("b p n -> (b p) n")).then_inc(win_in, 16)
                        pages(b, slice(512, 1024), sel_in)
                        for n in range(2):
                            sp.dma_start(VN[0:8, n, :], new_kv.rearrange("(b s) n -> b s n", s=8)[bass.ds(b, 1), :, 768 + 512 * n:1024 + 512 * n]
                                         .rearrange("b s n -> (b s) n")).then_inc(vnew_in, 16)

                    def branches(b):
                        sp.wait_ge(v_or, b + 2)
                        for n in range(3):
                            sp.dma_start(branch_out[n].rearrange("b q h d -> b h q d")[bass.ds(b, 1)].rearrange("b h q d -> (b h) q d"),
                                         OROW[:, n, :]).then_inc(st_or, 16)

                    pages(0, slice(0, 512), pages_in)
                    with sp.Fori(0, DEC_B - 1) as b:
                        batch(b)
                        sp.wait_ge(t_cmp, b + 1)
                        pages(b + 1, slice(0, 512), pages_in)
                        branches(b)
                    batch(DEC_B - 1)
                    branches(DEC_B - 1)
                    sp.wait_ge(st_or, 48 * DEC_B + 48)
                    sp.wait_ge(t_pv, 7 * DEC_B + 7)
                    for n in range(3):
                        sp.dma_start(OS[0:64, n, :], branch_out[n].rearrange("b q h d -> (b q) (h d)")).then_inc(ld_os, 16)
                sp.wait_ge(v_qk, 9 * t + 9)
                sp.wait_ge(v_u, 2 * t + 2)
                sp.dma_start(Z[t][:, ZQ:ZQ + 512], mlstm_norm_g.to_broadcast([P, 512])).then_inc(ld_g, 16)
                sp.dma_start(CW[t], conv_w.rearrange("a k n -> a (k n)").to_broadcast([P, 1536])).then_inc(ld_cw, 16)
                u = Z[t][r, CC:CC + 512]
                ext = ext_rows[t]
                if t == 0:
                    sp.dma_start(ext[0:2], ZERO2[0:2]).then_inc(st_u, 16)
                if t < 2:
                    sp.dma_start(ext[2 + P * t:2 + P * t + P], u).then_inc(st_u, 16)
                    sp.wait_ge(st_u, 32 + 16 * t)
                    if t == 1:
                        sp.dma_start(p_conv[0, 0], ext[256:258]).then_inc(st_out, 16)
                    for j, o in ((0, ZQ + 512), (1, CH)):
                        sp.dma_start(Z[t][:, o:o + 512], ext[P * t + j:P * t + j + P]).then_inc(ld_u, 16)
                else:
                    sp.dma_start(ext[:, 0:2], state_conv[0]).then_inc(st_u, 16)
                    sp.dma_start(ext[:, 2:10], u).then_inc(st_u, 16)
                    sp.wait_ge(st_u, 80)
                    sp.dma_start(s_conv[0], ext[:, 8:10]).then_inc(st_out, 16)
                    for j, o in ((0, ZQ + 512), (1, CH)):
                        sp.dma_start(Z[t][r, o:o + 512], ext[:, j:j + 8]).then_inc(ld_u, 16)
                if t == 1:
                    for h in range(MH):
                        sp.wait_ge(v_c, h + 1)
                        sp.dma_start(p_C[0, 0, h], CP).then_inc(st_c, 16)
                    sp.wait_ge(v_no, 1)
                    sp.dma_start(p_n[0, 0], N32[32:36]).then_inc(st_out, 16)
                    sp.dma_start(p_m[0], MNEW[0:1, 1]).then_inc(st_out, 16)
                if t == 2:
                    sp.dma_start(N32[0:32], state_mlstm_n[0].rearrange("b h d -> (b h) d")).then_inc(ld_m, 16)
                    sp.dma_start(M0B[0:8], state_mlstm_m[0]).then_inc(ld_m, 16)
                    for n in range(2 * MH):
                        h = n % MH
                        if 1 <= n <= MH:
                            sp.wait_ge(t_num, 2 * MH + n)
                        elif n > MH:
                            sp.wait_ge(st_c, 16 * n)
                        sp.dma_start(MC, state_mlstm_C[0].rearrange("b h d e -> h d b e")[h]).then_inc(ld_mc, 16)
                        if n >= MH:
                            sp.wait_ge(v_c, n + 1)
                            sp.dma_start(s_C[0].rearrange("b h d e -> h d b e")[h], MC).then_inc(st_c, 16)
                    sp.wait_ge(v_no, 2)
                    sp.dma_start(s_n[0].rearrange("b h d -> (b h) d"), N32[0:32]).then_inc(st_out, 16)
                    for b in range(DEC_B):
                        sp.dma_start(s_m[0, b:b + 1], MNEW[8 * b:8 * b + 1, 2]).then_inc(st_out, 16)
                sp.wait_ge(v_y, t + 1)
                sp.dma_start(X[r], x_rows[t]).then_inc(ld_xr, 16)
                sp.dma_start(G2B[t], norm2_g.to_broadcast([P, D])).then_inc(ld_g2, 16)
                for w, n0 in ((w_out, 4 * NFULL), (peer_wq, 4 * NFULL + 16)):
                    for n in range(16):
                        if n or w is peer_wq:
                            sp.wait_ge(w_used, W0 + n0 + n - 3)
                        sp.dma_start(RING[:, n % 4], w_part(w, n // 4, n % 4)).then_inc(w_slot[n % 4], 16)
                if t == 2:
                    sp.dma_start(s_win[0].rearrange("b w a h d -> b w (a h d)")[:, 0:WIN - 8],
                                 state_win_kv[0].rearrange("b w a h d -> b w (a h d)")[:, 8:WIN]).then_inc(st_out, 16)
                    sp.dma_start(s_win[0].rearrange("b w a h d -> b w (a h d)")[:, WIN - 8:WIN],
                                 new_kv.rearrange("(b s) n -> b s n", s=8)[:, :, 1024:1536]).then_inc(st_out, 16)
                if t:
                    sp.wait_ge(v_x2, t)
                    sp.dma_start(x2_rows[t - 1], ACC).then_inc(st_x2, 16)
            sp.wait_ge(v_route, TILES)
            sp.dma_start(GFB, final_norm_g.rearrange("(a n) -> a n", a=1).to_broadcast([P, D])).then_inc(ld_gf, 16)
            sp.wait_ge(st_x2, 32)
            for t in range(2):
                sp.dma_start(X2[:, t], x2_rows[t]).then_inc(ld_x2, 16)
            for t in range(TILES):
                sp.wait_ge(v_out, t + 1)
                out = y_prompt[0, P * t:P * t + P] if t < 2 else y_sample.rearrange("b s d -> (b s) d")
                sp.dma_start(out, (X2[:, t] if t < 2 else ACC)[rows(t)]).then_inc(st_out, 16)
            sp.wait_ge(st_c, 16 * 2 * MH)
            sp.wait_ge(st_out, 16 * 23)

        @block.tensor
        def _(pe):
            ident, ones, comp = k_("ident"), k_("ones"), k_("compress")
            pe.wait_ge(ld_const, 16)

            def transposed(t, src, done):
                r = ROWS[t]
                for j in range(4):
                    for q in range(4):
                        k = 4 * j + q
                        last = nc.tensor.transpose(ps[:, j, q * P:q * P + r], src[0:r, k * P:(k + 1) * P], ident[0:r, 0:r])
                    last.then_inc(done, 1)

            for t in range(TILES):
                r = ROWS[t]
                W0 = W_LOADS * t
                z = Z[t]
                if t:
                    pe.wait_ge(a_sc, 4 * t)
                pe.wait_ge(a_xn, t + 1)
                transposed(t, X, t_x)
                pe.wait_ge(v_xt, 4 * t + 4)
                with pe.Fori(0, NFULL // 4) as i:
                    for c in range(4):
                        pe.wait_ge(a_z, i * 4 + (13 * t + c + 1))
                        for s in range(NSLOT):
                            pe.wait_ge(w_slot[s], i * 64 + (16 * (W_LOADS // 4) * t + 16 * c + 16))
                            for j in range(KS):
                                k = KS * s + j
                                last = nc.tensor.matmul(ps[0:r, 4 + c, :], XT[:, k, 0:r], RING[:, s, j, :], start=(k == 0), stop=(k == KT - 1))
                            last.then_inc(w_used, 1)
                pe.wait_ge(w_tail, 16 * t + 16)
                pe.wait_ge(a_z, 13 * t + NFULL + 1)
                for k in range(KT):
                    last = nc.tensor.matmul(ps[0:r, 4, 0:TAIL], XT[:, k, 0:r], TAILW[:, k, :], start=(k == 0), stop=(k == KT - 1))
                last.then_inc(z_done, 1)
                pe.wait_ge(a_z, 13 * t + 17)
                for n in range(12):
                    o = ZQ + P * n if n < 8 else ZKV + 512 * (1 + (n - 8) // 2) + P * (n % 2)
                    last = nc.tensor.transpose(ps[:, n // 4, (n % 4) * P:(n % 4) * P + r], z[0:r, o:o + P], ident[0:r, 0:r])
                    if n % 4 == 3:
                        last.then_inc(t_qk, 1)

                def mlstm_qk():
                    for n, o in ((0, ZMQ), (1, ZMK)):
                        for h in range(MH):
                            last = nc.tensor.transpose(ps[:, 3 + 2 * n, h * P:h * P + r], z[0:r, o + h * P:o + h * P + P], ident[0:r, 0:r])
                        last.then_inc(t_mt, 1)

                if t < 2:
                    mlstm_qk()
                pe.wait_ge(v_qk, 9 * t + 9)
                if t == 2:
                    sample_nsa(pe)
                    mlstm_qk()
                else:
                    pe.wait_ge(a_mt, 2 * t + 2)
                    prompt_nsa(pe, t)
                if t == 2:
                    pe.wait_ge(a_mt, 6)
                    pe.wait_ge(ld_m, 32)
                    nc.tensor.transpose(ps[:, 6, 0:32], N32[0:32, :], ident[0:32, 0:32])
                    nc.tensor.matmul(ps[0:64, 7, 0:4], k_("spread")[0:8, :], M0B[0:8, :], start=True, stop=True).then_inc(t_mn, 1)
                pe.wait_ge(v_flog, t + 1)
                if t < 2:
                    if t:
                        nc.tensor.matmul(ps[:, 2, 0:4], ones, FLOG[:, 0], start=True, stop=False)
                    nc.tensor.matmul(ps[:, 2, 0:4], k_("tri"), FLOG[:, t], start=(t == 0), stop=True).then_inc(t_bc, 1)
                else:
                    nc.tensor.matmul(ps[0:64, 2, 0:4], k_("blocktri")[0:64, :], FLOG[0:64, 2], start=True, stop=True).then_inc(t_bc, 1)
                    pe.wait_ge(v_mn, 2)
                tiles = range(t + 1) if t < 2 else (2,)
                w = P * (t + 1) if t < 2 else 64
                for h in range(MH):
                    hh = MH * t + h
                    vals = [Z[u][0:ROWS[u], ZMV + h * P:ZMV + h * P + P] for u in tiles]
                    pe.wait_ge(v_dg, hh + 1)
                    if h:
                        pe.wait_ge(v_wqk, hh)
                    for n in range(len(tiles)):
                        nc.tensor.matmul(ps[0:r, 0, n * P:n * P + min(r, P)], ones[0:r, 0:r], DG[0:r, n * P:n * P + r], start=True, stop=True)
                    nc.tensor.matmul(ps[0:r, 1, 0:w], MQT[:, h, 0:r], MKT[:, h, 0:w], start=True, stop=True).then_inc(t_gr, 1)
                    pe.wait_ge(v_wqk, hh + 1)
                    for n in range(len(tiles)):
                        last = nc.tensor.transpose(ps[0:r, 2, n * P:n * P + r], MW[0:r, n * P:n * P + r], ident[0:r, 0:r])
                    last.then_inc(t_mwt, 1)
                    pe.wait_ge(a_mwt, hh + 1)
                    if h:
                        pe.wait_ge(v_hn, hh)
                    for n, v in enumerate(vals):
                        last = nc.tensor.matmul(ps[0:r, 3, 0:P], MWT[0:r, n * P:n * P + r], v, start=(n == 0), stop=(n == len(vals) - 1))
                    if t == 2:
                        nc.tensor.matmul(ps[0:64, 3, P:P + 8], MQT[:, h, 0:64], NT.rearrange("p (b h) -> p h b", h=MH)[:, h], start=True, stop=True)
                        pe.wait_ge(ld_mc, 16 * h + 16)
                        for j in range(2):
                            last = nc.tensor.matmul(ps[0:64, 4 + j, :], MQT[:, h, 0:64], MC[:, 4 * j:4 * j + 4], start=True, stop=True)
                    last.then_inc(t_num, 1)
                if t:
                    pe.wait_ge(v_bm, t)
                    pe.wait_ge(v_hn, MH * t + MH)
                    lastrow = k_("lastrow") if t == 1 else k_("blocklast")[0:64]
                    nc.tensor.matmul(ps[0:r, 0, 0:4], lastrow, MMAX[0:r, t], start=True, stop=True)
                    nc.tensor.matmul(ps[0:r, 0, 8:12], lastrow, BM[0:r, t], start=True, stop=True).then_inc(t_ml, 1)
                    if t == 2:
                        pe.wait_ge(v_decd, 4)
                        nc.tensor.matmul(ps[:, 1, 0:32], ones[0:64], DECD[0:64].rearrange("p h b -> p (h b)"), start=True, stop=True).then_inc(t_decb, 1)
                    for h in range(MH):
                        n_c = MH * (t - 1) + h
                        pe.wait_ge(v_kw, n_c + 1)
                        if h:
                            pe.wait_ge(v_c, n_c)
                        if t == 1:
                            for u in range(2):
                                nc.tensor.matmul(ps[:, 2, 0:P], KW[:, u], Z[u][:, ZMV + h * P:ZMV + h * P + P], start=(u == 0), stop=(u == 1))
                            for u in range(2):
                                last = nc.tensor.matmul(ps[:, 2, P:P + 1], KW[:, u], ones[:, 0:1], start=(u == 0), stop=(u == 1))
                        else:
                            nc.tensor.matmul(ps[:, 2, 0:8], KW[0:64, 0], k_("batchmask")[0:64], start=True, stop=True)
                            for j in range(2):
                                last = nc.tensor.matmul(ps[:, 3 + j, :], KW[0:64, 0], VB[0:64, 4 * j:4 * j + 4], start=True, stop=True)
                        last.then_inc(t_c, 1)
                    pe.wait_ge(v_c, MH * t)
                    nc.tensor.transpose(ps[0:36, 0, 0:128], NO, ident).then_inc(t_no, 1)
                    pe.wait_ge(v_no, t)
                pe.wait_ge(v_y, t + 1)
                pe.wait_ge(v_hn, MH * t + MH)
                transposed(t, Y, t_y)
                pe.wait_ge(a_yt, 4 * t + 4)
                for c in range(4):
                    for s in range(NSLOT):
                        pe.wait_ge(w_slot[s], 16 * ((W_LOADS // 4) * t + NFULL + c + 1))
                        for j in range(KS):
                            k = KS * s + j
                            last = nc.tensor.matmul(ps[0:r, 4 + c, :], XT[:, k, 0:r], RING[:, s, j, :], start=(k == 0), stop=(k == KT - 1))
                        last.then_inc(w_used, 1)
                if t == 0:
                    pe.wait_ge(ld_sk, 16)
                    for j in range(4):
                        for q in range(4):
                            last = nc.tensor.transpose(ps[:, j, q * P:q * P + P], SK[:, 4 * j + q], ident)
                        last.then_inc(t_sk, 1)
                    pe.wait_ge(v_sk, 4)
                pe.wait_ge(a_h, t + 1)
                transposed(t, H[t], t_h)
                pe.wait_ge(a_ht, 16 * t + 16)
                pe.wait_ge(v_x1, 4 * t + 4)
                for c in range(4):
                    if c >= 2:
                        pe.wait_ge(a_qp, 16 * t + 4 * c - 4)
                    for s in range(NSLOT):
                        pe.wait_ge(w_slot[s], 16 * ((W_LOADS // 4) * t + NFULL + 4 + c + 1))
                        for j in range(4):
                            for k in range(KS):
                                last = nc.tensor.matmul(ps[:, 4 * (c % 2) + j, 0:r], RING[:, s, k, j * P:j * P + P], XT[:, KS * s + k, 0:r],
                                                        start=(s == 0 and k == 0), stop=(s == 3 and k == KS - 1))
                        last.then_inc(w_used, 1)
                pe.wait_ge(a_qp, 16 * t + 16)
                for j in range(4):
                    for q in range(4):
                        last = nc.tensor.matmul(ps[0:r, j, q * P:q * P + P], QP[:, 4 * j + q, 0:r], SKT[:, 4 * j + q], start=True, stop=True)
                    last.then_inc(t_sc, 1)

        @block.scalar
        def _(act):
            act.sem_inc(a_z, 4)

            def gelu_exp(i):
                act.wait_ge(v_ge, i + 1)
                nc.scalar.activation(GE1, GE1, ACT.Exp, scale=-GELU_C).then_inc(a_ge, 1)

            for t in range(TILES):
                m, r, z = ROWS[t], rows(t), Z[t]
                W0 = W_LOADS * t
                act.wait_ge(ld_x, 16 * t + 16)
                nc.scalar.activation(Y[r], X[r], ACT.Square, accum_out=ss[r, 0:1]).then_inc(a_own, 1)
                act.wait_ge(v_rstd1, 2 * t + 1)
                nc.scalar.activation(rstd[r, 0:1], ss[r, 0:1], ACT.Sqrt).then_inc(a_own, 1)
                act.wait_ge(v_rstd1, 2 * t + 2)
                nc.scalar.activation(X[r], X[r], ACT.Copy, scale=rstd[r, 0:1]).then_inc(a_xn, 1)
                if t == 2:
                    act.wait_ge(st_out, 16 * 7)
                for c in range(NFULL):
                    act.wait_ge(w_used, W0 + 4 * c + 4)
                    nc.scalar.copy(z[r, c * WC:c * WC + WC], ps[r, 4 + c % 4, :]).then_inc(a_z, 1)
                    if c in GELU_CHUNKS[t]:
                        gelu_exp(PH * (t - 1) + GELU_CHUNKS[t].index(c))
                act.wait_ge(z_done, t + 1)
                nc.scalar.copy(z[r, NFULL * WC:ZC], ps[r, 4, 0:TAIL]).then_inc(a_z, 1)
                act.wait_ge(a_z, 13 * t + 17)
                nc.scalar.activation(GATE[r], z[r, ZG:ZG + 48], ACT.Exp, scale=-1.0).then_inc(a_gate, 1)
                nc.scalar.activation(z[r, ZMO:ZMO + 512], z[r, ZMO:ZMO + 512], ACT.Exp, scale=-1.0).then_inc(a_sig, 1)

                def mlstm_qk():
                    for bank, out in ((3, MQT[:, :, 0:m]), (5, MKT[:, :, P * (t % 2):P * (t % 2) + m])):
                        act.wait_ge(t_mt, 2 * t + 1 + bank // 5)
                        nc.scalar.copy(out, ps[:, bank].rearrange("p (h n) -> p h n", h=MH)[:, :, 0:m]).then_inc(a_mt, 1)

                if t < 2:
                    mlstm_qk()
                    act.wait_ge(v_pcm, t + 1)
                    nc.scalar.activation(PCM, PCM, ACT.Exp, scale=SCALE).then_inc(a_pce, 1)

                    def unit_exp(n):
                        act.wait_ge(v_um, NU * t + n + 1)
                        for g in range(GRP):
                            row = PP[:, n % 2, g, 0:(t + 1) * P]
                            nc.scalar.activation(row, row, ACT.Exp, bias=pmx[:, n % 2, g:g + 1], scale=SCALE,
                                                 accum_out=psm[:, n % 2, g:g + 1]).then_inc(a_ue, 1)

                    unit_exp(0)
                    for n in range(NU):
                        if n + 1 < NU:
                            unit_exp(n + 1)
                        act.wait_ge(t_uv, NU * t + n) if NU * t + n else None
                        for kt in range(t + 1):
                            act.wait_ge(t_ut, UT0[t] + (t + 1) * n + kt + 1)
                            nc.scalar.copy(PPT[:, kt], ps[:, 4 + kt, :]).then_inc(a_ut, 1)
                        if t and n % 4 == 1:
                            gelu_exp(3 + n // 4)
                else:
                    with act.Fori(0, DEC_B // 2) as bb:
                        for x in range(2):
                            def at_batch(per, more):
                                return bb * (2 * per) + (x * per + more)

                            if x == 1:
                                gelu_exp(bb + (PH + 2))
                            act.wait_ge(t_cmp, at_batch(1, 1))
                            nc.scalar.copy(CK.rearrange("p a b -> p (a b)"), ps[:, 6, 0:256]).then_inc(a_cmp, 1)
                            nc.scalar.copy(CV, ps[:, 6, 256:512]).then_inc(a_cmp, 1)

                            def keys(g):
                                act.wait_ge(t_kt, at_batch(5, g + 1))
                                if g == 2:
                                    act.wait_ge(t_wins, at_batch(1, 1))
                                elif g > 2:
                                    act.wait_ge(t_sel, at_batch(4, g - 2))
                                bank = (4, 2)[g % 2]
                                nc.scalar.copy((KTG, PTB)[g % 2], ps[:, bank:bank + 2, :]).then_inc(a_kt, 1)

                            def probs(n):
                                act.wait_ge(t_pt, at_batch(7, n + 1))
                                act.wait_ge(t_pv, at_batch(7, n + 6))
                                if n == 0:
                                    nc.scalar.copy(PTB[:, 0, 0:128], ps[:, 4, 0:128]).then_inc(a_pt, 1)
                                elif n == 2:
                                    nc.scalar.copy(PTB[0:8, 0, 0:256], ps[0:8, 4, 0:256]).then_inc(a_pt, 1)
                                else:
                                    nc.scalar.copy(PTB[:, n % 2, :], ps[:, 4 + n % 2, :]).then_inc(a_pt, 1)

                            keys(0)
                            keys(1)
                            act.wait_ge(v_cmpm, at_batch(1, 1))
                            nc.scalar.activation(PC[:, 0:127], PC[:, 0:127], ACT.Exp, bias=smx[:, 0:1], scale=SCALE,
                                                 accum_out=ssum[:, 0:1]).then_inc(a_p, 1)
                            keys(2)
                            act.wait_ge(v_winm, at_batch(1, 1))
                            nc.scalar.activation(SW, SW, ACT.Exp, bias=smx[:, 2:3], scale=SCALE, accum_out=ssum[:, 2:3]).then_inc(a_p, 1)
                            keys(3)
                            keys(4)
                            probs(0)
                            probs(1)
                            act.wait_ge(v_selm, at_batch(1, 1))
                            nc.scalar.activation(SS, SS, ACT.Exp, bias=smx[:, 1:2], scale=SCALE, accum_out=ssum[:, 1:2]).then_inc(a_p, 1)
                            for n in range(2, 7):
                                probs(n)
                    act.wait_ge(v_u, 6)
                    mlstm_qk()
                act.wait_ge(v_mf, 2 * t + 1)
                nc.scalar.activation(MT2[r, t], MT2[r, t], ACT.Exp, scale=-1.0).then_inc(a_mf, 1)
                act.wait_ge(v_mf, 2 * t + 2)
                nc.scalar.activation(MT2[r, t], MT2[r, t], ACT.Ln).then_inc(a_mf, 1)
                w = P * (t + 1) if t < 2 else 64
                for h in range(MH):
                    act.wait_ge(v_md, MH * t + h + 1)
                    nc.scalar.activation(MW[r, 0:w], MD[r, 0:w], ACT.Exp, bias=MT1[r, t, h:h + 1]).then_inc(a_mw, 1)
                    nc.scalar.activation(EX[r, 0:1 + t // 2], EX[r, 0:1 + t // 2], ACT.Exp).then_inc(a_mw, 1)
                    act.wait_ge(t_mwt, MH * t + h + 1)
                    nc.scalar.copy(MWT[r, 0:w], ps[r, 2, 0:w]).then_inc(a_mwt, 1)
                    if t and h == 1:
                        gelu_exp((5, PH + 6)[t - 1])
                if t == 1:
                    act.wait_ge(v_wl, 1)
                    nc.scalar.activation(WL[:, 0:2], WL[:, 0:2], ACT.Exp).then_inc(a_wl, 1)
                if t == 2:
                    act.wait_ge(v_wl, 3)
                    nc.scalar.activation(WL[r, 2], WL[r, 2], ACT.Exp).then_inc(a_wl, 1)
                    nc.scalar.activation(MT1[r, 2], MT1[r, 2], ACT.Exp).then_inc(a_wl, 1)
                act.wait_ge(v_ssq, t + 1)
                nc.scalar.activation(SSQ[r, t], SSQ[r, t], ACT.Sqrt).then_inc(a_ssq, 1)
                for j in range(4):
                    act.wait_ge(t_y, 4 * t + j + 1)
                    nc.scalar.copy(XT[:, 4 * j:4 * j + 4, 0:m], ps[:, j].rearrange("p (q n) -> p q n", q=4)[:, :, 0:m]).then_inc(a_yt, 1)
                if t:
                    gelu_exp(PH * (t - 1) + 5 + t)
                act.wait_ge(v_x1, 4 * t + 4)
                nc.scalar.activation(Y[r], X[r], ACT.Square, accum_out=ss[r, 1:2]).then_inc(a_ss2, 1)
                act.wait_ge(v_ss2, 2 * t + 1)
                nc.scalar.activation(rstd[r, 1:2], ss[r, 1:2], ACT.Sqrt).then_inc(a_ss2, 1)
                act.wait_ge(v_ss2, 2 * t + 2)
                nc.scalar.activation(H[t][r], X[r], ACT.Copy, scale=rstd[r, 1:2]).then_inc(a_h, 1)
                for k in range(KT):
                    if k % 4 == 0:
                        act.wait_ge(t_h, 4 * t + k // 4 + 1)
                    nc.scalar.activation(XT[:, k, 0:m], ps[:, k // 4, (k % 4) * P:(k % 4) * P + m], ACT.Copy, scale=G2T[:, k:k + 1]).then_inc(a_ht, 1)
                for c in range(4):
                    act.wait_ge(w_used, W0 + 4 * NFULL + 16 + 4 * c + 4)
                    for j in range(4):
                        nc.scalar.copy(QP[:, 4 * c + j, 0:m], ps[:, 4 * (c % 2) + j, 0:m]).then_inc(a_qp, 1)
                    if t == 1 and c == 1:
                        gelu_exp(7)
                for j in range(4):
                    act.wait_ge(t_sc, 4 * t + j + 1)
                    nc.scalar.copy(SC[r, 4 * j:4 * j + 4], ps[r, j].rearrange("p (q n) -> p q n", q=4)).then_inc(a_sc, 1)
                act.wait_ge(v_cd, t + 1)
                nc.scalar.activation(GG[r, t % 2], GG[r, t % 2], ACT.Exp).then_inc(a_cd, 1)

            def final_norm(t):
                x2 = X2[:, t] if t < 2 else ACC
                nc.scalar.activation(JUNK[t % 2][rows(t)], x2[rows(t)], ACT.Square, accum_out=ss[rows(t), t:t + 1]).then_inc(a_ss3, 1)
                act.wait_ge(v_ss3, t + 1)
                nc.scalar.activation(rstd[rows(t), t:t + 1], ss[rows(t), t:t + 1], ACT.Sqrt).then_inc(a_ss3, 1)

            act.wait_ge(v_acc0, TILES)
            act.wait_ge(ld_x2, 32)
            final_norm(0)
            final_norm(1)
            with act.Fori(2 * PH, 2 * PH + TURNS[2]) as i:
                gelu_exp(i)
            act.wait_ge(v_x2, TILES)
            final_norm(2)


        @block.vector
        def _(dve):
            cnt = Counts(dve)
            PER_BATCH, PER_GATE = 34, 6

            def own(ins, plain=False):
                cnt.own(ins, v_own)
                if plain:
                    nc.vector.memset(WAITED, 0.0)

            def expert_steps(i, t, first, last):
                r = slice(0, P)
                for n in range(first, last):
                    dve.wait_ge(g_in[n % NBUF], i * 128 + (16 * (n // NBUF) + 16))
                    if n < 16:
                        nc.vector.tensor_tensor_reduce(out=PROD[r], in0=BUF[r, n % NBUF], in1=H[t][r], scale=1.0, scalar=0.0, op0=ALU.mult,
                                                       op1=ALU.add, accum_out=DOTS[r, n:n + 1]).then_inc(g_used, 1)
                    else:
                        nc.vector.scalar_tensor_tensor(out=ACC[r], in0=BUF[r, n % NBUF], scalar=WV[r, n - 16:n - 15], in1=ACC[r],
                                                       op0=ALU.mult, op1=ALU.add).then_inc(g_used, 1)
                    dve.wait_ge(g_used, i * 32 + (n + NBUF + 1))

            def expert_weights(i, t, h):
                r = slice(0, P)
                own(nc.vector.tensor_tensor(GE1[r], DOTS[r], DOTS[r], ALU.mult))
                own(nc.vector.tensor_scalar(GE1[r], GE1[r], GELU_K, 1.0, ALU.mult, ALU.add))
                nc.vector.tensor_tensor(GE1[r], GE1[r], DOTS[r], ALU.mult).then_inc(v_ge, 1)
                dve.wait_ge(a_ge, i + 1)
                own(nc.vector.tensor_scalar(GE2[r], GE1[r], 1.0, None, ALU.add))
                own(nc.vector.reciprocal(GE2[r], GE2[r]))
                own(nc.vector.tensor_tensor(GE2[r], GE2[r], DOTS[r], ALU.mult))
                own(nc.vector.tensor_tensor(WV[r], GE2[r], GG[r, t % 2, bass.ds(h * TOPK, TOPK)], ALU.mult))

            def expert_loop(t, first, last):
                with dve.Fori(first, last) as h:
                    cnt.enter(h - first, {v_own: PER_GATE})
                    expert_steps(h + PH * t, t, 0, 16)
                    expert_weights(h + PH * t, t, h)
                    expert_steps(h + PH * t, t, 16, 32)
                    cnt.leave(last - first)

            def best(r, vals, idx, src, work, n):
                for first in (True, False):
                    k = slice(0, 8) if first else slice(8, 16)
                    for i in range(n):
                        ins = nc.vector.max(vals[r, i, k], (src if first else work)[r, i])
                    own(ins)
                    for i in range(n):
                        ins = nc.vector.max_index(idx[r, i, k], vals[r, i, k], (src if first else work)[r, i])
                        if first:
                            ins = nc.vector.match_replace(work[r, i], vals[r, i, k], src[r, i], NEG)
                    own(ins)

            dve.wait_ge(ld_const, 16)
            own(nc.vector.memset(GE1, 0.0))
            own(nc.vector.memset(NO, 0.0))
            own(nc.vector.memset(ZERO2, 0.0))
            dve.sem_inc(g_used, NBUF)
            for t in range(TILES):
                m, r, z = ROWS[t], rows(t), Z[t]
                W0 = W_LOADS * t
                dve.wait_ge(a_own, 2 * t + 1)
                nc.vector.tensor_scalar(ss[r, 0:1], ss[r, 0:1], 1.0 / D, EPS, ALU.mult, ALU.add).then_inc(v_rstd1, 1)
                dve.wait_ge(a_own, 2 * t + 2)
                nc.vector.reciprocal(rstd[r, 0:1], rstd[r, 0:1]).then_inc(v_rstd1, 1)
                dve.wait_ge(ld_small, 48)
                for j in range(4):
                    dve.wait_ge(t_x, 4 * t + j + 1)
                    nc.vector.tensor_tensor(XT[:, 4 * j:4 * j + 4, 0:m], ps[:, j].rearrange("p (q n) -> p q n", q=4)[:, :, 0:m],
                                            bc(G1T[:, 4 * j:4 * j + 4].unsqueeze(2), [P, 4, m]), ALU.mult).then_inc(v_xt, 1)
                if t:
                    expert_loop(t - 1, 0, len(GELU_CHUNKS[t]))
                qt = QTS if t == 2 else QT
                for bank in range(2):
                    dve.wait_ge(t_qk, 3 * t + bank + 1)
                    for e in range(2):
                        for x in range(2):
                            nc.vector.tensor_copy(qt[64 * e:64 * e + 64, 4 * bank:4 * bank + 4].rearrange("p (m x) n -> p x m n", x=2)[:, x, :, 0:m],
                                                  ps[64 * x:64 * x + 64, bank].rearrange("p (e m n) -> p e m n", e=2, m=2)[:, e, :, 0:m]
                                                  ).then_inc(v_qk, 1)
                dve.wait_ge(t_qk, 3 * t + 3)
                if t < 2:
                    nc.vector.tensor_copy(mem3(R_TEMP + 1024, 4, SEQ)[:, :, P * t:P * t + P], ps[:, 2].rearrange("p (i n) -> p i n", i=4)).then_inc(v_qk, 1)
                else:
                    nc.vector.tensor_copy(KTN.rearrange("p b i n -> p (b i) n"), ps[:, 2].rearrange("p (i n) -> p i n", i=4)[:, :, 0:64]).then_inc(v_qk, 1)
                dve.wait_ge(a_gate, t + 1)
                own(nc.vector.tensor_scalar(GATE[r], GATE[r], 1.0, None, ALU.add))
                own(nc.vector.reciprocal(GATE[r], GATE[r]))
                gate = GATE[r].rearrange("p (h n) -> p n h", n=3)
                if t < 2:
                    for u in range(t + 1):
                        nc.vector.tensor_copy(CREP[:, u].rearrange("p (h c) -> p h c", c=16),
                                              bc(k_("compress")[:, 120 - 8 * u:136 - 8 * u].unsqueeze(1), [P, 8, 16])).then_inc(v_crep, 1)
                    dve.wait_ge(a_z, 13 * t + 17)
                    dve.sem_inc(v_u, 1)
                    nc.vector.tensor_tensor(z[r, CC:CC + 512], z[r, CC:CC + 512], z[r, CH:CH + 512], ALU.mult).then_inc(v_u, 1)
                    dve.wait_ge(t_pc, t + 1)
                    nc.vector.tensor_copy(KC.rearrange("p a b -> p (a b)"), ps[:, 5, 0:32]).then_inc(v_pck, 1)
                    for o in range(2):
                        for v in range(2):
                            nc.vector.tensor_tensor(VBD[:, o, 256 * v:256 * v + 256].rearrange("p (g d) -> p g d", g=GRP),
                                                    bc(ps[:, 6, (2 * o + v) * 64:(2 * o + v) * 64 + 64].unsqueeze(1), [P, GRP, HD]),
                                                    bc(k_("headmask")[:, 4 * v:4 * v + 4].unsqueeze(2), [P, GRP, HD]), ALU.mult).then_inc(v_pck, 1)
                    s3 = PCM.rearrange("p (h c) -> p h c", c=16)
                    dve.wait_ge(t_pcs, t + 1)
                    for e in range(2):
                        own(nc.vector.tensor_tensor(PCM.rearrange("p (k e g c) -> p e k g c", e=2, k=2, g=GRP)[:, e],
                                                    ps[:, 0 if e else 7, 0:128].rearrange("p (k g c) -> p k g c", k=2, g=GRP),
                                                    bc(k_("cmpneg%d" % t).unsqueeze(1).unsqueeze(1), [P, 2, GRP, 16]), ALU.add))
                    own(nc.vector.reduce_max(cmx, s3, AX))
                    nc.vector.tensor_tensor(s3, s3, bc(cmx.unsqueeze(2), [P, HEADS, 16]), ALU.subtract).then_inc(v_pcm, 1)
                    dve.wait_ge(a_pce, t + 1)
                    nc.vector.tensor_tensor(s3, s3, bc(k_("cmpone%d" % t).unsqueeze(1), [P, HEADS, 16]), ALU.mult).then_inc(v_pcp, 1)
                    dve.wait_ge(v_pcp, t + 1)
                    own(nc.vector.reduce_sum(csm, s3, AX))
                    own(nc.vector.tensor_scalar(csm, csm, 1e-30, None, ALU.max))
                    own(nc.vector.reciprocal(csm, csm))
                    own(nc.vector.tensor_tensor(csm, csm, gate[:, 0], ALU.mult))
                    dve.wait_ge(t_pct, t + 1)
                    nc.vector.tensor_copy(PCT, ps[:, 5, 0:256]).then_inc(v_pct, 1)
                    for o in range(2):
                        dve.wait_ge(t_pcv, 2 * t + o + 1)
                        nc.vector.tensor_tensor(Y[:, YB + o * 512:YB + o * 512 + 512].rearrange("p (h d) -> p h d", d=HD),
                                                ps[:, 6 + o].rearrange("p (h d) -> p h d", d=HD),
                                                bc(csm[:, 8 * o:8 * o + 8].unsqueeze(2), [P, 8, HD]), ALU.mult).then_inc(v_pcy, 1)

                    def unit_mask(n):
                        if n >= 2:
                            dve.wait_ge(t_ut, UT0[t] + (t + 1) * (n - 1))
                        dve.wait_ge(t_us, NU * t + n + 1)
                        src = ps[:, 2 * (n % 2):2 * (n % 2) + 2].rearrange("p b (g n) -> p (b g) n", n=256)
                        if t:
                            own(nc.vector.tensor_copy(PP[:, n % 2, :, 0:P], src[:, :, 0:P]))
                        own(nc.vector.tensor_tensor(PP[:, n % 2, :, t * P:t * P + P], src[:, :, t * P:t * P + P],
                                                    bc(k_("causal").unsqueeze(1), [P, GRP, P]), ALU.add))
                        own(nc.vector.reduce_max(pmx[:, n % 2], PP[:, n % 2, :, 0:(t + 1) * P], AX))
                        nc.vector.tensor_scalar(pmx[:, n % 2], pmx[:, n % 2], -SCALE, None, ALU.mult).then_inc(v_um, 1)

                    unit_mask(0)
                    dve.wait_ge(v_pcy, 2 * t + 2)
                    for n, (br, kv) in enumerate(UNITS):
                        if n + 1 < NU:
                            unit_mask(n + 1)
                        if t:
                            expert_steps(3 + n // 4, 0, 8 * (n % 4), 8 * (n % 4) + 4)
                        dve.wait_ge(a_ue, 4 * (NU * t + n) + 4)
                        own(nc.vector.reciprocal(pfac[:, n % 2], psm[:, n % 2]))
                        own(nc.vector.tensor_tensor(pfac[:, n % 2], pfac[:, n % 2], gate[:, br, 4 * kv:4 * kv + 4], ALU.mult))
                        dve.wait_ge(t_uv, NU * t + n + 1)
                        own(nc.vector.tensor_tensor(OTMP.rearrange("p (g d) -> p g d", g=GRP),
                                                    ps[:, 6 + n % 2, 0:256].rearrange("p (g d) -> p g d", g=GRP),
                                                    bc(pfac[:, n % 2].unsqueeze(2), [P, GRP, HD]), ALU.mult))
                        y = Y[:, YB + kv * 256:YB + kv * 256 + 256]
                        nc.vector.tensor_tensor(y, y, OTMP, ALU.add).then_inc(v_uy, 1)
                        dve.wait_ge(v_uy, NU * t + n + 1)
                        if t:
                            expert_steps(3 + n // 4, 0, 8 * (n % 4) + 4, 8 * (n % 4) + 8)
                            if n % 4 == 1:
                                expert_weights(3 + n // 4, 0, 3 + n // 4)
                else:
                    own(nc.vector.memset(QB, 0.0))
                    own(nc.vector.memset(PC[:, 127:128], 0.0))
                    dve.sem_inc(v_or, 1)
                    dve.sem_inc(st_or, 48)
                    with dve.Fori(0, DEC_B // 2) as bb:
                        cnt.enter(bb, {v_own: 2 * PER_BATCH + PER_GATE})
                        for x in range(2):
                            def at_batch(per, more):
                                return bb * (2 * per) + (x * per + more)

                            for hp in range(2):
                                for e in range(2):
                                    o = (2 * hp + e) * 32
                                    nc.vector.tensor_copy(QB[64 * e:64 * e + 64, hp, o:o + 32].rearrange("p (g q) -> p g q", g=GRP),
                                                          QTS[64 * e:64 * e + 64, hp * 4:hp * 4 + 4, bass.ds(bb * 16 + 8 * x, 8)]).then_inc(v_qb, 1)
                            if x == 1:
                                expert_weights(bb + (PH + 2), 1, bb + 2)
                            expert_steps(bb + (PH + 2), 1, 16 * x, 16 * x + 8)
                            dve.wait_ge(t_small, at_batch(1, 1))
                            own(nc.vector.tensor_copy(PC[:, 0:127], ps[:, 7, 0:127]))
                            own(nc.vector.tensor_tensor(SS[:, 2048:2056], ps[:, 7, 128:136], k_("newneg"), ALU.add))
                            own(nc.vector.tensor_tensor(SW[:, 512:520], ps[:, 7, 136:144], k_("newneg"), ALU.add))
                            own(nc.vector.reduce_max(smx[:, 0:1], PC[:, 0:127], AX))
                            nc.vector.tensor_scalar(smx[:, 0:1], smx[:, 0:1], -SCALE, None, ALU.mult).then_inc(v_cmpm, 1)
                            dve.wait_ge(t_wins, at_batch(1, 1))
                            own(nc.vector.tensor_tensor(SW[:, 0:8], ps[:, 6, 0:8], k_("oldneg"), ALU.add))
                            own(nc.vector.tensor_copy(SW[:, 8:512], ps[:, 6, 8:512]))
                            own(nc.vector.reduce_max(smx[:, 2:3], SW, AX))
                            nc.vector.tensor_scalar(smx[:, 2:3], smx[:, 2:3], -SCALE, None, ALU.mult).then_inc(v_winm, 1)
                            dve.wait_ge(a_p, at_batch(3, 1))
                            own(nc.vector.reciprocal(srec[:, 0:1], ssum[:, 0:1]))
                            nc.vector.tensor_scalar(PC, PC, srec[:, 0:1], None, ALU.mult).then_inc(v_pc, 1)
                            expert_steps(bb + (PH + 2), 1, 16 * x + 8, 16 * x + 12)
                            dve.wait_ge(t_imp, at_batch(1, 1))
                            own(nc.vector.reduce_sum(blk[:, 0:32], ps[:, 7, 0:128].rearrange("p (n c) -> p n c", c=4), AX))
                            own(nc.vector.memset(blk[:, 0:1], BIG))
                            own(nc.vector.memset(blk[:, 31:33], BIG), plain=True)
                            own(nc.vector.max(top8, blk), plain=True)
                            own(nc.vector.match_replace(blkw, top8, blk, NEG), plain=True)
                            own(nc.vector.max(top8, blkw), plain=True)
                            own(nc.vector.match_replace(blkw, top8, blkw, NEG))
                            own(nc.vector.tensor_tensor(blkb, blk, blkw, ALU.is_equal))
                            own(nc.vector.tensor_scalar(blkb, blkb, NEG, None, ALU.mult))
                            for g in range(4):
                                dve.wait_ge(t_sel, at_batch(4, g + 1))
                                own(nc.vector.tensor_tensor(SS[:, g * 512:g * 512 + 512].rearrange("p (n k) -> p n k", k=64),
                                                            ps[:, g].rearrange("p (n k) -> p n k", k=64),
                                                            bc(blkb[:, 8 * g:8 * g + 8].unsqueeze(2), [P, 8, 64]), ALU.add))
                            own(nc.vector.reduce_max(smx[:, 1:2], SS, AX))
                            nc.vector.tensor_scalar(smx[:, 1:2], smx[:, 1:2], -SCALE, None, ALU.mult).then_inc(v_selm, 1)
                            expert_steps(bb + (PH + 2), 1, 16 * x + 12, 16 * x + 16)
                            dve.wait_ge(a_p, at_batch(3, 3))
                            own(nc.vector.reciprocal(srec[:, 1:3], ssum[:, 1:3]))
                            dve.wait_ge(st_or, at_batch(48, 48))
                            dve.wait_ge(t_pv, at_batch(7, 14))
                            for kv in range(KVH):
                                k = slice(32 * kv, 32 * kv + 32)
                                own(nc.vector.tensor_copy(OROW[k, 0], ps[k, 6, 64 * kv:64 * kv + 64]))
                                own(nc.vector.tensor_scalar(OROW[k, 2], ps[k, 6, 256 + 64 * kv:320 + 64 * kv], srec[k, 2:3], None, ALU.mult))
                                ins = nc.vector.tensor_scalar(OROW[k, 1], ps[k, 7, 256 + 64 * kv:320 + 64 * kv], srec[k, 1:2], None, ALU.mult)
                                own(ins) if kv < 3 else ins.then_inc(v_or, 1)
                        cnt.leave(DEC_B // 2)
                    dve.wait_ge(ld_os, 48)
                    for n in range(3):
                        o = OS[r, n].rearrange("p (h d) -> p h d", d=HD)
                        own(nc.vector.tensor_tensor(o, o, bc(gate[:, n].unsqueeze(2), [m, HEADS, HD]), ALU.mult))
                    own(nc.vector.tensor_tensor(Y[r, YB:YB + NSA_W], OS[r, 0], OS[r, 1], ALU.add))
                    own(nc.vector.tensor_tensor(Y[r, YB:YB + NSA_W], Y[r, YB:YB + NSA_W], OS[r, 2], ALU.add))
                    dve.sem_inc(v_u, 1)
                    nc.vector.tensor_tensor(z[r, CC:CC + 512], z[r, CC:CC + 512], z[r, CH:CH + 512], ALU.mult).then_inc(v_u, 1)
                own(nc.vector.tensor_tensor(ILOG[r, t], z[r, ZMI:ZMI + 4], GB[r, 0:4], ALU.add))
                own(nc.vector.tensor_tensor(FLOG[r, t], z[r, ZMF:ZMF + 4], GB[r, 4:8], ALU.add))
                nc.vector.scalar_tensor_tensor(out=MT2[r, t], in0=FLOG[r, t], scalar=-1.0, in1=FLOG[r, t], op0=ALU.mult, op1=ALU.max).then_inc(v_mf, 1)
                dve.wait_ge(a_mf, 2 * t + 1)
                nc.vector.tensor_scalar(MT2[r, t], MT2[r, t], 1.0, None, ALU.add).then_inc(v_mf, 1)
                dve.wait_ge(a_mf, 2 * t + 2)
                nc.vector.scalar_tensor_tensor(out=FLOG[r, t], in0=FLOG[r, t], scalar=0.0, in1=MT2[r, t], op0=ALU.min, op1=ALU.subtract).then_inc(v_flog, 1)
                if t == 2:
                    dve.wait_ge(t_mn, 1)
                    nc.vector.tensor_copy(NT, ps[:, 6, 0:32]).then_inc(v_mn, 1)
                    nc.vector.tensor_copy(M0[r], ps[r, 7, 0:4]).then_inc(v_mn, 1)
                    dve.wait_ge(v_mn, 2)
                dve.wait_ge(t_bc, t + 1)
                own(nc.vector.tensor_copy(BCUM[r, t], ps[r, 2, 0:4]))
                own(nc.vector.tensor_tensor(GLOG[r, t], ILOG[r, t], BCUM[r, t], ALU.subtract))
                for h in range(MH):
                    hh = MH * t + h
                    tiles = range(t + 1) if t < 2 else (2,)
                    w = P * (t + 1) if t < 2 else 64
                    for n, u in enumerate(tiles):
                        ins = nc.vector.tensor_scalar(DG[r, n * P:n * P + m], k_("ident")[r, r], GLOG[r, u, h:h + 1], None, ALU.mult)
                    ins.then_inc(v_dg, 1)
                    dve.wait_ge(t_gr, hh + 1)
                    if t == 1:
                        own(nc.vector.tensor_copy(MD[:, 0:P], ps[:, 0, 0:P]))
                    own(nc.vector.tensor_tensor(MD[r, w - m:w], ps[r, 0, w - m:w], k_("blockcausal")[r] if t == 2 else k_("causal"), ALU.add))
                    own(nc.vector.reduce_max(MMAX[r, t, h:h + 1], MD[r, 0:w], AX))
                    if t < 2:
                        own(nc.vector.tensor_scalar(MMAX[r, t, h:h + 1], MMAX[r, t, h:h + 1], 0.0, None, ALU.max))
                    else:
                        own(nc.vector.tensor_tensor(MMAX[r, t, h:h + 1], MMAX[r, t, h:h + 1], M0[r, h:h + 1], ALU.max))
                        own(nc.vector.tensor_tensor(EX[r, 1:2], M0[r, h:h + 1], MMAX[r, 2, h:h + 1], ALU.subtract))
                    own(nc.vector.tensor_scalar(MT1[r, t, h:h + 1], MMAX[r, t, h:h + 1], -1.0, None, ALU.mult))
                    nc.vector.tensor_tensor(EX[r, 0:1], MT1[r, t, h:h + 1], BCUM[r, t, h:h + 1], ALU.subtract).then_inc(v_md, 1)
                    dve.wait_ge(a_mw, 2 * hh + 2)
                    nc.vector.scalar_tensor_tensor(out=MW[r, 0:w], in0=ps[r, 1, 0:w], scalar=DH ** -0.5, in1=MW[r, 0:w],
                                                   op0=ALU.mult, op1=ALU.mult, accum_out=DEN[r, 0:1]).then_inc(v_wqk, 1)
                    dve.wait_ge(v_wqk, hh + 1)
                    dve.wait_ge(t_num, hh + 1)
                    if t == 2:
                        bm = k_("batchmask")
                        own(nc.vector.tensor_tensor(QCM[r], ps[r, 4:6, :].rearrange("p j (b e) -> p (j b) e", e=DH),
                                                    bc(bm[r].unsqueeze(2), [m, DEC_B, DH]), ALU.mult))
                        own(nc.vector.reduce_sum(HN[r], QCM[r].rearrange("p b e -> p e b"), AX))
                        own(nc.vector.scalar_tensor_tensor(out=HN[r], in0=HN[r], scalar=EX[r, 1:2], in1=ps[r, 3, 0:P], op0=ALU.mult, op1=ALU.add))
                        own(nc.vector.tensor_tensor(QN[r], ps[r, 3, P:P + 8], bm[r], ALU.mult))
                        own(nc.vector.reduce_sum(DEN[r, 1:2], QN[r], AX))
                        own(nc.vector.scalar_tensor_tensor(out=DEN[r, 0:1], in0=DEN[r, 1:2], scalar=EX[r, 1:2], in1=DEN[r, 0:1], op0=ALU.mult, op1=ALU.add))
                    den = DEN[r, 0:1]
                    own(nc.vector.scalar_tensor_tensor(out=den, in0=den, scalar=-1.0, in1=den, op0=ALU.mult, op1=ALU.max))
                    own(nc.vector.tensor_tensor(den, den, EX[r, 0:1], ALU.max))
                    own(nc.vector.reciprocal(den, den))
                    yh = Y[r, YM + h * DH:YM + h * DH + DH]
                    own(nc.vector.tensor_scalar(yh, HN[r] if t == 2 else ps[:, 3, 0:P], den, None, ALU.mult))
                    own(nc.vector.tensor_tensor_reduce(out=HN[r], in0=yh, in1=yh, scale=1.0, scalar=0.0, op0=ALU.mult, op1=ALU.add,
                                                       accum_out=SSQ[r, t, h:h + 1]))
                    dve.sem_inc(v_hn, 1)
                    if t:
                        expert_steps(PH * (t - 1) + 4 + t, t - 1, 8 * h, 8 * h + 8)
                        if h == 1:
                            expert_weights(PH * (t - 1) + 4 + t, t - 1, 4 + t)
                if t:
                    nc.vector.tensor_tensor(BM[r, t], BCUM[r, t], MMAX[r, t], ALU.add).then_inc(v_bm, 1)
                    dve.wait_ge(t_ml, t)
                    own(nc.vector.tensor_copy(MLAST[r, t], ps[r, 0, 0:4]))
                    own(nc.vector.tensor_copy(MNEW[r, t], ps[r, 0, 8:12]))
                if t == 1:
                    nc.vector.tensor_tensor(WL[:, 0:2], GLOG[:, 0:2], bc(MLAST[:, 1:2], [P, 2, MH]), ALU.subtract).then_inc(v_wl, 1)
                    dve.wait_ge(a_wl, 1)
                if t == 2:
                    nc.vector.tensor_tensor(WL[r, 2], GLOG[r, 2], MLAST[r, 2], ALU.subtract).then_inc(v_wl, 1)
                    nc.vector.tensor_tensor(MT1[r, 2], M0[r], MLAST[r, 2], ALU.subtract).then_inc(v_wl, 1)
                    dve.wait_ge(a_wl, 3)
                    for h in range(MH):
                        nc.vector.tensor_scalar(DECD[r, h], k_("lastmask")[r], MT1[r, 2, h:h + 1], None, ALU.mult).then_inc(v_decd, 1)
                    dve.wait_ge(t_decb, 1)
                    own(nc.vector.tensor_copy(DECB.rearrange("p h b -> p (h b)"), ps[:, 1, 0:32]))
                for h in range(MH if t else 0):
                    n_c = MH * (t - 1) + h
                    if t == 1:
                        for u in range(2):
                            ins = nc.vector.tensor_scalar(KW[:, u], Z[u][:, ZMK + h * DH:ZMK + h * DH + DH], WL[:, u, h:h + 1], DH ** -0.5,
                                                          ALU.mult, ALU.mult)
                        ins.then_inc(v_kw, 1)
                        dve.wait_ge(t_c, n_c + 1)
                        own(nc.vector.tensor_copy(NO[:, 32 + h:33 + h], ps[:, 2, P:P + 1]))
                        if h:
                            dve.wait_ge(st_c, 16 * h)
                        nc.vector.tensor_copy(CP, ps[:, 2, 0:P]).then_inc(v_c, 1)
                    else:
                        nc.vector.tensor_scalar(KW[r, 0], z[r, ZMK + h * DH:ZMK + h * DH + DH], WL[r, 2, h:h + 1], DH ** -0.5, ALU.mult, ALU.mult)
                        nc.vector.tensor_tensor(VB[r], bc(z[r, ZMV + h * DH:ZMV + h * DH + DH].unsqueeze(1), [m, DEC_B, DH]),
                                                bc(k_("batchmask")[r].unsqueeze(2), [m, DEC_B, DH]), ALU.mult).then_inc(v_kw, 1)
                        dve.wait_ge(ld_mc, 16 * (MH + h) + 16)
                        own(nc.vector.tensor_tensor(MC, MC, bc(DECB[:, h].unsqueeze(2), [P, DEC_B, DH]), ALU.mult))
                        nt = NT.rearrange("p (b h) -> p h b", h=MH)[:, h]
                        no = NO[:, 0:32].rearrange("p (b h) -> p h b", h=MH)[:, h]
                        own(nc.vector.tensor_tensor(no, nt, DECB[:, h], ALU.mult))
                        dve.wait_ge(t_c, n_c + 1)
                        own(nc.vector.tensor_tensor(no, no, ps[:, 2, 0:8], ALU.add))
                        nc.vector.tensor_tensor(MC, MC, ps[:, 3:5, :].rearrange("p j (b e) -> p (j b) e", e=DH), ALU.add).then_inc(v_c, 1)
                if t:
                    dve.wait_ge(t_no, t)
                    nc.vector.tensor_copy(N32[0:36], ps[0:36, 0, 0:128]).then_inc(v_no, 1)
                nc.vector.tensor_scalar(SSQ[r, t], SSQ[r, t], 1.0 / DH, EPS, ALU.mult, ALU.add).then_inc(v_ssq, 1)
                dve.wait_ge(a_sig, t + 1)
                dve.wait_ge(ld_g, 16 * t + 16)
                o, y = z[r, ZMO:ZMO + 512], Y[r, YM:YM + ML_W]
                own(nc.vector.tensor_scalar(o, o, 1.0, None, ALU.add))
                own(nc.vector.reciprocal(o, o))
                own(nc.vector.tensor_tensor(o, o, z[r, ZQ:ZQ + 512], ALU.mult))
                own(nc.vector.tensor_tensor(y, y, o, ALU.mult))
                dve.wait_ge(a_ssq, t + 1)
                own(nc.vector.reciprocal(SSQ[r, t], SSQ[r, t]))
                y = y.rearrange("p (h e) -> p h e", h=MH)
                own(nc.vector.tensor_tensor(y, y, bc(SSQ[r, t].unsqueeze(2), [m, MH, DH]), ALU.mult))
                dve.wait_ge(ld_u, 32 * t + 32)
                dve.wait_ge(ld_cw, 16 * t + 16)
                u = [z[r, ZQ + 512:ZQ + 1024], z[r, CH:CH + 512], z[r, CC:CC + 512]]
                for j in range(3):
                    own(nc.vector.tensor_tensor(u[j], u[j], CW[t][r, j], ALU.mult))
                own(nc.vector.tensor_tensor(u[0], u[0], u[1], ALU.add))
                own(nc.vector.tensor_tensor(u[0], u[0], u[2], ALU.add))
                nc.vector.tensor_tensor(Y[r, 0:512], z[r, CB:CB + 512], u[0], ALU.mult).then_inc(v_y, 1)
                dve.wait_ge(ld_xr, 16 * t + 16)
                for c in range(4):
                    if t:
                        h = 5 + t
                        expert_steps(PH * (t - 1) + h, t - 1, 8 * c, 8 * c + 8)
                        if c == 1:
                            expert_weights(PH * (t - 1) + h, t - 1, h)
                    dve.wait_ge(w_used, W0 + 4 * NFULL + 4 * c + 4)
                    x = X[r, c * WC:c * WC + WC]
                    nc.vector.tensor_tensor(x, x, ps[r, 4 + c, :], ALU.add).then_inc(v_x1, 1)
                if t == 2:
                    dve.sem_inc(v_x2, 1)
                if t == 0:
                    for j in range(4):
                        dve.wait_ge(t_sk, j + 1)
                        nc.vector.tensor_copy(SKT[:, 4 * j:4 * j + 4], ps[:, j].rearrange("p (q n) -> p q n", q=4)).then_inc(v_sk, 1)
                dve.wait_ge(a_ss2, 2 * t + 1)
                nc.vector.tensor_scalar(ss[r, 1:2], ss[r, 1:2], 1.0 / D, EPS, ALU.mult, ALU.add).then_inc(v_ss2, 1)
                dve.wait_ge(a_ss2, 2 * t + 2)
                nc.vector.reciprocal(rstd[r, 1:2], rstd[r, 1:2]).then_inc(v_ss2, 1)
                dve.wait_ge(t_h, 4 * t + 4)
                dve.wait_ge(ld_g2, 16 * t + 16)
                own(nc.vector.tensor_tensor(H[t][r], H[t][r], G2B[t][r], ALU.mult))
                if t == 1:
                    expert_steps(7, 0, 0, 16)
                    expert_weights(7, 0, 7)
                    expert_steps(7, 0, 16, 32)
                    dve.sem_inc(v_x2, 1)
                tv = lambda c: TV[r].rearrange("p (h c) k -> p c h k", c=2)[:, c]
                ti = lambda c: TIF[r].rearrange("p (h c) k -> p c h k", c=2)[:, c]
                dve.wait_ge(a_sc, 4 * t + 4)
                best(r, TV, TI, SC, SCW, 16)
                own(nc.vector.tensor_copy(TIF[r], TI[r]))
                own(nc.vector.tensor_tensor(CAND[r].rearrange("p h (i j) -> p h i j", i=TOPK), bc(tv(0).unsqueeze(3), [m, PH, TOPK, TOPK]),
                                            bc(tv(1).unsqueeze(2), [m, PH, TOPK, TOPK]), ALU.add))
                best(r, CVAL, CPOS, CAND, CANDW, PH)
                g = GG[r, t % 2].rearrange("p (h k) -> p h k", h=PH)
                nc.vector.tensor_tensor(g, CVAL[r], bc(CVAL[r, :, 0:1], [m, PH, TOPK]), ALU.subtract).then_inc(v_cd, 1)
                own(nc.vector.tensor_scalar(CHI[r], CPOS[r], 4, None, ALU.logical_shift_right))
                own(nc.vector.tensor_scalar(CLO[r], CPOS[r], 15, None, ALU.bitwise_and))
                own(nc.vector.tensor_copy(FHI[r], CHI[r]))
                own(nc.vector.tensor_copy(FLO[r], CLO[r]))
                for c, rank, num in ((0, FHI, E1), (1, FLO, E2)):
                    oh = OH[r].rearrange("p (h k i) -> p h k i", h=PH, k=TOPK)
                    own(nc.vector.tensor_tensor(OH[r].rearrange("p (x i) -> p x i", i=TOPK), bc(k_("iota16")[r].unsqueeze(1), [m, 128, TOPK]),
                                                bc(rank[r].rearrange("p h k -> p (h k)").unsqueeze(2), [m, 128, TOPK]), ALU.is_equal))
                    own(nc.vector.tensor_tensor(oh, oh, bc(ti(c).unsqueeze(2), [m, PH, TOPK, TOPK]), ALU.mult))
                    own(nc.vector.reduce_sum(num[r].rearrange("p h k -> p (h k)"), OH[r].rearrange("p (x i) -> p x i", i=TOPK), AX))
                own(nc.vector.scalar_tensor_tensor(out=EIDX[r, t % 2], in0=E1[r].rearrange("p h k -> p (h k)"), scalar=float(NKEY),
                                                   in1=E2[r].rearrange("p h k -> p (h k)"), op0=ALU.mult, op1=ALU.add))
                if t == 2:
                    own(nc.vector.tensor_copy(EIDX[64:P, 0, 0:64], EIDX[r, 0, 64:P]))
                    own(nc.vector.tensor_copy(H[2][64:P], H[2][r]))
                dve.sem_inc(v_route, 1)
                dve.wait_ge(a_cd, t + 1)
                own(nc.vector.reduce_sum(GSUM[r], g, AX))
                own(nc.vector.reciprocal(GSUM[r], GSUM[r]))
                own(nc.vector.tensor_tensor(g, g, bc(GSUM[r].unsqueeze(2), [m, PH, TOPK]), ALU.mult))
                if t == 2:
                    own(nc.vector.tensor_copy(GG[64:P, 0, 0:64], GG[r, 0, 64:P]))
                if t:
                    dve.wait_ge(st_x2, 16 * t)
                if t == 2:
                    own(nc.vector.memset(ACC[64:P], 0.0))
                nc.vector.tensor_copy(ACC[r], X[r]).then_inc(v_acc0, 1)
                dve.wait_ge(v_acc0, t + 1)

            def final_norm(t):
                x2, c = (X2[:, t] if t < 2 else ACC)[rows(t)], slice(t, t + 1)
                dve.wait_ge(a_ss3, 2 * t + 1)
                nc.vector.tensor_scalar(ss[rows(t), c], ss[rows(t), c], 1.0 / D, EPS, ALU.mult, ALU.add).then_inc(v_ss3, 1)
                dve.wait_ge(a_ss3, 2 * t + 2)
                own(nc.vector.reciprocal(rstd[rows(t), c], rstd[rows(t), c]))
                nc.vector.scalar_tensor_tensor(out=x2, in0=x2, scalar=rstd[rows(t), c], in1=GFB[rows(t)], op0=ALU.mult, op1=ALU.mult).then_inc(v_out, 1)

            dve.wait_ge(ld_gf, 16)
            final_norm(0)
            final_norm(1)
            expert_loop(2, 0, TURNS[2])
            own(nc.vector.tensor_copy(X[rows(2)], ACC[64:P]))
            nc.vector.tensor_tensor(ACC[rows(2)], ACC[rows(2)], X[rows(2)], ALU.add).then_inc(v_x2, 1)
            final_norm(2)

        @block.gpsimd
        def _(pool):
            u_rows, v_rows = peer_u[0], peer_v[0]

            def wait_apart(sem, value, cell):
                pool.wait_ge(sem, value)
                one = k_("ones")[:, 0:1]
                nc.gpsimd.tensor_tensor(WCELL[:, cell:cell + 1], one, one, ALU.add)

            for t in range(TILES):
                pool.wait_ge(v_route, t + 1)
                with pool.Fori(t * (PH // 2), t * (PH // 2) + TURNS[t] // 2) as i:
                    for x in range(2):
                        pool.wait_ge(g_used, i * 64 + 32 * x + 1)
                        nc.gpsimd.tensor_copy(CUR[:, x], EIDX[:, t % 2, bass.ds((i * 2 + x - t * PH) * TOPK, TOPK)]).then_inc(p_cur, 1)
                        wait_apart(p_cur, i * 2 + x + 1, 33 * x)
                        for n in range(32):
                            wait_apart(g_used, i * 64 + 32 * x + n + 1, 1 + n)
                            nc.gpsimd.indirect_dma_start(BUF[:, n % NBUF], None, u_rows if n < 16 else v_rows,
                                                         bass.IndirectOffsetOnAxis(CUR[:, x, n % 16:n % 16 + 1].bitcast(U32), 0)
                                                         ).then_inc(g_in[n % NBUF], 16)


_INS = ["x_prompt", "x_sample", "cache_nsa_kv", "state_win_kv", "state_conv", "state_mlstm_C", "state_mlstm_n",
        "state_mlstm_m", "page_table", "norm1_g", "w_in", "conv_w", "mlstm_gate_b", "mlstm_norm_g", "w_out", "norm2_g",
        "peer_wq", "peer_subkeys", "peer_u", "peer_v", "final_norm_g"]
_OUTS = [("y_prompt", (1, 256, 2048)), ("y_sample", (8, 8, 2048)), ("p_rows", (1, 1, 256, 4, 4, 64)),
         ("p_win", (1, 1, 256, 2, 4, 64)), ("p_conv", (1, 1, 2, 512)), ("p_C", (1, 1, 4, 128, 128)), ("p_n", (1, 1, 4, 128)),
         ("p_m", (1, 1, 4)), ("s_rows", (1, 8, 8, 4, 4, 64)), ("s_win", (1, 8, 512, 2, 4, 64)), ("s_conv", (1, 8, 2, 512)),
         ("s_C", (1, 8, 4, 128, 128)), ("s_n", (1, 8, 4, 128)), ("s_m", (1, 8, 4))]


def kernel(**inputs):
    import concourse.bacc as _bacc
    from concourse.bass_utils import run_bass_kernel_spmd as _run

    nc = _bacc.Bacc("TRN2", target_bir_lowering=False, num_devices=1)
    at, const = constants()
    arrays = {"in_const_dram": const}
    args = [nc.dram_tensor("in_const_dram", const.shape, F32, kind="ExternalInput").ap()]
    for name in _INS:
        a = np.ascontiguousarray(inputs[name])
        arrays["in_%s_dram" % name] = a
        args.append(nc.dram_tensor("in_%s_dram" % name, a.shape, mybir.dt.from_np(a.dtype), kind="ExternalInput").ap())
    for name, shape in _OUTS:
        args.append(nc.dram_tensor("out_%s_dram" % name, shape, F32, kind="ExternalOutput").ap())
    for name, shape in (("new_kv", (64, 1536)), ("conv_ext", (340, 512)), ("branch_out", (3, 8, 8, 16, 64)), ("x2_rows", (3, 128, 2048))):
        args.append(nc.dram_tensor(name, shape, F32, kind="Internal").ap())
    hybrid_step(nc, at, const.shape[1], *args)
    r = _run(nc, [arrays], core_ids=[0])
    return tuple(r.results[0]["out_%s_dram" % name] for name, _ in _OUTS)
```

```python
from contextlib import ExitStack

import numpy as np

import concourse.bass as bass
from concourse import mybir

F32 = mybir.dt.float32
I32 = mybir.dt.int32
BF16 = mybir.dt.bfloat16
U32 = mybir.dt.uint32
ALU = mybir.AluOpType
ACT = mybir.ActivationFunctionType
AX = mybir.AxisListType.X

P = 128
D = 2048
SEQ, DEC_B, DEC_S = 256, 8, 8
PAST, PAGE = 2048, 128
NPAGE = PAST // PAGE
CONV_W, NSA_W, ML_W = 512, 1024, 512
HD, KVH, GRP = 64, 4, 4
HEADS = KVH * GRP
WIN = 512
MH, DH = 4, 128
PH, NKEY, TOPK = 8, 128, 16
EPS = 1e-6
NEG = -1e30
BIG = 1e9
GELU_C = 2.0 * (2.0 / np.pi) ** 0.5
GELU_K = 0.044715

CB, CC, CH = 0, 512, 1024
ZQ = 1536
ZKV = 2560
ZG = 4096
ZMQ, ZMK, ZMV, ZMO = 4144, 4656, 5168, 5680
ZMI, ZMF = 6192, 6196
ZC = 6200

TILES = 3
ROWS = [128, 128, 64]
KT = D // P

WC = 512
NFULL = ZC // WC
TAIL = ZC - NFULL * WC
NSLOT = 4
KS = KT // NSLOT
W_IN, W_REST = 4 * NFULL, 32
NBUF = 4


def constants():
    r = np.arange(P)
    parts = {}
    parts["ident"] = np.eye(P)
    parts["ones"] = np.ones((P, P))
    parts["tri"] = (r[:, None] <= r[None, :]) * 1.0
    s = np.arange(64)
    same = (s[:, None] // 8 == s[None, :] // 8)
    parts["blocktri"] = np.concatenate([(same & (s[:, None] <= s[None, :])) * 1.0, np.zeros((64, 64))])
    parts["causal"] = np.where(r[None, :] <= r[:, None], 0.0, NEG)
    parts["blockcausal"] = np.concatenate([np.where(same & (s[None, :] <= s[:, None]), 0.0, NEG), np.zeros((64, 64))])
    parts["batchmask"] = np.concatenate([(s[:, None] // 8 == np.arange(8)[None, :]) * 1.0, np.zeros((64, 8))])
    parts["lastmask"] = np.concatenate([(s[:, None] == 8 * np.arange(8)[None, :] + 7) * 1.0, np.zeros((64, 8))])
    parts["lastrow"] = (r[:, None] == 127) * np.ones((P, P))
    parts["blocklast"] = np.concatenate([(s[:, None] == 8 * (s[None, :] // 8) + 7) * 1.0, np.zeros((64, 64))])
    e8 = np.zeros((P, 64))
    e8[:8] = (np.arange(8)[:, None] == s[None, :] // 8)
    parts["spread"] = e8
    y = np.arange(248) - 120
    parts["compress"] = ((16 * y[None, :] <= r[:, None]) & (r[:, None] < 16 * y[None, :] + 32)) / 32.0
    c = np.arange(16)
    for t in range(2):
        q = t * 128 + r
        parts["cmpneg%d" % t] = np.where(16 * c[None, :] + 31 <= q[:, None], 0.0, NEG)
        parts["cmpone%d" % t] = (16 * c[None, :] + 31 <= q[:, None]) * 1.0
    kv, q = r // 32, r % 8
    parts["groupsum"] = ((kv[:, None] == kv[None, :]) & (q[:, None] == q[None, :])) * 1.0
    j = np.arange(8)
    parts["newneg"] = np.where(j[None, :] <= q[:, None], 0.0, NEG)
    parts["oldneg"] = np.where(j[None, :] > q[:, None], 0.0, NEG)
    parts["headmask"] = (r[:, None] // 16 == np.arange(8)[None, :]) * 1.0
    parts["iota16"] = np.ones((P, 1)) * c[None, :]
    at, cols, n = {}, [], 0
    for k, v in parts.items():
        at[k] = (n, n + v.shape[1])
        n += v.shape[1]
        cols.append(v)
    return at, np.ascontiguousarray(np.concatenate(cols, axis=1).astype(np.float32))


class Counts:

    def __init__(self, eng):
        self.eng, self.n, self.i, self.per, self.base = eng, {}, None, {}, {}

    def value(self, sem):
        if self.i is not None and sem in self.per:
            return self.i * self.per[sem] + (self.base.get(sem, 0) + self.n.get(sem, 0))
        return self.n.get(sem, 0)

    def sig(self, ins, sem, amount=1):
        assert self.i is None or sem in self.per, "a semaphore without a count for this loop"
        self.n[sem] = self.n.get(sem, 0) + amount
        ins.then_inc(sem, amount)

    def own(self, ins, sem):
        self.sig(ins, sem)
        self.eng.wait_ge(sem, self.value(sem))

    def enter(self, i, per):
        self.i, self.per = i, per
        self.base = {s: self.n.get(s, 0) for s in per}
        for s in per:
            self.n[s] = 0

    def leave(self, count):
        for s, k in self.per.items():
            assert self.n[s] == k, ("per iteration", self.n[s], "stated", k)
            self.n[s] = self.base[s] + count * k
        self.i, self.per = None, {}


def bc(ap, shape):
    return ap.to_broadcast(shape)


def hybrid_step(nc, at, ncol, const, x_prompt, x_sample, cache_nsa_kv, state_win_kv, state_conv, state_mlstm_C,
                state_mlstm_n, state_mlstm_m, page_table, norm1_g, w_in, conv_w, mlstm_gate_b, mlstm_norm_g,
                w_out, norm2_g, peer_wq, peer_subkeys, peer_u, peer_v, final_norm_g,
                y_prompt, y_sample, p_rows, p_win, p_conv, p_C, p_n, p_m,
                s_rows, s_win, s_conv, s_C, s_n, s_m,
                new_kv, conv_ext, branch_out, x2_rows, z_rows):
    with ExitStack() as ctx:
        def sem(name):
            return ctx.enter_context(nc.semaphore(name))

        CONST = 0
        SMALL = CONST + ncol
        R_BUF = SMALL + 1500
        R_H = R_BUF + NBUF * D
        R_ACC = R_H + 2 * D
        R_PROD = R_ACC + D
        R_X = R_PROD + D // 2
        R_XT = R_X + D
        R_Y = R_XT + D
        R_SKT = R_Y + D
        R_RING = R_SKT + D
        R_Z = R_RING + NSLOT * KS * WC
        R_TEMP = R_Z + 2 * ZC
        ARENA = 53200
        arena = ctx.enter_context(nc.sbuf_tensor("arena", [P, ARENA], F32))

        def mem(start, cols):
            assert start + cols <= ARENA
            return arena[:, start:start + cols]

        def mem3(start, a, b):
            return mem(start, a * b).rearrange("p (a b) -> p a b", a=a)

        KONST = mem(CONST, ncol)
        X, XT, Y = mem(R_X, D), mem3(R_XT, KT, P), mem(R_Y, D)
        QP = mem3(R_Y, 16, P)
        RING = mem(R_RING, NSLOT * KS * WC).rearrange("p (s k n) -> p s k n", s=NSLOT, k=KS)
        TAILW = mem3(R_RING, KT, TAIL)
        Z = [mem(R_Z, ZC), mem(R_Z + ZC, ZC), mem(R_Z, ZC)]
        G2B = [z[:, 0:D] for z in Z]
        XS, XTS = mem(R_Z + ZC, D), mem3(R_Y, KT, 64)
        STAGE = mem3(R_Y + 1024, 2, WC)
        SKT = mem3(R_SKT, 16, P)
        SK = mem3(R_Z + ZC, 16, P)
        BUF = mem3(R_BUF, NBUF, D)
        H = [mem(R_H, D), mem(R_H + D, D), mem(R_H, D)]
        ACC = mem(R_ACC, D)
        PROD = mem(R_PROD, D // 2).bitcast(BF16)
        PP = mem(R_RING, 2048).rearrange("p (u g n) -> p u g n", u=2, g=4)
        PPT = mem3(R_RING + 2048, 2, 512)
        PCM, PCT = mem(R_RING + 3072, 256), mem(R_RING + 3328, 256)
        VBD = mem3(R_RING + 3584, 2, 512)
        KC = mem3(R_RING + 4608, 2, 16)
        OTMP = mem(R_RING + 4640, 256)
        CREP = mem3(R_RING + 4896, 2, 128)
        CW = [mem3(R_X, 3, 512)] * 2 + [mem3(R_Z + ZC + 3072, 3, 512)]
        QT, KTS, KTW = mem3(R_TEMP, 8, P), mem3(R_TEMP + 1024, 2, SEQ), mem3(R_TEMP + 1536, 2, SEQ)
        MQT = mem3(R_TEMP + 2048, MH, P)
        MKT = mem3(R_TEMP + 2560, MH, SEQ)
        MD, MW, MWT, DG = (mem(R_TEMP + 3584 + 256 * n, 256) for n in range(4))
        KW = mem3(R_TEMP + 4608, 2, DH)
        HN = mem(R_TEMP + 4864, DH)
        CP = mem(R_TEMP + 4992, DH)
        N32 = mem(R_TEMP + 5120, DH)
        ZERO2 = mem(R_TEMP + 5248, 512)
        PAGES = [mem(R_Z + ZC + 1024 * g, 1024) for g in range(6)] + [mem(R_RING + 1024 * g, 1024) for g in range(8)] \
            + [mem(R_XT + 1024 * g, 1024) for g in range(2)]
        WINP = [Z[2][:, ZQ + 512 * w:ZQ + 512 * w + 512] for w in range(2)] + [mem(R_X + 512 * w, 512) for w in range(2)]
        QTS = mem3(R_X + 1024, 8, 64)
        KTN = mem(R_X + 1536, 256).rearrange("p (b i n) -> p b i n", b=2, i=2)
        OROW = mem3(R_X + 1792, 3, 64)
        SS, SW, PC = mem(R_TEMP, 2056), mem(R_TEMP + 2056, 520), mem(R_TEMP + 2576, 128)
        KTG, PTB = mem3(R_TEMP + 2704, 2, 512), mem3(R_TEMP + 3728, 2, 512)
        CK, CV = mem3(R_TEMP + 4752, 2, 128), mem(R_TEMP + 5008, 256)
        QB, VN = mem3(R_TEMP + 5264, 2, 128), mem3(R_TEMP + 5520, 2, 256)
        assert R_TEMP + 6032 <= ARENA
        OS = [mem(R_XT, 1024), mem(R_XT + 1024, 1024), mem(R_Z + ZC + 4608, 1024)]
        MC, VB, QCM = (mem3(R_Z + ZC + 1024 * n, DEC_B, DH) for n in range(3))
        SC, SCW = mem3(R_RING, 16, P), mem3(R_RING + D, 16, P)
        CAND, CANDW = mem3(R_RING + 2 * D, PH, 256), mem3(R_RING + 3 * D, PH, 256)
        OH = mem(R_XT, D)
        TV, TIF = mem3(R_Y, 16, TOPK), mem3(R_Y + 256, 16, TOPK)
        TI = mem3(R_Y + 512, 16, TOPK).bitcast(U32)
        CVAL, FHI, FLO, E1, E2 = (mem3(R_Y + 768 + 128 * n, PH, TOPK) for n in range(5))
        CPOS, CHI, CLO = (mem3(R_Y + 1408 + 128 * n, PH, TOPK).bitcast(U32) for n in range(3))
        GSUM = mem(R_Y + 1792, PH)
        X2, GFB = mem3(R_Z, TILES, D), mem(R_RING, D)
        XSQ = mem(R_TEMP + 3584, D)
        JUNK = [XSQ, mem(R_RING + D, D)]

        def k_(name):
            a, b = at[name]
            return KONST[:, a:b]

        small_at = [SMALL]

        def small(cols):
            a = small_at[0]
            small_at[0] += cols
            assert small_at[0] <= R_BUF, small_at[0] - SMALL
            return arena[:, a:a + cols]

        def small3(a, b):
            return small(a * b).rearrange("p (a b) -> p a b", a=a)

        G1T, G2T, GB = small(KT), small(KT), small(8)
        ss, rstd = small(4), small(4)
        WAITED = small(1)
        GATE = small(48)
        PT_ROW = small(128).bitcast(I32)
        smx, ssum, srec = small(4), small(4), small(4)
        blk, blkw, blkb, top8 = small(33), small(33), small(33), small(8)
        pmx, psm, pfac = small3(2, 4), small3(2, 4), small3(2, 4)
        cmx, csm = small(16), small(16)
        ILOG, FLOG, BCUM, GLOG, MMAX, MT1, MT2, MLAST, MNEW, WL, SSQ, BM = (small3(TILES, MH) for _ in range(12))
        M0, M0B, DEN, EX, QN = small(MH), small(MH), small(2), small(2), small(8)
        DECD, DECB = small3(MH, DEC_B), small3(MH, DEC_B)
        NT, NO = small(32), small(36)
        EIDX, GG = small3(2, 128).bitcast(I32), small3(2, 128)
        CUR = small3(2, TOPK).bitcast(I32)
        DOTS, GE1, GE2, WV = small(TOPK), small(TOPK), small(TOPK), small(TOPK)
        WCELL = small(34)

        ps = ctx.enter_context(nc.psum_tensor("ps", [P, 8, 512], F32))

        ld_const, ld_x, ld_small, ld_pt = sem("ld_const"), sem("x_in"), sem("ld_small"), sem("ld_page_table")
        v_own, a_own, a_xn = sem("vector_step_done"), sem("x_ss_or_root"), sem("x_scaled")
        v_rstd1, t_x, v_xt = sem("rstd1_ready"), sem("x_transposed"), sem("xt_stored")
        w_slot = [sem("w_slot%d_in" % s) for s in range(NSLOT)]
        w_used, w_tail = sem("w_slot_used"), sem("w_tail_in")
        z_done, a_z = sem("z_product_done"), sem("z_stored")
        ld_xs, a_zs, st_z, ld_z = sem("sample_x_in"), sem("sample_z_staged"), [sem("sample_z_stored%d" % n) for n in range(2)], sem("sample_z_in")
        st_kv, st_out = sem("new_kv_stored"), sem("outputs_stored")
        t_qk, v_qk = sem("qk_transposed"), sem("qkt_stored")
        pages_in, pv_in, win_in, vnew_in = sem("pages_in"), sem("page_values_in"), sem("window_in"), sem("new_values_in")
        v_qb, t_cmp, a_cmp, t_kt, a_kt = sem("qb_ready"), sem("cmp_kv_done"), sem("cmp_kv_stored"), sem("keys_transposed"), sem("keys_stored")
        t_wins, t_small, t_sel = sem("win_scores_done"), sem("cmp_new_scores_done"), sem("sel_scores_done")
        v_winm, v_cmpm, v_selm = sem("win_masked"), sem("cmp_max_ready"), sem("sel_masked")
        a_p, v_pc, t_imp = sem("sample_exp_done"), sem("cmp_probs_ready"), sem("importance_done")
        t_pt, a_pt, t_pv, v_or = sem("probs_transposed"), sem("probs_t_stored"), sem("values_done"), sem("branch_rows_ready")
        st_or, ld_os, a_gate = sem("branch_rows_stored"), sem("branch_rows_in"), sem("gate_exp_done")
        v_crep, t_pc, v_pck, t_pcs, v_pcm, a_pce = (sem("compress_repeated"), sem("pcmp_kv_done"), sem("pcmp_kv_stored"),
                                                    sem("pcmp_scores_done"), sem("pcmp_masked"), sem("pcmp_exp_done"))
        v_pcp, t_pct, v_pct, t_pcv, v_pcy = sem("pcmp_probs_ready"), sem("pcmp_transposed"), sem("pcmp_t_stored"), sem("pcmp_values_done"), sem("pcmp_y_ready")
        t_us, v_um, a_ue, t_ut, a_ut, t_uv, v_uy = (sem("unit_scores_done"), sem("unit_masked"), sem("unit_exp_done"),
                                                    sem("unit_transposed"), sem("unit_t_stored"), sem("unit_values_done"), sem("unit_y_ready"))
        v_u, st_u, ld_u, ld_cw, v_y = sem("conv_u_ready"), sem("conv_u_stored"), sem("shifted_u_in"), sem("conv_w_in"), sem("y_ready")
        ld_m, t_mt, a_mt, t_mn, v_mn = sem("mlstm_state_in"), sem("mlstm_qk_transposed"), sem("mlstm_qkt_stored"), sem("n_m_spread"), sem("n_m_stored")
        v_mf, a_mf, v_flog, t_bc = sem("gate_columns"), sem("gate_exp_ln_done"), sem("log_forget_ready"), sem("cumsum_done")
        v_dg, t_gr, v_md, a_mw, v_wqk = sem("gate_diag_ready"), sem("weights_scores_done"), sem("log_weights_masked"), sem("mlstm_exp_done"), sem("weighted_scores_ready")
        t_mwt, a_mwt, ld_mc, t_num, v_hn = sem("mlstm_w_transposed"), sem("mlstm_wt_stored"), sem("memory_in"), sem("numerator_done"), sem("head_out_ready")
        v_bm, t_ml, v_wl, a_wl, v_decd, t_decb, v_kw, t_c, v_c, st_c = (
            sem("last_columns_ready"), sem("last_rows_spread"), sem("state_weight_logs"), sem("state_weights_exp"), sem("decay_diag_ready"),
            sem("decay_spread"), sem("weighted_keys_ready"), sem("memory_update_done"), sem("memory_ready"), sem("memory_stored"))
        t_no, v_no, a_sig, v_ssq, a_ssq, ld_g = sem("n_transposed"), sem("n_ready"), sem("out_gate_exp"), sem("head_ss_ready"), sem("head_rms_ready"), sem("mlstm_g_in")
        t_y, a_yt, v_x1, ld_xr, a_ss2, v_ss2, a_h, t_h, a_ht = (
            sem("y_transposed"), sem("yt_stored"), sem("x1_ready"), sem("x_again_in"), sem("x1_ss"), sem("x1_rstd"), sem("h_scaled"),
            sem("h_transposed"), sem("ht_stored"))
        ld_g2, ld_gf, ld_sk, t_sk, v_sk, a_qp, t_sc, a_sc = (
            sem("norm2_g_in"), sem("final_g_in"), sem("subkeys_in"), sem("subkeys_transposed"), sem("subkeys_t_stored"),
            sem("peer_q_stored"), sem("key_scores_done"), sem("key_scores_stored"))
        v_cd, a_cd, v_route, v_acc0 = sem("candidates_shifted"), sem("gates_exp"), sem("routes_ready"), sem("peer_sum_starts")
        g_in = [sem("rows_in%d" % n) for n in range(NBUF)]
        g_used, p_cur = sem("rows_used"), sem("numbers_copied")
        v_ge, a_ge = sem("gelu_in_ready"), sem("gelu_exp_done")
        v_x2, st_x2, ld_x2, a_ss3, v_ss3, v_out = sem("x2_ready"), sem("x2_stored"), sem("x2_in"), sem("x2_ss"), sem("x2_rstd"), sem("y_out_ready")
        block = ctx.enter_context(nc.Block())

        SCALE = HD ** -0.5
        YB = CONV_W
        YM = CONV_W + NSA_W
        UNITS = [(br, kv) for br in (1, 2) for kv in range(KVH)]
        NU = len(UNITS)
        UT0 = [0, NU]
        rows = lambda t: slice(0, ROWS[t])
        W0, W1 = [0, W_IN + W_REST], [W_IN, 2 * W_IN + W_REST, 2 * W_IN + 2 * W_REST]
        TURNS = [PH, PH, PH // 2]
        GELU_CHUNKS = [[], [2, 6, 10], []]
        AT_NSA = [None, 3, 0]
        AT_ROWS, AT_STATE, AT_OUT, AT_WQ = [None, 5, 4], [None, None, 5], [None, 6, 6], [None, 7, 7]

        def w_part(w, c, part):
            return w[0].rearrange("(k p) n -> p k n", p=P)[:, KS * part:KS * part + KS, bass.ts(c, WC)]

        def sample_nsa(pe):
            ident, comp = k_("ident"), k_("compress")
            pe.sem_inc(t_pv, 7)
            with pe.Fori(0, DEC_B) as b:
                pe.wait_ge(v_or, b + 1)
                pe.wait_ge(pages_in, b * 256 + 256)

                def selected_keys(g):
                    for hp in range(2):
                        for q in range(4):
                            last = nc.tensor.transpose(ps[:, (2, 4)[g % 2] + hp, q * 128:q * 128 + 128],
                                                       PAGES[4 * g + q][:, 512 + hp * 128:640 + hp * 128], ident)
                    last.then_inc(t_kt, 1)

                for hp in range(2):
                    for g in range(NPAGE):
                        nc.tensor.matmul(ps[:, 6, hp * 128:hp * 128 + 128], PAGES[g][:, hp * 128:hp * 128 + 128],
                                         comp[:, 120 - 8 * g:248 - 8 * g], start=(g == 0), stop=(g == NPAGE - 1))
                for g in range(NPAGE):
                    last = nc.tensor.matmul(ps[:, 6, 256:512], comp[:, 120 - 8 * g:248 - 8 * g], PAGES[g][:, 256:512],
                                            start=(g == 0), stop=(g == NPAGE - 1))
                last.then_inc(t_cmp, 1)
                pe.wait_ge(win_in, b * 64 + 64)
                for hp in range(2):
                    for w in range(4):
                        last = nc.tensor.transpose(ps[:, 4 + hp, w * 128:w * 128 + 128], WINP[w][:, hp * 128:hp * 128 + 128], ident)
                last.then_inc(t_kt, 1)
                selected_keys(0)
                pe.wait_ge(v_qb, b * 4 + 4)
                pe.wait_ge(a_cmp, b * 2 + 2)
                pe.wait_ge(a_kt, b * 5 + 1)
                for hp in range(2):
                    last = nc.tensor.matmul(ps[:, 6, :], QB[:, hp], KTG[:, hp], start=(hp == 0), stop=(hp == 1))
                last.then_inc(t_wins, 1)
                for hp in range(2):
                    nc.tensor.matmul(ps[:, 7, 0:128], QB[:, hp], CK[:, hp], start=(hp == 0), stop=(hp == 1))
                for n in range(2):
                    for hp in range(2):
                        last = nc.tensor.matmul(ps[:, 7, 128 + 8 * n:136 + 8 * n], QB[:, hp], KTN[:, n, hp, bass.ds(b * 8, 8)],
                                                start=(hp == 0), stop=(hp == 1))
                last.then_inc(t_small, 1)
                for g in range(4):
                    if g < 3:
                        selected_keys(g + 1)
                    pe.wait_ge(a_kt, b * 5 + g + 2)
                    for hp in range(2):
                        last = nc.tensor.matmul(ps[:, g, :], QB[:, hp], (PTB, KTG)[g % 2][:, hp], start=(hp == 0), stop=(hp == 1))
                    last.then_inc(t_sel, 1)
                pe.wait_ge(v_pc, b + 1)
                nc.tensor.matmul(ps[:, 7, 0:128], k_("groupsum"), PC, start=True, stop=True).then_inc(t_imp, 1)

                def turn(n):
                    bank = 4 + n % 2
                    if n == 0:
                        last = nc.tensor.transpose(ps[:, bank, 0:128], PC, ident)
                    elif n == 1:
                        pe.wait_ge(a_p, b * 3 + 2)
                        for w in range(4):
                            last = nc.tensor.transpose(ps[:, bank, w * 128:w * 128 + 128], SW[:, w * 128:w * 128 + 128], ident)
                    elif n == 2:
                        pe.wait_ge(a_p, b * 3 + 3)
                        nc.tensor.transpose(ps[0:8, bank, 0:128], SW[:, 512:520], ident)
                        last = nc.tensor.transpose(ps[0:8, bank, 128:256], SS[:, 2048:2056], ident)
                    else:
                        for q in range(4):
                            o = (n - 3) * 512 + q * 128
                            last = nc.tensor.transpose(ps[:, bank, q * 128:q * 128 + 128], SS[:, o:o + 128], ident)
                    last.then_inc(t_pt, 1)

                def values(n):
                    pe.wait_ge(a_pt, b * 7 + n + 1)
                    if n == 0:
                        pe.wait_ge(v_winm, b + 1)
                        last = nc.tensor.matmul(ps[:, 6, 0:256], PTB[:, 0, 0:128], CV, start=True, stop=True)
                    elif n == 1:
                        for w in range(4):
                            last = nc.tensor.matmul(ps[:, 6, 256:512], PTB[:, 1, w * 128:w * 128 + 128], WINP[w][:, 256:512],
                                                    start=(w == 0), stop=False)
                    elif n == 2:
                        pe.wait_ge(vnew_in, b * 32 + 32)
                        nc.tensor.matmul(ps[:, 6, 256:512], PTB[0:8, 0, 0:128], VN[0:8, 1], start=False, stop=True)
                        last = nc.tensor.matmul(ps[:, 7, 256:512], PTB[0:8, 0, 128:256], VN[0:8, 0], start=True, stop=False)
                    else:
                        if n == 3:
                            pe.wait_ge(pv_in, b * 256 + 256)
                        for q in range(4):
                            last = nc.tensor.matmul(ps[:, 7, 256:512], PTB[:, n % 2, q * 128:q * 128 + 128],
                                                    PAGES[(n - 3) * 4 + q][:, 768:1024], start=False, stop=(n == 6 and q == 3))
                    last.then_inc(t_pv, 1)

                turn(0)
                for n in range(7):
                    if n < 6:
                        turn(n + 1)
                    values(n)
            pe.wait_ge(v_or, DEC_B + 1)

        def prompt_nsa(pe, t):
            ident, comp = k_("ident"), k_("compress")
            for hp in range(2):
                for u in range(t + 1):
                    nc.tensor.matmul(ps[:, 5, hp * 16:hp * 16 + 16], Z[u][:, ZKV + hp * 128:ZKV + hp * 128 + 128],
                                     comp[:, 120 - 8 * u:136 - 8 * u], start=(u == 0), stop=(u == t))
            pe.wait_ge(v_crep, (1, 3)[t])
            for u in range(t + 1):
                last = nc.tensor.matmul(ps[:, 6, 0:256], CREP[:, u], Z[u][:, ZKV + 256:ZKV + 512], start=(u == 0), stop=(u == t))
            last.then_inc(t_pc, 1)
            pe.wait_ge(v_pck, 5 * t + 5)
            for h in range(HEADS):
                hp, e, g = h // 8, h // 4 % 2, h % 4
                last = nc.tensor.matmul(ps[:, 0 if e else 7, (hp * 4 + g) * 16:(hp * 4 + g) * 16 + 16], QT[64 * e:64 * e + 64, hp * 4 + g, :],
                                        KC[64 * e:64 * e + 64, hp], start=True, stop=True)
            last.then_inc(t_pcs, 1)
            pe.wait_ge(v_pcp, t + 1)
            for o in range(2):
                last = nc.tensor.transpose(ps[:, 5, o * 128:o * 128 + 128], PCM[:, o * 128:o * 128 + 128], ident)
            last.then_inc(t_pct, 1)
            pe.wait_ge(v_pct, t + 1)
            for o in range(2):
                nc.tensor.matmul(ps[:, 6 + o, :], PCT[:, o * 128:o * 128 + 128], VBD[:, o], start=True, stop=True).then_inc(t_pcv, 1)

            def unit_scores(n):
                br, kv = UNITS[n]
                hp, e = kv // 2, kv % 2
                w = (t + 1) * P
                keys = (KTS, KTW)[br - 1]
                if n >= 2:
                    pe.wait_ge(v_um, NU * t + n - 1)
                for g in range(GRP):
                    out = ps[:, 2 * (n % 2) + g // 2, (g % 2) * 256:(g % 2) * 256 + w]
                    last = nc.tensor.matmul(out, QT[64 * e:64 * e + 64, hp * 4 + g, :], keys[64 * e:64 * e + 64, hp, 0:w], start=True, stop=True)
                last.then_inc(t_us, 1)

            pe.wait_ge(v_pcy, 2 * t + 2)
            unit_scores(0)
            for n, (br, kv) in enumerate(UNITS):
                if n + 1 < NU:
                    unit_scores(n + 1)
                pe.wait_ge(a_ue, 4 * (NU * t + n) + 4)
                for kt in range(t + 1):
                    for g in range(GRP):
                        last = nc.tensor.transpose(ps[:, 4 + kt, g * P:g * P + P], PP[:, n % 2, g, kt * P:kt * P + P], ident)
                    last.then_inc(t_ut, 1)
                pe.wait_ge(a_ut, UT0[t] + (t + 1) * (n + 1))
                if n >= 2:
                    pe.wait_ge(v_uy, NU * t + n - 1)
                for g in range(GRP):
                    for kt in range(t + 1):
                        o = ZKV + 512 * br + 256 + kv * 64
                        last = nc.tensor.matmul(ps[:, 6 + n % 2, g * 64:g * 64 + 64], PPT[:, kt, g * P:g * P + P],
                                                Z[kt][:, o:o + 64], start=(kt == 0), stop=(kt == t))
                last.then_inc(t_uv, 1)

        @block.sync
        def _(sp):
            sp.dma_start(KONST, const).then_inc(ld_const, 16)
            sp.dma_start(GB, mlstm_gate_b.rearrange("a b h -> a (b h)").to_broadcast([P, 8])).then_inc(ld_small, 16)
            sp.dma_start(PT_ROW[0:1, :], page_table.rearrange("(a b) g -> a (b g)", a=1)).then_inc(ld_pt, 16)
            x_rows = [x_prompt[0, 0:P], x_prompt[0, P:SEQ], x_sample.rearrange("b s d -> (b s) d")]
            ext_rows = [conv_ext[0:258], conv_ext[0:258], conv_ext[258:338].rearrange("(b s) n -> b s n", s=10)]
            for t in range(TILES):
                r = rows(t)
                if t < 2:
                    if t:
                        sp.wait_ge(v_acc0, 1)
                    sp.dma_start(X[r], x_rows[t]).then_inc(ld_x, 16)
                    if t:
                        sp.dma_start(XS[rows(2)], x_rows[2]).then_inc(ld_xs, 16)
                        sp.wait_ge(v_cd, 1)
                    else:
                        with nc.allow_non_contiguous_dma(reason="vectors laid along partitions"):
                            sp.dma_start(G1T, norm1_g[0].rearrange("(k p) -> p k", p=P)).then_inc(ld_small, 16)
                            sp.dma_start(G2T, norm2_g[0].rearrange("(k p) -> p k", p=P)).then_inc(ld_small, 16)
                    for s in range(NSLOT):
                        sp.dma_start(RING[:, s], w_part(w_in, 0, s)).then_inc(w_slot[s], 16)
                    with sp.Fori(1, NFULL) as i:
                        for s in range(NSLOT):
                            sp.wait_ge(w_used, i * NSLOT + (W0[t] + s - 3))
                            sp.dma_start(RING[:, s], w_part(w_in, i, s)).then_inc(w_slot[s], 16)
                    sp.wait_ge(w_used, W0[t] + 4 * NFULL - 3)
                    sp.dma_start(TAILW, w_in[0].rearrange("(k p) n -> p k n", p=P)[:, :, NFULL * WC:]).then_inc(w_tail, 16)
                    if t == 0:
                        sp.dma_start(SK, peer_subkeys[0].rearrange("h c n d -> n (h c) d")).then_inc(ld_sk, 16)
                    sp.wait_ge(a_z, 13 * t + 17)
                else:
                    sp.wait_ge(v_c, MH)
                    sp.wait_ge(st_out, 16 * 7)
                    sp.wait_ge(st_z[0], 16 * 7)
                    sp.wait_ge(st_z[1], 16 * 6)
                    sp.dma_start(Z[2][r], z_rows).then_inc(ld_z, 16)
                    sp.wait_ge(ld_z, 16)
                kv = Z[t][r, ZKV:ZKV + 1536]
                if t < 2:
                    q = slice(P * t, P * t + P)
                    sp.dma_start(p_rows[0, 0, q].rearrange("p a h d -> p (a h d)"), kv[:, 0:1024]).then_inc(st_out, 16)
                    sp.dma_start(p_win[0, 0, q].rearrange("p a h d -> p (a h d)"), kv[:, 1024:1536]).then_inc(st_out, 16)
                else:
                    sp.dma_start(new_kv, kv).then_inc(st_kv, 16)
                    sp.dma_start(s_rows[0].rearrange("b s a h d -> (b s) (a h d)"), kv[:, 0:1024]).then_inc(st_out, 16)
                    sp.wait_ge(st_kv, 16)
                    sp.wait_ge(ld_pt, 16)
                    sp.wait_ge(v_qk, 9 * 3)

                    def pages(b, part, done):
                        for g in range(NPAGE):
                            page = sp.value_load(PT_ROW[0:1, bass.ds(b * NPAGE + g, 1)], min_val=0, max_val=cache_nsa_kv.shape[1] - 1)
                            sp.dma_start(PAGES[g][:, part], cache_nsa_kv[0].rearrange("g p a h d -> g p (a h d)")[bass.ds(page, 1)]
                                         .rearrange("g p n -> (g p) n")[:, part]).then_inc(done, 16)

                    def window(b):
                        for w in range(4):
                            sp.dma_start(WINP[w], state_win_kv[0].rearrange("b (w p) a h d -> b w p (a h d)", p=P)[bass.ds(b, 1), w]
                                         .rearrange("b p n -> (b p) n")).then_inc(win_in, 16)

                    def values(b):
                        sp.wait_ge(t_pv, b * 7 + 7)
                        for n in range(2):
                            sp.dma_start(VN[0:8, n, :], new_kv.rearrange("(b s) n -> b s n", s=8)[bass.ds(b, 1), :, 768 + 512 * n:1024 + 512 * n]
                                         .rearrange("b s n -> (b s) n")).then_inc(vnew_in, 16)
                        pages(b, slice(768, 1024), pv_in)

                    def branches(b):
                        sp.wait_ge(v_or, b + 2)
                        for n in range(3):
                            sp.dma_start(branch_out[n].rearrange("b q h d -> b h q d")[bass.ds(b, 1)].rearrange("b h q d -> (b h) q d"),
                                         OROW[:, n, :]).then_inc(st_or, 16)

                    pages(0, slice(0, 768), pages_in)
                    window(0)
                    with sp.Fori(0, DEC_B - 1) as b:
                        values(b)
                        sp.wait_ge(t_kt, b * 5 + 5)
                        pages(b + 1, slice(0, 768), pages_in)
                        sp.wait_ge(t_pv, b * 7 + 9)
                        window(b + 1)
                        branches(b)
                    values(DEC_B - 1)
                    branches(DEC_B - 1)
                    sp.dma_start(N32[0:32], state_mlstm_n[0].rearrange("b h d -> (b h) d")).then_inc(ld_m, 16)
                    sp.dma_start(M0B[0:8], state_mlstm_m[0]).then_inc(ld_m, 16)
                sp.wait_ge(v_qk, 9 * t + 9)
                sp.wait_ge(v_u, 2 * t + 2)
                sp.dma_start(Z[t][:, ZQ:ZQ + 512], mlstm_norm_g.to_broadcast([P, 512])).then_inc(ld_g, 16)
                sp.dma_start(CW[t], conv_w.rearrange("a k n -> a (k n)").to_broadcast([P, 1536])).then_inc(ld_cw, 16)
                u = Z[t][r, CC:CC + 512]
                ext = ext_rows[t]
                if t == 0:
                    sp.dma_start(ext[0:2], ZERO2[0:2]).then_inc(st_u, 16)
                if t < 2:
                    sp.dma_start(ext[2 + P * t:2 + P * t + P], u).then_inc(st_u, 16)
                    sp.wait_ge(st_u, 32 + 16 * t)
                    if t == 1:
                        sp.dma_start(p_conv[0, 0], ext[256:258]).then_inc(st_out, 16)
                    for j, o in ((0, ZQ + 512), (1, CH)):
                        sp.dma_start(Z[t][:, o:o + 512], ext[P * t + j:P * t + j + P]).then_inc(ld_u, 16)
                else:
                    sp.dma_start(ext[:, 0:2], state_conv[0]).then_inc(st_u, 16)
                    sp.dma_start(ext[:, 2:10], u).then_inc(st_u, 16)
                    sp.wait_ge(st_u, 80)
                    sp.dma_start(s_conv[0], ext[:, 8:10]).then_inc(st_out, 16)
                    for j, o in ((0, ZQ + 512), (1, CH)):
                        sp.dma_start(Z[t][r, o:o + 512], ext[:, j:j + 8]).then_inc(ld_u, 16)
                if t < 2:
                    sp.wait_ge(v_uy, NU * t + NU)
                for n in range(4):
                    sp.dma_start(RING[:, n], w_part(w_out, 0, n)).then_inc(w_slot[n], 16)
                if t == 1:
                    for h in range(MH):
                        sp.wait_ge(v_c, h + 1)
                        sp.dma_start(p_C[0, 0, h], CP).then_inc(st_c, 16)
                    sp.wait_ge(v_no, 1)
                    sp.dma_start(p_n[0, 0], N32[32:36]).then_inc(st_out, 16)
                    sp.dma_start(p_m[0], MNEW[0:1, 1]).then_inc(st_out, 16)
                if t == 2:
                    sp.wait_ge(st_or, 48 * DEC_B + 48)
                    sp.wait_ge(t_pv, 7 * DEC_B + 7)
                    for n in range(3):
                        sp.dma_start(OS[n][0:64], branch_out[n].rearrange("b q h d -> (b q) (h d)")).then_inc(ld_os, 16)
                    for n in range(2 * MH):
                        h = n % MH
                        if 1 <= n <= MH:
                            sp.wait_ge(t_num, 2 * MH + n)
                        elif n > MH:
                            sp.wait_ge(st_c, 16 * n)
                        sp.dma_start(MC, state_mlstm_C[0].rearrange("b h d e -> h d b e")[h]).then_inc(ld_mc, 16)
                        if n >= MH:
                            sp.wait_ge(v_c, n + 1)
                            sp.dma_start(s_C[0].rearrange("b h d e -> h d b e")[h], MC).then_inc(st_c, 16)
                    sp.wait_ge(v_no, 2)
                    sp.dma_start(s_n[0].rearrange("b h d -> (b h) d"), N32[0:32]).then_inc(st_out, 16)
                    for b in range(DEC_B):
                        sp.dma_start(s_m[0, b:b + 1], MNEW[8 * b:8 * b + 1, 2]).then_inc(st_out, 16)
                sp.wait_ge(v_y, t + 1)
                sp.dma_start(X[r], x_rows[t]).then_inc(ld_xr, 16)
                sp.dma_start(G2B[t], norm2_g.to_broadcast([P, D])).then_inc(ld_g2, 16)
                for w, n0 in ((w_out, 0), (peer_wq, 16)):
                    for n in range(4 if w is w_out else 0, 16):
                        sp.wait_ge(w_used, W1[t] + n0 + n - 3)
                        sp.dma_start(RING[:, n % 4], w_part(w, n // 4, n % 4)).then_inc(w_slot[n % 4], 16)
                if t == 2:
                    sp.dma_start(s_win[0].rearrange("b w a h d -> b w (a h d)")[:, 0:WIN - 8],
                                 state_win_kv[0].rearrange("b w a h d -> b w (a h d)")[:, 8:WIN]).then_inc(st_out, 16)
                    sp.dma_start(s_win[0].rearrange("b w a h d -> b w (a h d)")[:, WIN - 8:WIN],
                                 new_kv.rearrange("(b s) n -> b s n", s=8)[:, :, 1024:1536]).then_inc(st_out, 16)
                if t:
                    sp.wait_ge(v_x2, t)
                    sp.dma_start(x2_rows[t - 1], ACC).then_inc(st_x2, 16)
            sp.wait_ge(v_route, TILES)
            sp.dma_start(GFB, final_norm_g.rearrange("(a n) -> a n", a=1).to_broadcast([P, D])).then_inc(ld_gf, 16)
            sp.wait_ge(st_x2, 32)
            for t in range(2):
                sp.dma_start(X2[:, t], x2_rows[t]).then_inc(ld_x2, 16)
            for t in range(TILES):
                sp.wait_ge(v_out, t + 1)
                out = y_prompt[0, P * t:P * t + P] if t < 2 else y_sample.rearrange("b s d -> (b s) d")
                sp.dma_start(out, (X2[:, t] if t < 2 else ACC)[rows(t)]).then_inc(st_out, 16)
            sp.wait_ge(st_c, 16 * 2 * MH)
            sp.wait_ge(st_out, 16 * 23)

        @block.tensor
        def _(pe):
            ident, ones, comp = k_("ident"), k_("ones"), k_("compress")
            pe.wait_ge(ld_const, 16)

            def transposed(t, src, done, bank=0):
                r = ROWS[t]
                for j in range(4):
                    for q in range(4):
                        k = 4 * j + q
                        last = nc.tensor.transpose(ps[:, bank + j, q * P:q * P + r], src[0:r, k * P:(k + 1) * P], ident[0:r, 0:r])
                    last.then_inc(done, 1)

            for t in range(TILES):
                r = ROWS[t]
                z = Z[t]
                if t:
                    pe.wait_ge(a_sc, 4 * t)
                if t < 2:
                    pe.wait_ge(a_xn, t + 1)
                    transposed(t, X, t_x)
                    if t:
                        pe.wait_ge(a_xn, 3)
                        transposed(2, XS, t_x, 4)
                    pe.wait_ge(v_xt, (4, 12)[t])
                    with pe.Fori(0, NFULL // 4) as i:
                        for c in range(4):
                            pe.wait_ge(a_z, i * 4 + (13 * t + c + 1))
                            if t:
                                pe.wait_ge(a_zs, i * 4 + (c + 1))
                            for s in range(NSLOT):
                                pe.wait_ge(w_slot[s], i * 64 + (4 * W0[t] + 16 * c + 16))
                                for bank, lhs, m in ((4 + c, XT, P), (c, XTS, 64))[:t + 1]:
                                    for j in range(KS):
                                        k = KS * s + j
                                        last = nc.tensor.matmul(ps[0:m, bank, :], lhs[:, k, 0:m], RING[:, s, j, :], start=(k == 0), stop=(k == KT - 1))
                                last.then_inc(w_used, 1)
                    pe.wait_ge(w_tail, 16 * t + 16)
                    pe.wait_ge(a_z, 13 * t + NFULL + 1)
                    if t:
                        pe.wait_ge(a_zs, NFULL + 1)
                    for bank, lhs, m in ((4, XT, P), (0, XTS, 64))[:t + 1]:
                        for k in range(KT):
                            last = nc.tensor.matmul(ps[0:m, bank, 0:TAIL], lhs[:, k, 0:m], TAILW[:, k, :], start=(k == 0), stop=(k == KT - 1))
                    last.then_inc(z_done, 1)
                    pe.wait_ge(a_z, 13 * t + 17)
                    if t:
                        pe.wait_ge(a_zs, 17)
                else:
                    pe.wait_ge(ld_z, 16)
                for n in range(12):
                    o = ZQ + P * n if n < 8 else ZKV + 512 * (1 + (n - 8) // 2) + P * (n % 2)
                    last = nc.tensor.transpose(ps[:, n // 4, (n % 4) * P:(n % 4) * P + r], z[0:r, o:o + P], ident[0:r, 0:r])
                    if n % 4 == 3:
                        last.then_inc(t_qk, 1)

                def mlstm_qk():
                    for n, o in ((0, ZMQ), (1, ZMK)):
                        for h in range(MH):
                            last = nc.tensor.transpose(ps[:, 3 + 2 * n, h * P:h * P + r], z[0:r, o + h * P:o + h * P + P], ident[0:r, 0:r])
                        last.then_inc(t_mt, 1)

                if t < 2:
                    mlstm_qk()
                pe.wait_ge(v_qk, 9 * t + 9)
                if t == 2:
                    sample_nsa(pe)
                    mlstm_qk()
                else:
                    pe.wait_ge(a_mt, 2 * t + 2)
                    prompt_nsa(pe, t)
                if t == 2:
                    pe.wait_ge(a_mt, 6)
                    pe.wait_ge(ld_m, 32)
                    nc.tensor.transpose(ps[:, 6, 0:32], N32[0:32, :], ident[0:32, 0:32])
                    nc.tensor.matmul(ps[0:64, 7, 0:4], k_("spread")[0:8, :], M0B[0:8, :], start=True, stop=True).then_inc(t_mn, 1)
                pe.wait_ge(v_flog, t + 1)
                if t < 2:
                    if t:
                        nc.tensor.matmul(ps[:, 2, 0:4], ones, FLOG[:, 0], start=True, stop=False)
                    nc.tensor.matmul(ps[:, 2, 0:4], k_("tri"), FLOG[:, t], start=(t == 0), stop=True).then_inc(t_bc, 1)
                else:
                    nc.tensor.matmul(ps[0:64, 2, 0:4], k_("blocktri")[0:64, :], FLOG[0:64, 2], start=True, stop=True).then_inc(t_bc, 1)
                    pe.wait_ge(v_mn, 2)
                tiles = range(t + 1) if t < 2 else (2,)
                w = P * (t + 1) if t < 2 else 64
                for h in range(MH):
                    hh = MH * t + h
                    vals = [Z[u][0:ROWS[u], ZMV + h * P:ZMV + h * P + P] for u in tiles]
                    pe.wait_ge(v_dg, hh + 1)
                    if h:
                        pe.wait_ge(v_wqk, hh)
                    for n in range(len(tiles)):
                        nc.tensor.matmul(ps[0:r, 0, n * P:n * P + min(r, P)], ones[0:r, 0:r], DG[0:r, n * P:n * P + r], start=True, stop=True)
                    nc.tensor.matmul(ps[0:r, 1, 0:w], MQT[:, h, 0:r], MKT[:, h, 0:w], start=True, stop=True).then_inc(t_gr, 1)
                    pe.wait_ge(v_wqk, hh + 1)
                    for n in range(len(tiles)):
                        last = nc.tensor.transpose(ps[0:r, 2, n * P:n * P + r], MW[0:r, n * P:n * P + r], ident[0:r, 0:r])
                    last.then_inc(t_mwt, 1)
                    pe.wait_ge(a_mwt, hh + 1)
                    if h:
                        pe.wait_ge(v_hn, hh)
                    for n, v in enumerate(vals):
                        last = nc.tensor.matmul(ps[0:r, 3, 0:P], MWT[0:r, n * P:n * P + r], v, start=(n == 0), stop=(n == len(vals) - 1))
                    if t == 2:
                        nc.tensor.matmul(ps[0:64, 3, P:P + 8], MQT[:, h, 0:64], NT.rearrange("p (b h) -> p h b", h=MH)[:, h], start=True, stop=True)
                        pe.wait_ge(ld_mc, 16 * h + 16)
                        for j in range(2):
                            last = nc.tensor.matmul(ps[0:64, 4 + j, :], MQT[:, h, 0:64], MC[:, 4 * j:4 * j + 4], start=True, stop=True)
                    last.then_inc(t_num, 1)
                if t:
                    pe.wait_ge(v_bm, t)
                    pe.wait_ge(v_hn, MH * t + MH)
                    lastrow = k_("lastrow") if t == 1 else k_("blocklast")[0:64]
                    nc.tensor.matmul(ps[0:r, 0, 0:4], lastrow, MMAX[0:r, t], start=True, stop=True)
                    nc.tensor.matmul(ps[0:r, 0, 8:12], lastrow, BM[0:r, t], start=True, stop=True).then_inc(t_ml, 1)
                    if t == 2:
                        pe.wait_ge(v_decd, 4)
                        nc.tensor.matmul(ps[:, 1, 0:32], ones[0:64], DECD[0:64].rearrange("p h b -> p (h b)"), start=True, stop=True).then_inc(t_decb, 1)
                    for h in range(MH):
                        n_c = MH * (t - 1) + h
                        pe.wait_ge(v_kw, n_c + 1)
                        if h:
                            pe.wait_ge(v_c, n_c)
                        if t == 1:
                            for u in range(2):
                                nc.tensor.matmul(ps[:, 2, 0:P], KW[:, u], Z[u][:, ZMV + h * P:ZMV + h * P + P], start=(u == 0), stop=(u == 1))
                            for u in range(2):
                                last = nc.tensor.matmul(ps[:, 2, P:P + 1], KW[:, u], ones[:, 0:1], start=(u == 0), stop=(u == 1))
                        else:
                            nc.tensor.matmul(ps[:, 2, 0:8], KW[0:64, 0], k_("batchmask")[0:64], start=True, stop=True)
                            for j in range(2):
                                last = nc.tensor.matmul(ps[:, 3 + j, :], KW[0:64, 0], VB[0:64, 4 * j:4 * j + 4], start=True, stop=True)
                        last.then_inc(t_c, 1)
                    pe.wait_ge(v_c, MH * t)
                    nc.tensor.transpose(ps[0:36, 0, 0:128], NO, ident).then_inc(t_no, 1)
                    pe.wait_ge(v_no, t)
                pe.wait_ge(v_y, t + 1)
                pe.wait_ge(v_hn, MH * t + MH)
                transposed(t, Y, t_y)
                for c in range(4):
                    for s in range(NSLOT):
                        if c == 0:
                            pe.wait_ge(a_yt, 4 * t + s + 1)
                        pe.wait_ge(w_slot[s], 4 * W1[t] + 16 * c + 16)
                        for j in range(KS):
                            k = KS * s + j
                            last = nc.tensor.matmul(ps[0:r, 4 + c, :], XT[:, k, 0:r], RING[:, s, j, :], start=(k == 0), stop=(k == KT - 1))
                        last.then_inc(w_used, 1)
                if t == 0:
                    pe.wait_ge(ld_sk, 16)
                    for j in range(4):
                        for q in range(4):
                            last = nc.tensor.transpose(ps[:, j, q * P:q * P + P], SK[:, 4 * j + q], ident)
                        last.then_inc(t_sk, 1)
                    pe.wait_ge(v_sk, 4)
                pe.wait_ge(a_h, t + 1)
                transposed(t, H[t], t_h)
                pe.wait_ge(v_x1, 4 * t + 4)
                for c in range(4):
                    if c >= 2:
                        pe.wait_ge(a_qp, 16 * t + 4 * c - 4)
                    for s in range(NSLOT):
                        if c == 0:
                            pe.wait_ge(a_ht, 16 * t + 4 * s + 4)
                        pe.wait_ge(w_slot[s], 4 * W1[t] + 64 + 16 * c + 16)
                        for j in range(4):
                            for k in range(KS):
                                last = nc.tensor.matmul(ps[:, 4 * ((c + 1) % 2) + j, 0:r], RING[:, s, k, j * P:j * P + P], XT[:, KS * s + k, 0:r],
                                                        start=(s == 0 and k == 0), stop=(s == 3 and k == KS - 1))
                        last.then_inc(w_used, 1)
                pe.wait_ge(a_qp, 16 * t + 16)
                for j in range(4):
                    for q in range(4):
                        last = nc.tensor.matmul(ps[0:r, j, q * P:q * P + P], QP[:, 4 * j + q, 0:r], SKT[:, 4 * j + q], start=True, stop=True)
                    last.then_inc(t_sc, 1)

        @block.scalar
        def _(act):
            act.sem_inc(a_z, 4)
            act.sem_inc(a_zs, 4)

            def gelu_exp(i):
                act.wait_ge(v_ge, i + 1)
                nc.scalar.activation(GE1, GE1, ACT.Exp, scale=-GELU_C).then_inc(a_ge, 1)

            for t in range(TILES):
                m, r, z = ROWS[t], rows(t), Z[t]
                for u, x in ([(0, X)], [(1, X), (2, XS)], [])[t]:
                    act.wait_ge(ld_x, 16 * u + 16) if u < 2 else act.wait_ge(ld_xs, 16)
                    nc.scalar.activation(XSQ[rows(u)], x[rows(u)], ACT.Square, accum_out=ss[rows(u), 0:1]).then_inc(a_own, 1)
                    act.wait_ge(v_rstd1, 2 * u + 1)
                    nc.scalar.activation(rstd[rows(u), 0:1], ss[rows(u), 0:1], ACT.Sqrt).then_inc(a_own, 1)
                    act.wait_ge(v_rstd1, 2 * u + 2)
                    nc.scalar.activation(x[rows(u)], x[rows(u)], ACT.Copy, scale=rstd[rows(u), 0:1]).then_inc(a_xn, 1)
                    act.wait_ge(a_xn, u + 1)
                if t < 2:
                    for c in range(NFULL + 1):
                        o, w = c * WC, WC if c < NFULL else TAIL
                        act.wait_ge(w_used, W0[t] + 4 * c + 4) if c < NFULL else act.wait_ge(z_done, t + 1)
                        nc.scalar.copy(z[r, o:o + w], ps[r, 4 + c % 4, 0:w]).then_inc(a_z, 1)
                        if t:
                            if c >= 2:
                                act.wait_ge(st_z[c % 2], 16 * (c // 2))
                            nc.scalar.copy(STAGE[rows(2), c % 2, 0:w], ps[rows(2), c % 4, 0:w]).then_inc(a_zs, 1)
                            act.wait_ge(a_zs, c + 5)
                            act.dma_start(z_rows[:, o:o + w], STAGE[rows(2), c % 2, 0:w]).then_inc(st_z[c % 2], 16)
                        if c in GELU_CHUNKS[t]:
                            gelu_exp(PH * (t - 1) + GELU_CHUNKS[t].index(c))
                    act.wait_ge(a_z, 13 * t + 17)
                else:
                    act.wait_ge(ld_z, 16)
                nc.scalar.activation(GATE[r], z[r, ZG:ZG + 48], ACT.Exp, scale=-1.0).then_inc(a_gate, 1)
                nc.scalar.activation(z[r, ZMO:ZMO + 512], z[r, ZMO:ZMO + 512], ACT.Exp, scale=-1.0).then_inc(a_sig, 1)

                def mlstm_qk():
                    for bank, out in ((3, MQT[:, :, 0:m]), (5, MKT[:, :, P * (t % 2):P * (t % 2) + m])):
                        act.wait_ge(t_mt, 2 * t + 1 + bank // 5)
                        nc.scalar.copy(out, ps[:, bank].rearrange("p (h n) -> p h n", h=MH)[:, :, 0:m]).then_inc(a_mt, 1)

                if t < 2:
                    mlstm_qk()
                    act.wait_ge(v_pcm, t + 1)
                    nc.scalar.activation(PCM, PCM, ACT.Exp, scale=SCALE).then_inc(a_pce, 1)

                    def unit_exp(n):
                        act.wait_ge(v_um, NU * t + n + 1)
                        for g in range(GRP):
                            row = PP[:, n % 2, g, 0:(t + 1) * P]
                            nc.scalar.activation(row, row, ACT.Exp, bias=pmx[:, n % 2, g:g + 1], scale=SCALE,
                                                 accum_out=psm[:, n % 2, g:g + 1]).then_inc(a_ue, 1)

                    unit_exp(0)
                    for n in range(NU):
                        act.wait_ge(t_uv, NU * t + n) if NU * t + n else None
                        for kt in range(t + 1):
                            act.wait_ge(t_ut, UT0[t] + (t + 1) * n + kt + 1)
                            nc.scalar.copy(PPT[:, kt], ps[:, 4 + kt, :]).then_inc(a_ut, 1)
                        if n + 1 < NU:
                            unit_exp(n + 1)
                        if t and n % 4 == 1:
                            gelu_exp(AT_NSA[1] + n // 4)
                else:
                    with act.Fori(0, DEC_B // 2) as bb:
                        for x in range(2):
                            def at_batch(per, more):
                                return bb * (2 * per) + (x * per + more)

                            if x == 1:
                                gelu_exp(bb + (PH + AT_NSA[2]))
                            act.wait_ge(t_cmp, at_batch(1, 1))
                            nc.scalar.copy(CK.rearrange("p a b -> p (a b)"), ps[:, 6, 0:256]).then_inc(a_cmp, 1)
                            nc.scalar.copy(CV, ps[:, 6, 256:512]).then_inc(a_cmp, 1)

                            def keys(g):
                                act.wait_ge(t_kt, at_batch(5, g + 1))
                                if g == 2:
                                    act.wait_ge(t_wins, at_batch(1, 1))
                                elif g > 2:
                                    act.wait_ge(t_sel, at_batch(4, g - 2))
                                bank = (4, 2)[g % 2]
                                nc.scalar.copy((KTG, PTB)[g % 2], ps[:, bank:bank + 2, :]).then_inc(a_kt, 1)

                            def probs(n):
                                act.wait_ge(t_pt, at_batch(7, n + 1))
                                act.wait_ge(t_pv, at_batch(7, n + 6))
                                if n == 0:
                                    nc.scalar.copy(PTB[:, 0, 0:128], ps[:, 4, 0:128]).then_inc(a_pt, 1)
                                elif n == 2:
                                    nc.scalar.copy(PTB[0:8, 0, 0:256], ps[0:8, 4, 0:256]).then_inc(a_pt, 1)
                                else:
                                    nc.scalar.copy(PTB[:, n % 2, :], ps[:, 4 + n % 2, :]).then_inc(a_pt, 1)

                            keys(0)
                            keys(1)
                            act.wait_ge(v_cmpm, at_batch(1, 1))
                            nc.scalar.activation(PC[:, 0:127], PC[:, 0:127], ACT.Exp, bias=smx[:, 0:1], scale=SCALE,
                                                 accum_out=ssum[:, 0:1]).then_inc(a_p, 1)
                            keys(2)
                            act.wait_ge(v_winm, at_batch(1, 1))
                            nc.scalar.activation(SW, SW, ACT.Exp, bias=smx[:, 2:3], scale=SCALE, accum_out=ssum[:, 2:3]).then_inc(a_p, 1)
                            keys(3)
                            keys(4)
                            probs(0)
                            probs(1)
                            act.wait_ge(v_selm, at_batch(1, 1))
                            nc.scalar.activation(SS, SS, ACT.Exp, bias=smx[:, 1:2], scale=SCALE, accum_out=ssum[:, 1:2]).then_inc(a_p, 1)
                            for n in range(2, 7):
                                probs(n)
                    mlstm_qk()
                act.wait_ge(v_mf, 2 * t + 1)
                nc.scalar.activation(MT2[r, t], MT2[r, t], ACT.Exp, scale=-1.0).then_inc(a_mf, 1)
                act.wait_ge(v_mf, 2 * t + 2)
                nc.scalar.activation(MT2[r, t], MT2[r, t], ACT.Ln).then_inc(a_mf, 1)
                w = P * (t + 1) if t < 2 else 64
                for h in range(MH):
                    act.wait_ge(v_md, MH * t + h + 1)
                    nc.scalar.activation(MW[r, 0:w], MD[r, 0:w], ACT.Exp, bias=MT1[r, t, h:h + 1]).then_inc(a_mw, 1)
                    nc.scalar.activation(EX[r, 0:1 + t // 2], EX[r, 0:1 + t // 2], ACT.Exp).then_inc(a_mw, 1)
                    act.wait_ge(t_mwt, MH * t + h + 1)
                    nc.scalar.copy(MWT[r, 0:w], ps[r, 2, 0:w]).then_inc(a_mwt, 1)
                    if h == (None, 1, 0)[t]:
                        gelu_exp(PH * (t - 1) + AT_ROWS[t])
                if t == 1:
                    act.wait_ge(v_wl, 1)
                    nc.scalar.activation(WL[:, 0:2], WL[:, 0:2], ACT.Exp).then_inc(a_wl, 1)
                if t == 2:
                    act.wait_ge(v_wl, 3)
                    nc.scalar.activation(WL[r, 2], WL[r, 2], ACT.Exp).then_inc(a_wl, 1)
                    nc.scalar.activation(MT1[r, 2], MT1[r, 2], ACT.Exp).then_inc(a_wl, 1)
                if AT_STATE[t] is not None:
                    gelu_exp(PH * (t - 1) + AT_STATE[t])
                act.wait_ge(v_ssq, t + 1)
                nc.scalar.activation(SSQ[r, t], SSQ[r, t], ACT.Sqrt).then_inc(a_ssq, 1)
                for j in range(4):
                    act.wait_ge(t_y, 4 * t + j + 1)
                    nc.scalar.copy(XT[:, 4 * j:4 * j + 4, 0:m], ps[:, j].rearrange("p (q n) -> p q n", q=4)[:, :, 0:m]).then_inc(a_yt, 1)
                if t:
                    gelu_exp(PH * (t - 1) + AT_OUT[t])
                act.wait_ge(v_x1, 4 * t + 4)
                nc.scalar.activation(Y[r], X[r], ACT.Square, accum_out=ss[r, 1:2]).then_inc(a_ss2, 1)
                act.wait_ge(v_ss2, 2 * t + 1)
                nc.scalar.activation(rstd[r, 1:2], ss[r, 1:2], ACT.Sqrt).then_inc(a_ss2, 1)
                act.wait_ge(v_ss2, 2 * t + 2)
                nc.scalar.activation(H[t][r], X[r], ACT.Copy, scale=rstd[r, 1:2]).then_inc(a_h, 1)
                for k in range(KT):
                    if k % 4 == 0:
                        act.wait_ge(t_h, 4 * t + k // 4 + 1)
                    nc.scalar.activation(XT[:, k, 0:m], ps[:, k // 4, (k % 4) * P:(k % 4) * P + m], ACT.Copy, scale=G2T[:, k:k + 1]).then_inc(a_ht, 1)
                for c in range(4):
                    act.wait_ge(w_used, W1[t] + 16 + 4 * c + 4)
                    for j in range(4):
                        nc.scalar.copy(QP[:, 4 * c + j, 0:m], ps[:, 4 * ((c + 1) % 2) + j, 0:m]).then_inc(a_qp, 1)
                    if AT_WQ[t] is not None and c == 1:
                        gelu_exp(PH * (t - 1) + AT_WQ[t])
                for j in range(4):
                    act.wait_ge(t_sc, 4 * t + j + 1)
                    nc.scalar.copy(SC[r, 4 * j:4 * j + 4], ps[r, j].rearrange("p (q n) -> p q n", q=4)).then_inc(a_sc, 1)
                act.wait_ge(v_cd, t + 1)
                nc.scalar.activation(GG[r, t % 2], GG[r, t % 2], ACT.Exp).then_inc(a_cd, 1)

            def final_norm(t):
                x2 = X2[:, t] if t < 2 else ACC
                nc.scalar.activation(JUNK[t % 2][rows(t)], x2[rows(t)], ACT.Square, accum_out=ss[rows(t), t:t + 1]).then_inc(a_ss3, 1)
                act.wait_ge(v_ss3, t + 1)
                nc.scalar.activation(rstd[rows(t), t:t + 1], ss[rows(t), t:t + 1], ACT.Sqrt).then_inc(a_ss3, 1)

            act.wait_ge(v_route, TILES)
            act.wait_ge(ld_x2, 32)
            final_norm(0)
            final_norm(1)
            with act.Fori(2 * PH, 2 * PH + TURNS[2]) as i:
                gelu_exp(i)
            act.wait_ge(v_x2, TILES)
            final_norm(2)


        @block.vector
        def _(dve):
            cnt = Counts(dve)
            PER_BATCH, PER_GATE = 34, 6

            def own(ins, plain=False):
                cnt.own(ins, v_own)
                if plain:
                    nc.vector.memset(WAITED, 0.0)

            def expert_steps(i, t, first, last):
                r = slice(0, P)
                for n in range(first, last):
                    dve.wait_ge(g_in[n % NBUF], i * 128 + (16 * (n // NBUF) + 16))
                    if n < 16:
                        nc.vector.tensor_tensor_reduce(out=PROD[r], in0=BUF[r, n % NBUF], in1=H[t][r], scale=1.0, scalar=0.0, op0=ALU.mult,
                                                       op1=ALU.add, accum_out=DOTS[r, n:n + 1]).then_inc(g_used, 1)
                    else:
                        nc.vector.scalar_tensor_tensor(out=ACC[r], in0=BUF[r, n % NBUF], scalar=WV[r, n - 16:n - 15], in1=ACC[r],
                                                       op0=ALU.mult, op1=ALU.add).then_inc(g_used, 1)
                    dve.wait_ge(g_used, i * 32 + (n + NBUF + 1))

            def expert_weights(i, t, h):
                r = slice(0, P)
                own(nc.vector.tensor_tensor(GE1[r], DOTS[r], DOTS[r], ALU.mult))
                own(nc.vector.tensor_scalar(GE1[r], GE1[r], GELU_K, 1.0, ALU.mult, ALU.add))
                nc.vector.tensor_tensor(GE1[r], GE1[r], DOTS[r], ALU.mult).then_inc(v_ge, 1)
                dve.wait_ge(a_ge, i + 1)
                own(nc.vector.tensor_scalar(GE2[r], GE1[r], 1.0, None, ALU.add))
                own(nc.vector.reciprocal(GE2[r], GE2[r]))
                own(nc.vector.tensor_tensor(GE2[r], GE2[r], DOTS[r], ALU.mult))
                own(nc.vector.tensor_tensor(WV[r], GE2[r], GG[r, t % 2, bass.ds(h * TOPK, TOPK)], ALU.mult))

            def first_mean(t):
                dve.wait_ge(a_own, 2 * t + 1)
                nc.vector.tensor_scalar(ss[rows(t), 0:1], ss[rows(t), 0:1], 1.0 / D, EPS, ALU.mult, ALU.add).then_inc(v_rstd1, 1)

            def first_rstd(t):
                dve.wait_ge(a_own, 2 * t + 2)
                nc.vector.reciprocal(rstd[rows(t), 0:1], rstd[rows(t), 0:1]).then_inc(v_rstd1, 1)

            def interleaved(t, h, quarter):
                i = PH * (t - 1) + h
                expert_steps(i, t - 1, 8 * quarter, 8 * quarter + 8)
                if quarter == 1:
                    expert_weights(i, t - 1, h)

            def besides_head(t, h):
                r, z = rows(t), Z[t]
                u = [z[r, ZQ + 512:ZQ + 1024], z[r, CH:CH + 512], z[r, CC:CC + 512]]
                if h == 0:
                    o = z[r, ZMO:ZMO + 512]
                    dve.wait_ge(a_sig, t + 1)
                    dve.wait_ge(ld_g, 16 * t + 16)
                    own(nc.vector.tensor_scalar(o, o, 1.0, None, ALU.add))
                    own(nc.vector.reciprocal(o, o))
                    own(nc.vector.tensor_tensor(o, o, z[r, ZQ:ZQ + 512], ALU.mult))
                elif h == 1:
                    dve.wait_ge(ld_u, 32 * t + 32)
                    dve.wait_ge(ld_cw, 16 * t + 16)
                    own(nc.vector.tensor_tensor(u[0], u[0], CW[t][r, 0], ALU.mult))
                    own(nc.vector.tensor_tensor(u[1], u[1], CW[t][r, 1], ALU.mult))
                elif h == 2:
                    own(nc.vector.tensor_tensor(u[2], u[2], CW[t][r, 2], ALU.mult))
                    own(nc.vector.tensor_tensor(u[0], u[0], u[1], ALU.add))
                else:
                    own(nc.vector.tensor_tensor(u[0], u[0], u[2], ALU.add))
                    own(nc.vector.tensor_tensor(Y[r, 0:512], z[r, CB:CB + 512], u[0], ALU.mult))

            def expert_loop(t, first, last):
                with dve.Fori(first, last) as h:
                    cnt.enter(h - first, {v_own: PER_GATE})
                    expert_steps(h + PH * t, t, 0, 16)
                    expert_weights(h + PH * t, t, h)
                    expert_steps(h + PH * t, t, 16, 32)
                    cnt.leave(last - first)

            def best(r, vals, idx, src, work, n):
                for first in (True, False):
                    k = slice(0, 8) if first else slice(8, 16)
                    for i in range(n):
                        ins = nc.vector.max(vals[r, i, k], (src if first else work)[r, i])
                    own(ins)
                    for i in range(n):
                        ins = nc.vector.max_index(idx[r, i, k], vals[r, i, k], (src if first else work)[r, i])
                        if first:
                            ins = nc.vector.match_replace(work[r, i], vals[r, i, k], src[r, i], NEG)
                    own(ins)

            dve.wait_ge(ld_const, 16)
            own(nc.vector.memset(GE1, 0.0))
            own(nc.vector.memset(NO, 0.0))
            dve.sem_inc(g_used, NBUF)
            for t in range(TILES):
                m, r, z = ROWS[t], rows(t), Z[t]
                if t == 0:
                    first_mean(0)
                    first_rstd(0)
                    dve.wait_ge(ld_small, 48)
                if t == 1:
                    first_mean(2)
                    first_rstd(2)
                for u, xt, bank in ([(0, XT, 0)], [(1, XT, 0), (2, XTS, 4)], [])[t]:
                    n = ROWS[u]
                    for j in range(4):
                        dve.wait_ge(t_x, 4 * u + j + 1)
                        nc.vector.tensor_tensor(xt[:, 4 * j:4 * j + 4, 0:n], ps[:, bank + j].rearrange("p (q n) -> p q n", q=4)[:, :, 0:n],
                                                bc(G1T[:, 4 * j:4 * j + 4].unsqueeze(2), [P, 4, n]), ALU.mult).then_inc(v_xt, 1)
                if GELU_CHUNKS[t]:
                    expert_loop(t - 1, 0, len(GELU_CHUNKS[t]))
                qt = QTS if t == 2 else QT
                for bank in range(2):
                    dve.wait_ge(t_qk, 3 * t + bank + 1)
                    for e in range(2):
                        for x in range(2):
                            nc.vector.tensor_copy(qt[64 * e:64 * e + 64, 4 * bank:4 * bank + 4].rearrange("p (m x) n -> p x m n", x=2)[:, x, :, 0:m],
                                                  ps[64 * x:64 * x + 64, bank].rearrange("p (e m n) -> p e m n", e=2, m=2)[:, e, :, 0:m]
                                                  ).then_inc(v_qk, 1)
                dve.wait_ge(t_qk, 3 * t + 3)
                if t < 2:
                    nc.vector.tensor_copy(mem3(R_TEMP + 1024, 4, SEQ)[:, :, P * t:P * t + P], ps[:, 2].rearrange("p (i n) -> p i n", i=4)).then_inc(v_qk, 1)
                else:
                    nc.vector.tensor_copy(KTN.rearrange("p b i n -> p (b i) n"), ps[:, 2].rearrange("p (i n) -> p i n", i=4)[:, :, 0:64]).then_inc(v_qk, 1)
                dve.wait_ge(a_gate, t + 1)
                own(nc.vector.tensor_scalar(GATE[r], GATE[r], 1.0, None, ALU.add))
                own(nc.vector.reciprocal(GATE[r], GATE[r]))
                gate = GATE[r].rearrange("p (h n) -> p n h", n=3)
                if t == 0:
                    own(nc.vector.memset(ZERO2, 0.0))
                dve.sem_inc(v_u, 1)
                nc.vector.tensor_tensor(z[r, CC:CC + 512], z[r, CC:CC + 512], z[r, CH:CH + 512], ALU.mult).then_inc(v_u, 1)
                if t < 2:
                    for u in range(t + 1):
                        nc.vector.tensor_copy(CREP[:, u].rearrange("p (h c) -> p h c", c=16),
                                              bc(k_("compress")[:, 120 - 8 * u:136 - 8 * u].unsqueeze(1), [P, 8, 16])).then_inc(v_crep, 1)
                    dve.wait_ge(t_pc, t + 1)
                    nc.vector.tensor_copy(KC.rearrange("p a b -> p (a b)"), ps[:, 5, 0:32]).then_inc(v_pck, 1)
                    for o in range(2):
                        for v in range(2):
                            nc.vector.tensor_tensor(VBD[:, o, 256 * v:256 * v + 256].rearrange("p (g d) -> p g d", g=GRP),
                                                    bc(ps[:, 6, (2 * o + v) * 64:(2 * o + v) * 64 + 64].unsqueeze(1), [P, GRP, HD]),
                                                    bc(k_("headmask")[:, 4 * v:4 * v + 4].unsqueeze(2), [P, GRP, HD]), ALU.mult).then_inc(v_pck, 1)
                    s3 = PCM.rearrange("p (h c) -> p h c", c=16)
                    dve.wait_ge(t_pcs, t + 1)
                    for e in range(2):
                        own(nc.vector.tensor_tensor(PCM.rearrange("p (k e g c) -> p e k g c", e=2, k=2, g=GRP)[:, e],
                                                    ps[:, 0 if e else 7, 0:128].rearrange("p (k g c) -> p k g c", k=2, g=GRP),
                                                    bc(k_("cmpneg%d" % t).unsqueeze(1).unsqueeze(1), [P, 2, GRP, 16]), ALU.add))
                    own(nc.vector.reduce_max(cmx, s3, AX))
                    nc.vector.tensor_tensor(s3, s3, bc(cmx.unsqueeze(2), [P, HEADS, 16]), ALU.subtract).then_inc(v_pcm, 1)
                    dve.wait_ge(a_pce, t + 1)
                    nc.vector.tensor_tensor(s3, s3, bc(k_("cmpone%d" % t).unsqueeze(1), [P, HEADS, 16]), ALU.mult).then_inc(v_pcp, 1)
                    dve.wait_ge(v_pcp, t + 1)
                    own(nc.vector.reduce_sum(csm, s3, AX))
                    own(nc.vector.tensor_scalar(csm, csm, 1e-30, None, ALU.max))
                    own(nc.vector.reciprocal(csm, csm))
                    own(nc.vector.tensor_tensor(csm, csm, gate[:, 0], ALU.mult))
                    dve.wait_ge(t_pct, t + 1)
                    nc.vector.tensor_copy(PCT, ps[:, 5, 0:256]).then_inc(v_pct, 1)
                    if t:
                        dve.wait_ge(st_z[0], 16 * 7)
                        dve.wait_ge(st_z[1], 16 * 6)
                    for o in range(2):
                        dve.wait_ge(t_pcv, 2 * t + o + 1)
                        nc.vector.tensor_tensor(Y[:, YB + o * 512:YB + o * 512 + 512].rearrange("p (h d) -> p h d", d=HD),
                                                ps[:, 6 + o].rearrange("p (h d) -> p h d", d=HD),
                                                bc(csm[:, 8 * o:8 * o + 8].unsqueeze(2), [P, 8, HD]), ALU.mult).then_inc(v_pcy, 1)

                    def unit_mask(n):
                        if n >= 2:
                            dve.wait_ge(t_ut, UT0[t] + (t + 1) * (n - 1))
                        dve.wait_ge(t_us, NU * t + n + 1)
                        src = ps[:, 2 * (n % 2):2 * (n % 2) + 2].rearrange("p b (g n) -> p (b g) n", n=256)
                        if t:
                            own(nc.vector.tensor_copy(PP[:, n % 2, :, 0:P], src[:, :, 0:P]))
                        own(nc.vector.tensor_tensor(PP[:, n % 2, :, t * P:t * P + P], src[:, :, t * P:t * P + P],
                                                    bc(k_("causal").unsqueeze(1), [P, GRP, P]), ALU.add))
                        own(nc.vector.reduce_max(pmx[:, n % 2], PP[:, n % 2, :, 0:(t + 1) * P], AX))
                        nc.vector.tensor_scalar(pmx[:, n % 2], pmx[:, n % 2], -SCALE, None, ALU.mult).then_inc(v_um, 1)

                    unit_mask(0)
                    dve.wait_ge(v_pcy, 2 * t + 2)
                    for n, (br, kv) in enumerate(UNITS):
                        if n + 1 < NU:
                            unit_mask(n + 1)
                        if t:
                            expert_steps(AT_NSA[1] + n // 4, 0, 8 * (n % 4), 8 * (n % 4) + 4)
                        dve.wait_ge(a_ue, 4 * (NU * t + n) + 4)
                        own(nc.vector.reciprocal(pfac[:, n % 2], psm[:, n % 2]))
                        own(nc.vector.tensor_tensor(pfac[:, n % 2], pfac[:, n % 2], gate[:, br, 4 * kv:4 * kv + 4], ALU.mult))
                        dve.wait_ge(t_uv, NU * t + n + 1)
                        own(nc.vector.tensor_tensor(OTMP.rearrange("p (g d) -> p g d", g=GRP),
                                                    ps[:, 6 + n % 2, 0:256].rearrange("p (g d) -> p g d", g=GRP),
                                                    bc(pfac[:, n % 2].unsqueeze(2), [P, GRP, HD]), ALU.mult))
                        y = Y[:, YB + kv * 256:YB + kv * 256 + 256]
                        nc.vector.tensor_tensor(y, y, OTMP, ALU.add).then_inc(v_uy, 1)
                        dve.wait_ge(v_uy, NU * t + n + 1)
                        if t:
                            expert_steps(AT_NSA[1] + n // 4, 0, 8 * (n % 4) + 4, 8 * (n % 4) + 8)
                            if n % 4 == 1:
                                expert_weights(AT_NSA[1] + n // 4, 0, AT_NSA[1] + n // 4)
                else:
                    own(nc.vector.memset(QB, 0.0))
                    own(nc.vector.memset(PC[:, 127:128], 0.0))
                    dve.sem_inc(v_or, 1)
                    dve.sem_inc(st_or, 48)
                    with dve.Fori(0, DEC_B // 2) as bb:
                        cnt.enter(bb, {v_own: 2 * PER_BATCH + PER_GATE})
                        for x in range(2):
                            def at_batch(per, more):
                                return bb * (2 * per) + (x * per + more)

                            for hp in range(2):
                                for e in range(2):
                                    o = (2 * hp + e) * 32
                                    nc.vector.tensor_copy(QB[64 * e:64 * e + 64, hp, o:o + 32].rearrange("p (g q) -> p g q", g=GRP),
                                                          QTS[64 * e:64 * e + 64, hp * 4:hp * 4 + 4, bass.ds(bb * 16 + 8 * x, 8)]).then_inc(v_qb, 1)
                            if x == 1:
                                expert_weights(bb + (PH + AT_NSA[2]), 1, bb + AT_NSA[2])
                            expert_steps(bb + (PH + AT_NSA[2]), 1, 16 * x, 16 * x + 8)
                            dve.wait_ge(t_small, at_batch(1, 1))
                            own(nc.vector.tensor_copy(PC[:, 0:127], ps[:, 7, 0:127]))
                            own(nc.vector.tensor_tensor(SS[:, 2048:2056], ps[:, 7, 128:136], k_("newneg"), ALU.add))
                            own(nc.vector.tensor_tensor(SW[:, 512:520], ps[:, 7, 136:144], k_("newneg"), ALU.add))
                            own(nc.vector.reduce_max(smx[:, 0:1], PC[:, 0:127], AX))
                            nc.vector.tensor_scalar(smx[:, 0:1], smx[:, 0:1], -SCALE, None, ALU.mult).then_inc(v_cmpm, 1)
                            dve.wait_ge(t_wins, at_batch(1, 1))
                            own(nc.vector.tensor_tensor(SW[:, 0:8], ps[:, 6, 0:8], k_("oldneg"), ALU.add))
                            own(nc.vector.tensor_copy(SW[:, 8:512], ps[:, 6, 8:512]))
                            own(nc.vector.reduce_max(smx[:, 2:3], SW, AX))
                            nc.vector.tensor_scalar(smx[:, 2:3], smx[:, 2:3], -SCALE, None, ALU.mult).then_inc(v_winm, 1)
                            dve.wait_ge(a_p, at_batch(3, 1))
                            own(nc.vector.reciprocal(srec[:, 0:1], ssum[:, 0:1]))
                            nc.vector.tensor_scalar(PC, PC, srec[:, 0:1], None, ALU.mult).then_inc(v_pc, 1)
                            expert_steps(bb + (PH + AT_NSA[2]), 1, 16 * x + 8, 16 * x + 12)
                            dve.wait_ge(t_imp, at_batch(1, 1))
                            own(nc.vector.reduce_sum(blk[:, 0:32], ps[:, 7, 0:128].rearrange("p (n c) -> p n c", c=4), AX))
                            own(nc.vector.memset(blk[:, 0:1], BIG))
                            own(nc.vector.memset(blk[:, 31:33], BIG), plain=True)
                            own(nc.vector.max(top8, blk), plain=True)
                            own(nc.vector.match_replace(blkw, top8, blk, NEG), plain=True)
                            own(nc.vector.max(top8, blkw), plain=True)
                            own(nc.vector.match_replace(blkw, top8, blkw, NEG))
                            own(nc.vector.tensor_tensor(blkb, blk, blkw, ALU.is_equal))
                            own(nc.vector.tensor_scalar(blkb, blkb, NEG, None, ALU.mult))
                            for g in range(4):
                                dve.wait_ge(t_sel, at_batch(4, g + 1))
                                own(nc.vector.tensor_tensor(SS[:, g * 512:g * 512 + 512].rearrange("p (n k) -> p n k", k=64),
                                                            ps[:, g].rearrange("p (n k) -> p n k", k=64),
                                                            bc(blkb[:, 8 * g:8 * g + 8].unsqueeze(2), [P, 8, 64]), ALU.add))
                            own(nc.vector.reduce_max(smx[:, 1:2], SS, AX))
                            nc.vector.tensor_scalar(smx[:, 1:2], smx[:, 1:2], -SCALE, None, ALU.mult).then_inc(v_selm, 1)
                            expert_steps(bb + (PH + AT_NSA[2]), 1, 16 * x + 12, 16 * x + 16)
                            dve.wait_ge(a_p, at_batch(3, 3))
                            own(nc.vector.reciprocal(srec[:, 1:3], ssum[:, 1:3]))
                            dve.wait_ge(st_or, at_batch(48, 48))
                            dve.wait_ge(t_pv, at_batch(7, 14))
                            for kv in range(KVH):
                                k = slice(32 * kv, 32 * kv + 32)
                                own(nc.vector.tensor_copy(OROW[k, 0], ps[k, 6, 64 * kv:64 * kv + 64]))
                                own(nc.vector.tensor_scalar(OROW[k, 2], ps[k, 6, 256 + 64 * kv:320 + 64 * kv], srec[k, 2:3], None, ALU.mult))
                                ins = nc.vector.tensor_scalar(OROW[k, 1], ps[k, 7, 256 + 64 * kv:320 + 64 * kv], srec[k, 1:2], None, ALU.mult)
                                own(ins) if kv < 3 else ins.then_inc(v_or, 1)
                        cnt.leave(DEC_B // 2)
                    interleaved(2, AT_ROWS[2], 0)
                own(nc.vector.tensor_tensor(ILOG[r, t], z[r, ZMI:ZMI + 4], GB[r, 0:4], ALU.add))
                own(nc.vector.tensor_tensor(FLOG[r, t], z[r, ZMF:ZMF + 4], GB[r, 4:8], ALU.add))
                nc.vector.scalar_tensor_tensor(out=MT2[r, t], in0=FLOG[r, t], scalar=-1.0, in1=FLOG[r, t], op0=ALU.mult, op1=ALU.max).then_inc(v_mf, 1)
                dve.wait_ge(a_mf, 2 * t + 1)
                nc.vector.tensor_scalar(MT2[r, t], MT2[r, t], 1.0, None, ALU.add).then_inc(v_mf, 1)
                dve.wait_ge(a_mf, 2 * t + 2)
                nc.vector.scalar_tensor_tensor(out=FLOG[r, t], in0=FLOG[r, t], scalar=0.0, in1=MT2[r, t], op0=ALU.min, op1=ALU.subtract).then_inc(v_flog, 1)
                if t == 2:
                    dve.wait_ge(t_mn, 1)
                    nc.vector.tensor_copy(NT, ps[:, 6, 0:32]).then_inc(v_mn, 1)
                    nc.vector.tensor_copy(M0[r], ps[r, 7, 0:4]).then_inc(v_mn, 1)
                    dve.wait_ge(v_mn, 2)
                dve.wait_ge(t_bc, t + 1)
                own(nc.vector.tensor_copy(BCUM[r, t], ps[r, 2, 0:4]))
                own(nc.vector.tensor_tensor(GLOG[r, t], ILOG[r, t], BCUM[r, t], ALU.subtract))
                for h in range(MH):
                    hh = MH * t + h
                    tiles = range(t + 1) if t < 2 else (2,)
                    w = P * (t + 1) if t < 2 else 64
                    for n, u in enumerate(tiles):
                        ins = nc.vector.tensor_scalar(DG[r, n * P:n * P + m], k_("ident")[r, r], GLOG[r, u, h:h + 1], None, ALU.mult)
                    ins.then_inc(v_dg, 1)
                    dve.wait_ge(t_gr, hh + 1)
                    if t == 1:
                        own(nc.vector.tensor_copy(MD[:, 0:P], ps[:, 0, 0:P]))
                    own(nc.vector.tensor_tensor(MD[r, w - m:w], ps[r, 0, w - m:w], k_("blockcausal")[r] if t == 2 else k_("causal"), ALU.add))
                    own(nc.vector.reduce_max(MMAX[r, t, h:h + 1], MD[r, 0:w], AX))
                    if t < 2:
                        own(nc.vector.tensor_scalar(MMAX[r, t, h:h + 1], MMAX[r, t, h:h + 1], 0.0, None, ALU.max))
                    else:
                        own(nc.vector.tensor_tensor(MMAX[r, t, h:h + 1], MMAX[r, t, h:h + 1], M0[r, h:h + 1], ALU.max))
                        own(nc.vector.tensor_tensor(EX[r, 1:2], M0[r, h:h + 1], MMAX[r, 2, h:h + 1], ALU.subtract))
                    own(nc.vector.tensor_scalar(MT1[r, t, h:h + 1], MMAX[r, t, h:h + 1], -1.0, None, ALU.mult))
                    nc.vector.tensor_tensor(EX[r, 0:1], MT1[r, t, h:h + 1], BCUM[r, t, h:h + 1], ALU.subtract).then_inc(v_md, 1)
                    besides_head(t, h)
                    dve.wait_ge(a_mw, 2 * hh + 2)
                    nc.vector.scalar_tensor_tensor(out=MW[r, 0:w], in0=ps[r, 1, 0:w], scalar=DH ** -0.5, in1=MW[r, 0:w],
                                                   op0=ALU.mult, op1=ALU.mult, accum_out=DEN[r, 0:1]).then_inc(v_wqk, 1)
                    dve.wait_ge(v_wqk, hh + 1)
                    dve.wait_ge(t_num, hh + 1)
                    if t == 2:
                        bm = k_("batchmask")
                        own(nc.vector.tensor_tensor(QCM[r], ps[r, 4:6, :].rearrange("p j (b e) -> p (j b) e", e=DH),
                                                    bc(bm[r].unsqueeze(2), [m, DEC_B, DH]), ALU.mult))
                        own(nc.vector.reduce_sum(HN[r], QCM[r].rearrange("p b e -> p e b"), AX))
                        own(nc.vector.scalar_tensor_tensor(out=HN[r], in0=HN[r], scalar=EX[r, 1:2], in1=ps[r, 3, 0:P], op0=ALU.mult, op1=ALU.add))
                        own(nc.vector.tensor_tensor(QN[r], ps[r, 3, P:P + 8], bm[r], ALU.mult))
                        own(nc.vector.reduce_sum(DEN[r, 1:2], QN[r], AX))
                        own(nc.vector.scalar_tensor_tensor(out=DEN[r, 0:1], in0=DEN[r, 1:2], scalar=EX[r, 1:2], in1=DEN[r, 0:1], op0=ALU.mult, op1=ALU.add))
                    den = DEN[r, 0:1]
                    own(nc.vector.scalar_tensor_tensor(out=den, in0=den, scalar=-1.0, in1=den, op0=ALU.mult, op1=ALU.max))
                    own(nc.vector.tensor_tensor(den, den, EX[r, 0:1], ALU.max))
                    own(nc.vector.reciprocal(den, den))
                    yh = Y[r, YM + h * DH:YM + h * DH + DH]
                    own(nc.vector.tensor_scalar(yh, HN[r] if t == 2 else ps[:, 3, 0:P], den, None, ALU.mult))
                    own(nc.vector.tensor_tensor_reduce(out=HN[r], in0=yh, in1=yh, scale=1.0, scalar=0.0, op0=ALU.mult, op1=ALU.add,
                                                       accum_out=SSQ[r, t, h:h + 1]))
                    dve.sem_inc(v_hn, 1)
                    if t == 1:
                        interleaved(1, AT_ROWS[1], h)
                    if t == 2:
                        interleaved(2, *((AT_ROWS[2], h + 1) if h < 3 else (AT_STATE[2], 0)))
                if t == 2:
                    dve.wait_ge(ld_os, 48)
                    for n in range(3):
                        o = OS[n][r].rearrange("p (h d) -> p h d", d=HD)
                        own(nc.vector.tensor_tensor(o, o, bc(gate[:, n].unsqueeze(2), [m, HEADS, HD]), ALU.mult))
                    y = Y[r, YB:YB + NSA_W]
                    own(nc.vector.tensor_tensor(y, OS[0][r], OS[1][r], ALU.add))
                    own(nc.vector.tensor_tensor(y, y, OS[2][r], ALU.add))
                if t:
                    nc.vector.tensor_tensor(BM[r, t], BCUM[r, t], MMAX[r, t], ALU.add).then_inc(v_bm, 1)
                    dve.wait_ge(t_ml, t)
                    own(nc.vector.tensor_copy(MLAST[r, t], ps[r, 0, 0:4]))
                    own(nc.vector.tensor_copy(MNEW[r, t], ps[r, 0, 8:12]))
                if t == 1:
                    nc.vector.tensor_tensor(WL[:, 0:2], GLOG[:, 0:2], bc(MLAST[:, 1:2], [P, 2, MH]), ALU.subtract).then_inc(v_wl, 1)
                    dve.wait_ge(a_wl, 1)
                if t == 2:
                    nc.vector.tensor_tensor(WL[r, 2], GLOG[r, 2], MLAST[r, 2], ALU.subtract).then_inc(v_wl, 1)
                    nc.vector.tensor_tensor(MT1[r, 2], M0[r], MLAST[r, 2], ALU.subtract).then_inc(v_wl, 1)
                    dve.wait_ge(a_wl, 3)
                    for h in range(MH):
                        nc.vector.tensor_scalar(DECD[r, h], k_("lastmask")[r], MT1[r, 2, h:h + 1], None, ALU.mult).then_inc(v_decd, 1)
                    dve.wait_ge(t_decb, 1)
                    own(nc.vector.tensor_copy(DECB.rearrange("p h b -> p (h b)"), ps[:, 1, 0:32]))
                for h in range(MH if t else 0):
                    n_c = MH * (t - 1) + h
                    if t == 1:
                        for u in range(2):
                            ins = nc.vector.tensor_scalar(KW[:, u], Z[u][:, ZMK + h * DH:ZMK + h * DH + DH], WL[:, u, h:h + 1], DH ** -0.5,
                                                          ALU.mult, ALU.mult)
                        ins.then_inc(v_kw, 1)
                        dve.wait_ge(t_c, n_c + 1)
                        own(nc.vector.tensor_copy(NO[:, 32 + h:33 + h], ps[:, 2, P:P + 1]))
                        if h:
                            dve.wait_ge(st_c, 16 * h)
                        nc.vector.tensor_copy(CP, ps[:, 2, 0:P]).then_inc(v_c, 1)
                    else:
                        nc.vector.tensor_scalar(KW[r, 0], z[r, ZMK + h * DH:ZMK + h * DH + DH], WL[r, 2, h:h + 1], DH ** -0.5, ALU.mult, ALU.mult)
                        nc.vector.tensor_tensor(VB[r], bc(z[r, ZMV + h * DH:ZMV + h * DH + DH].unsqueeze(1), [m, DEC_B, DH]),
                                                bc(k_("batchmask")[r].unsqueeze(2), [m, DEC_B, DH]), ALU.mult).then_inc(v_kw, 1)
                        dve.wait_ge(ld_mc, 16 * (MH + h) + 16)
                        own(nc.vector.tensor_tensor(MC, MC, bc(DECB[:, h].unsqueeze(2), [P, DEC_B, DH]), ALU.mult))
                        nt = NT.rearrange("p (b h) -> p h b", h=MH)[:, h]
                        no = NO[:, 0:32].rearrange("p (b h) -> p h b", h=MH)[:, h]
                        own(nc.vector.tensor_tensor(no, nt, DECB[:, h], ALU.mult))
                        dve.wait_ge(t_c, n_c + 1)
                        own(nc.vector.tensor_tensor(no, no, ps[:, 2, 0:8], ALU.add))
                        nc.vector.tensor_tensor(MC, MC, ps[:, 3:5, :].rearrange("p j (b e) -> p (j b) e", e=DH), ALU.add).then_inc(v_c, 1)
                    if AT_STATE[t] is not None:
                        interleaved(2, *((AT_STATE[2], h + 1) if h < 3 else (AT_OUT[2], 0)))
                if t:
                    dve.wait_ge(t_no, t)
                    nc.vector.tensor_copy(N32[0:36], ps[0:36, 0, 0:128]).then_inc(v_no, 1)
                nc.vector.tensor_scalar(SSQ[r, t], SSQ[r, t], 1.0 / DH, EPS, ALU.mult, ALU.add).then_inc(v_ssq, 1)
                y = Y[r, YM:YM + ML_W]
                own(nc.vector.tensor_tensor(y, y, z[r, ZMO:ZMO + 512], ALU.mult))
                dve.wait_ge(a_ssq, t + 1)
                own(nc.vector.reciprocal(SSQ[r, t], SSQ[r, t]))
                y = y.rearrange("p (h e) -> p h e", h=MH)
                own(nc.vector.tensor_tensor(y, y, bc(SSQ[r, t].unsqueeze(2), [m, MH, DH]), ALU.mult))
                dve.sem_inc(v_y, 1)
                dve.wait_ge(ld_xr, 16 * t + 16)
                for c in range(4):
                    if t:
                        if t == 1:
                            interleaved(1, AT_OUT[1], c)
                        else:
                            interleaved(2, *((AT_OUT[2], c + 1) if c < 3 else (AT_WQ[2], 0)))
                    dve.wait_ge(w_used, W1[t] + 4 * c + 4)
                    x = X[r, c * WC:c * WC + WC]
                    nc.vector.tensor_tensor(x, x, ps[r, 4 + c, :], ALU.add).then_inc(v_x1, 1)
                if t and AT_WQ[t] is None:
                    dve.sem_inc(v_x2, 1)
                if t == 0:
                    for j in range(4):
                        dve.wait_ge(t_sk, j + 1)
                        nc.vector.tensor_copy(SKT[:, 4 * j:4 * j + 4], ps[:, j].rearrange("p (q n) -> p q n", q=4)).then_inc(v_sk, 1)
                dve.wait_ge(a_ss2, 2 * t + 1)
                nc.vector.tensor_scalar(ss[r, 1:2], ss[r, 1:2], 1.0 / D, EPS, ALU.mult, ALU.add).then_inc(v_ss2, 1)
                dve.wait_ge(a_ss2, 2 * t + 2)
                nc.vector.reciprocal(rstd[r, 1:2], rstd[r, 1:2]).then_inc(v_ss2, 1)
                dve.wait_ge(t_h, 4 * t + 4)
                dve.wait_ge(ld_g2, 16 * t + 16)
                own(nc.vector.tensor_tensor(H[t][r], H[t][r], G2B[t][r], ALU.mult))
                if AT_WQ[t] is not None:
                    for quarter in range(t - 1, 4):
                        interleaved(t, AT_WQ[t], quarter)
                    dve.sem_inc(v_x2, 1)
                if t == 0:
                    nc.vector.tensor_copy(ACC, X).then_inc(v_acc0, 1)
                    dve.wait_ge(v_acc0, 1)
                tv = lambda c: TV[r].rearrange("p (h c) k -> p c h k", c=2)[:, c]
                ti = lambda c: TIF[r].rearrange("p (h c) k -> p c h k", c=2)[:, c]
                dve.wait_ge(a_sc, 4 * t + 4)
                best(r, TV, TI, SC, SCW, 16)
                own(nc.vector.tensor_copy(TIF[r], TI[r]))
                own(nc.vector.tensor_tensor(CAND[r].rearrange("p h (i j) -> p h i j", i=TOPK), bc(tv(0).unsqueeze(3), [m, PH, TOPK, TOPK]),
                                            bc(tv(1).unsqueeze(2), [m, PH, TOPK, TOPK]), ALU.add))
                best(r, CVAL, CPOS, CAND, CANDW, PH)
                g = GG[r, t % 2].rearrange("p (h k) -> p h k", h=PH)
                nc.vector.tensor_tensor(g, CVAL[r], bc(CVAL[r, :, 0:1], [m, PH, TOPK]), ALU.subtract).then_inc(v_cd, 1)
                own(nc.vector.tensor_scalar(CHI[r], CPOS[r], 4, None, ALU.logical_shift_right))
                own(nc.vector.tensor_scalar(CLO[r], CPOS[r], 15, None, ALU.bitwise_and))
                own(nc.vector.tensor_copy(FHI[r], CHI[r]))
                own(nc.vector.tensor_copy(FLO[r], CLO[r]))
                for c, rank, num in ((0, FHI, E1), (1, FLO, E2)):
                    oh = OH[r].rearrange("p (h k i) -> p h k i", h=PH, k=TOPK)
                    own(nc.vector.tensor_tensor(OH[r].rearrange("p (x i) -> p x i", i=TOPK), bc(k_("iota16")[r].unsqueeze(1), [m, 128, TOPK]),
                                                bc(rank[r].rearrange("p h k -> p (h k)").unsqueeze(2), [m, 128, TOPK]), ALU.is_equal))
                    own(nc.vector.tensor_tensor(oh, oh, bc(ti(c).unsqueeze(2), [m, PH, TOPK, TOPK]), ALU.mult))
                    own(nc.vector.reduce_sum(num[r].rearrange("p h k -> p (h k)"), OH[r].rearrange("p (x i) -> p x i", i=TOPK), AX))
                own(nc.vector.scalar_tensor_tensor(out=EIDX[r, t % 2], in0=E1[r].rearrange("p h k -> p (h k)"), scalar=float(NKEY),
                                                   in1=E2[r].rearrange("p h k -> p (h k)"), op0=ALU.mult, op1=ALU.add))
                if t == 2:
                    own(nc.vector.tensor_copy(EIDX[64:P, 0, 0:64], EIDX[r, 0, 64:P]))
                    own(nc.vector.tensor_copy(H[2][64:P], H[2][r]))
                dve.sem_inc(v_route, 1)
                if t == 0:
                    first_mean(1)
                dve.wait_ge(a_cd, t + 1)
                own(nc.vector.reduce_sum(GSUM[r], g, AX))
                own(nc.vector.reciprocal(GSUM[r], GSUM[r]))
                own(nc.vector.tensor_tensor(g, g, bc(GSUM[r].unsqueeze(2), [m, PH, TOPK]), ALU.mult))
                if t == 0:
                    first_rstd(1)
                else:
                    dve.wait_ge(st_x2, 16 * t)
                    if t == 2:
                        own(nc.vector.memset(ACC[64:P], 0.0))
                    nc.vector.tensor_copy(ACC[r], X[r]).then_inc(v_acc0, 1)
                    dve.wait_ge(v_acc0, t + 1)
                if t == 2:
                    own(nc.vector.tensor_copy(GG[64:P, 0, 0:64], GG[r, 0, 64:P]))

            def final_norm(t):
                x2, c = (X2[:, t] if t < 2 else ACC)[rows(t)], slice(t, t + 1)
                dve.wait_ge(a_ss3, 2 * t + 1)
                nc.vector.tensor_scalar(ss[rows(t), c], ss[rows(t), c], 1.0 / D, EPS, ALU.mult, ALU.add).then_inc(v_ss3, 1)
                dve.wait_ge(a_ss3, 2 * t + 2)
                own(nc.vector.reciprocal(rstd[rows(t), c], rstd[rows(t), c]))
                nc.vector.scalar_tensor_tensor(out=x2, in0=x2, scalar=rstd[rows(t), c], in1=GFB[rows(t)], op0=ALU.mult, op1=ALU.mult).then_inc(v_out, 1)

            dve.wait_ge(ld_gf, 16)
            final_norm(0)
            final_norm(1)
            expert_loop(2, 0, TURNS[2])
            own(nc.vector.tensor_copy(X[rows(2)], ACC[64:P]))
            nc.vector.tensor_tensor(ACC[rows(2)], ACC[rows(2)], X[rows(2)], ALU.add).then_inc(v_x2, 1)
            final_norm(2)

        @block.gpsimd
        def _(pool):
            u_rows, v_rows = peer_u[0], peer_v[0]

            def wait_apart(sem, value, cell):
                pool.wait_ge(sem, value)
                one = k_("ones")[:, 0:1]
                nc.gpsimd.tensor_tensor(WCELL[:, cell:cell + 1], one, one, ALU.add)

            for t in range(TILES):
                pool.wait_ge(v_route, t + 1)
                with pool.Fori(t * (PH // 2), t * (PH // 2) + TURNS[t] // 2) as i:
                    for x in range(2):
                        pool.wait_ge(g_used, i * 64 + 32 * x + 1)
                        nc.gpsimd.tensor_copy(CUR[:, x], EIDX[:, t % 2, bass.ds((i * 2 + x - t * PH) * TOPK, TOPK)]).then_inc(p_cur, 1)
                        wait_apart(p_cur, i * 2 + x + 1, 33 * x)
                        for n in range(32):
                            wait_apart(g_used, i * 64 + 32 * x + n + 1, 1 + n)
                            nc.gpsimd.indirect_dma_start(BUF[:, n % NBUF], None, u_rows if n < 16 else v_rows,
                                                         bass.IndirectOffsetOnAxis(CUR[:, x, n % 16:n % 16 + 1].bitcast(U32), 0)
                                                         ).then_inc(g_in[n % NBUF], 16)


_INS = ["x_prompt", "x_sample", "cache_nsa_kv", "state_win_kv", "state_conv", "state_mlstm_C", "state_mlstm_n",
        "state_mlstm_m", "page_table", "norm1_g", "w_in", "conv_w", "mlstm_gate_b", "mlstm_norm_g", "w_out", "norm2_g",
        "peer_wq", "peer_subkeys", "peer_u", "peer_v", "final_norm_g"]
_OUTS = [("y_prompt", (1, 256, 2048)), ("y_sample", (8, 8, 2048)), ("p_rows", (1, 1, 256, 4, 4, 64)),
         ("p_win", (1, 1, 256, 2, 4, 64)), ("p_conv", (1, 1, 2, 512)), ("p_C", (1, 1, 4, 128, 128)), ("p_n", (1, 1, 4, 128)),
         ("p_m", (1, 1, 4)), ("s_rows", (1, 8, 8, 4, 4, 64)), ("s_win", (1, 8, 512, 2, 4, 64)), ("s_conv", (1, 8, 2, 512)),
         ("s_C", (1, 8, 4, 128, 128)), ("s_n", (1, 8, 4, 128)), ("s_m", (1, 8, 4))]


def kernel(**inputs):
    import concourse.bacc as _bacc
    from concourse.bass_utils import run_bass_kernel_spmd as _run

    nc = _bacc.Bacc("TRN2", target_bir_lowering=False, num_devices=1)
    at, const = constants()
    arrays = {"in_const_dram": const}
    args = [nc.dram_tensor("in_const_dram", const.shape, F32, kind="ExternalInput").ap()]
    for name in _INS:
        a = np.ascontiguousarray(inputs[name])
        arrays["in_%s_dram" % name] = a
        args.append(nc.dram_tensor("in_%s_dram" % name, a.shape, mybir.dt.from_np(a.dtype), kind="ExternalInput").ap())
    for name, shape in _OUTS:
        args.append(nc.dram_tensor("out_%s_dram" % name, shape, F32, kind="ExternalOutput").ap())
    for name, shape in (("new_kv", (64, 1536)), ("conv_ext", (340, 512)), ("branch_out", (3, 8, 8, 16, 64)), ("x2_rows", (2, 128, 2048)), ("z_rows", (64, ZC))):
        args.append(nc.dram_tensor(name, shape, F32, kind="Internal").ap())
    hybrid_step(nc, at, const.shape[1], *args)
    r = _run(nc, [arrays], core_ids=[0])
    return tuple(r.results[0]["out_%s_dram" % name] for name, _ in _OUTS)
```
